# Optimizing a Trainium2 kernel written in Bass

```python
import math, functools
import jax, jax.numpy as jnp
from jax import lax
import numpy as np

D_MODEL = 1024
BATCH = 1
SEQ = 1024
DEPTH = 2
DEC_BATCH = 8
DEC_SEQ = 1
PAST_LEN = 1024
PAGE_SIZE = 128

MIX_W = D_MODEL
POOL_W = MIX_W // 2
POOL_WINDOWS = (2, 4, 8, 16)
POOL_GROUPS = len(POOL_WINDOWS)
POOL_GC = POOL_W // POOL_GROUPS
POOL_HIST = max(POOL_WINDOWS) - 1
ATTN_W = MIX_W - POOL_W
HEAD_DIM = 64
VDIM = 2 * HEAD_DIM
N_HEADS = ATTN_W // VDIM
IN_W = POOL_W + 3 * ATTN_W
D_FF = 2816
CONV_W = 3
ROPE_THETA = 10000.0
Q_BLOCK = 128
EPS = 1e-6

kernel_name = "hymba_pool_diffattn_convffn_step"

F32 = jnp.float32

def rms_norm(x, g):
    xf = x.astype(F32)
    y = xf * lax.rsqrt(jnp.mean(xf * xf, axis=-1, keepdims=True) + EPS)
    return (y * g.astype(F32)).astype(x.dtype)

def lambda_init(layer):
    return 0.8 - 0.6 * math.exp(-0.3 * layer)

def rope(x, pos):
    half = HEAD_DIM // 2
    inv = 1.0 / (ROPE_THETA ** (jnp.arange(half, dtype=F32) * (2.0 / HEAD_DIM)))
    ang = pos.astype(F32)[:, None] * inv[None, :]
    cos = jnp.cos(ang)[None, :, None, None, :]
    sin = jnp.sin(ang)[None, :, None, None, :]
    xf = x.astype(F32)
    x1, x2 = xf[..., :half], xf[..., half:]
    return jnp.concatenate([x1 * cos - x2 * sin, x2 * cos + x1 * sin], axis=-1).astype(x.dtype)

def pool_mixer(u, prev, pos, pool_w, pool_scale):
    B, T, _ = u.shape
    ext = jnp.concatenate([prev, u], axis=1)
    c = jnp.cumsum(ext.astype(F32), axis=1)
    c = jnp.concatenate([jnp.zeros((B, 1, POOL_W), F32), c], axis=1)
    cg = c.reshape(B, POOL_HIST + T + 1, POOL_GROUPS, POOL_GC)
    end = cg[:, POOL_HIST + 1:]
    means = []
    for g, w in enumerate(POOL_WINDOWS):
        start = cg[:, POOL_HIST + 1 - w: POOL_HIST + 1 - w + T, g]
        cnt = jnp.minimum(pos + 1, w).astype(F32)[None, :, None]
        means.append((end[:, :, g] - start) / cnt)
    mean = jnp.stack(means, axis=2)
    ug = u.astype(F32).reshape(B, T, POOL_GROUPS, POOL_GC)
    d = (mean - ug).astype(u.dtype)
    y = jnp.einsum('btgc,gcd->btgd', d, pool_w) * pool_scale.reshape(POOL_GROUPS, POOL_GC)
    return y.reshape(B, T, POOL_W), ext[:, -POOL_HIST:]

def diff_core(q, k, v, q_pos, k_pos, lam):
    s = jnp.einsum('bqhcd,bkhcd->bhcqk', q, k).astype(F32) * (HEAD_DIM ** -0.5)
    mask = k_pos[None, :] <= q_pos[:, None]
    s = jnp.where(mask, s, -jnp.inf)
    p = jax.nn.softmax(s, axis=-1)
    a = p[:, :, 0] - lam * p[:, :, 1]
    return jnp.einsum('bhqk,bkhe->bqhe', a.astype(v.dtype), v)

def prompt_attention(q, k, v, lam, *, pos):
    B, S = q.shape[0], q.shape[1]
    nb = S // Q_BLOCK
    qb = jnp.moveaxis(q.reshape(B, nb, Q_BLOCK, N_HEADS, 2, HEAD_DIM), 1, 0)
    pb = pos.reshape(nb, Q_BLOCK)
    ob = lax.map(lambda a: diff_core(a[0], k, v, a[1], pos, lam), (qb, pb))
    return jnp.moveaxis(ob, 0, 1).reshape(B, S, N_HEADS, VDIM)

def sample_attention(q, k, v, lam, *, pos, cache_k_l, cache_v_l, page_table):
    DB, T = q.shape[0], q.shape[1]
    past = page_table.shape[1] * cache_k_l.shape[1]
    k_past = cache_k_l[page_table].reshape(DB, past, N_HEADS, 2, HEAD_DIM)
    v_past = cache_v_l[page_table].reshape(DB, past, N_HEADS, VDIM)
    k_all = jnp.concatenate([k_past, k.astype(k_past.dtype)], axis=1)
    v_all = jnp.concatenate([v_past, v.astype(v_past.dtype)], axis=1)
    k_pos = jnp.arange(past + T, dtype=jnp.int32)
    return diff_core(q, k_all, v_all, pos, k_pos, lam)

def conv_ffn(h, prev, w_up, conv_w, conv_b, w_down):
    up = h @ w_up
    a, b = up[..., :D_FF], up[..., D_FF:]
    ext = jnp.concatenate([prev, a], axis=1)
    c = lax.conv_general_dilated(ext, conv_w[:, None, :].astype(ext.dtype), window_strides=(1,),
                                 padding='VALID', dimension_numbers=('NWC', 'WIO', 'NWC'),
                                 feature_group_count=D_FF) + conv_b
    return (jax.nn.silu(c) * b) @ w_down, ext[:, -(CONV_W - 1):]

def layer(x, pos, prev_pool, prev_conv, attend, lam_init, p):
    B, T, _ = x.shape
    h = rms_norm(x, p['norm1_g'])
    proj = h @ p['w_in']
    u = proj[..., :POOL_W]
    q = proj[..., POOL_W:POOL_W + ATTN_W].reshape(B, T, N_HEADS, 2, HEAD_DIM)
    k = proj[..., POOL_W + ATTN_W:POOL_W + 2 * ATTN_W].reshape(B, T, N_HEADS, 2, HEAD_DIM)
    v = proj[..., POOL_W + 2 * ATTN_W:].reshape(B, T, N_HEADS, VDIM)
    q, k = rope(q, pos), rope(k, pos)
    pool_y, new_pool = pool_mixer(u, prev_pool, pos, p['pool_w'], p['pool_scale'])
    lam = (jnp.exp(jnp.sum(p['lam_q1'].astype(F32) * p['lam_k1'].astype(F32)))
           - jnp.exp(jnp.sum(p['lam_q2'].astype(F32) * p['lam_k2'].astype(F32))) + lam_init)
    o = attend(q, k, v, lam)
    attn_y = (rms_norm(o, p['subln_g']) * (1.0 - lam_init)).reshape(B, T, ATTN_W)
    x = x + jnp.concatenate([pool_y, attn_y.astype(pool_y.dtype)], axis=-1) @ p['w_out']
    f, new_conv = conv_ffn(rms_norm(x, p['norm2_g']), prev_conv, p['w_up'], p['conv_w'],
                           p['conv_b'], p['w_down'])
    return x + f, k, v, new_pool, new_conv

def setup_inputs(seed: int = 0) -> dict:
    key = jax.random.key(seed)
    ks = jax.random.split(key, 24)
    n = lambda i, shape: jax.random.normal(ks[i], shape, F32)
    n_pages = PAST_LEN // PAGE_SIZE
    n_used = DEC_BATCH * n_pages
    n_pool = n_used + max(1, n_used // 4)
    page_table = jax.random.permutation(ks[0], n_pool)[:n_used].reshape(DEC_BATCH, n_pages).astype(jnp.int32)
    return {
        "x_prompt": n(1, (BATCH, SEQ, D_MODEL)),
        "x_sample": n(2, (DEC_BATCH, DEC_SEQ, D_MODEL)),
        "cache_k": n(3, (DEPTH, n_pool, PAGE_SIZE, N_HEADS, VDIM)),
        "cache_v": n(4, (DEPTH, n_pool, PAGE_SIZE, N_HEADS, VDIM)),
        "state_pool": n(5, (DEPTH, DEC_BATCH, POOL_HIST, POOL_W)),
        "state_conv": n(6, (DEPTH, DEC_BATCH, CONV_W - 1, D_FF)),
        "page_table": page_table,
        "norm1_g": 1.0 + 0.02 * n(7, (DEPTH, D_MODEL)),
        "w_in": n(8, (DEPTH, D_MODEL, IN_W)) * D_MODEL ** -0.5,
        "pool_w": n(9, (DEPTH, POOL_GROUPS, POOL_GC, POOL_GC)) * POOL_GC ** -0.5,
        "pool_scale": 1.0 + 0.1 * n(10, (DEPTH, POOL_W)),
        "lam_q1": 0.1 * n(11, (DEPTH, HEAD_DIM)),
        "lam_k1": 0.1 * n(12, (DEPTH, HEAD_DIM)),
        "lam_q2": 0.1 * n(13, (DEPTH, HEAD_DIM)),
        "lam_k2": 0.1 * n(14, (DEPTH, HEAD_DIM)),
        "subln_g": 1.0 + 0.02 * n(15, (DEPTH, VDIM)),
        "w_out": n(16, (DEPTH, MIX_W, D_MODEL)) * MIX_W ** -0.5,
        "norm2_g": 1.0 + 0.02 * n(17, (DEPTH, D_MODEL)),
        "w_up": n(18, (DEPTH, D_MODEL, 2 * D_FF)) * D_MODEL ** -0.5,
        "conv_w": n(19, (DEPTH, CONV_W, D_FF)) * CONV_W ** -0.5,
        "conv_b": 0.01 * n(20, (DEPTH, D_FF)),
        "w_down": n(21, (DEPTH, D_FF, D_MODEL)) * D_FF ** -0.5,
        "final_g": 1.0 + 0.02 * n(22, (D_MODEL,)),
    }

def reference(x_prompt, x_sample, cache_k, cache_v, state_pool, state_conv, page_table,
              norm1_g, w_in, pool_w, pool_scale, lam_q1, lam_k1, lam_q2, lam_k2, subln_g,
              w_out, norm2_g, w_up, conv_w, conv_b, w_down, final_g):
    B, S, _ = x_prompt.shape
    DB, T, _ = x_sample.shape
    past = page_table.shape[1] * cache_k.shape[2]
    pos_p = jnp.arange(S, dtype=jnp.int32)
    pos_s = past + jnp.arange(T, dtype=jnp.int32)
    xp, xs = x_prompt, x_sample
    kp_l, vp_l, poolp_l, convp_l = [], [], [], []
    ks_l, vs_l, pools_l, convs_l = [], [], [], []
    for l in range(DEPTH):
        p = dict(norm1_g=norm1_g[l], w_in=w_in[l], pool_w=pool_w[l], pool_scale=pool_scale[l],
                 lam_q1=lam_q1[l], lam_k1=lam_k1[l], lam_q2=lam_q2[l], lam_k2=lam_k2[l],
                 subln_g=subln_g[l], w_out=w_out[l], norm2_g=norm2_g[l], w_up=w_up[l],
                 conv_w=conv_w[l], conv_b=conv_b[l], w_down=w_down[l])
        li = lambda_init(l)
        xp, kp, vp, poolp, convp = layer(
            xp, pos_p, jnp.zeros((B, POOL_HIST, POOL_W), xp.dtype),
            jnp.zeros((B, CONV_W - 1, D_FF), xp.dtype),
            functools.partial(prompt_attention, pos=pos_p), li, p)
        xs, ksn, vsn, pools, convs = layer(
            xs, pos_s, state_pool[l], state_conv[l],
            functools.partial(sample_attention, pos=pos_s, cache_k_l=cache_k[l],
                              cache_v_l=cache_v[l], page_table=page_table), li, p)
        kp_l.append(kp.reshape(B, S // PAGE_SIZE, PAGE_SIZE, N_HEADS, VDIM))
        vp_l.append(vp.reshape(B, S // PAGE_SIZE, PAGE_SIZE, N_HEADS, VDIM))
        poolp_l.append(poolp)
        convp_l.append(convp)
        ks_l.append(ksn.reshape(DB, T, N_HEADS, VDIM))
        vs_l.append(vsn)
        pools_l.append(pools)
        convs_l.append(convs)
    y_prompt = rms_norm(xp, final_g)
    y_sample = rms_norm(xs, final_g)
    k_new_prompt = jnp.stack(kp_l)
    v_new_prompt = jnp.stack(vp_l)
    pool_new_prompt = jnp.stack(poolp_l)
    conv_new_prompt = jnp.stack(convp_l)
    k_new_sample = jnp.stack(ks_l)
    v_new_sample = jnp.stack(vs_l)
    pool_new_sample = jnp.stack(pools_l)
    conv_new_sample = jnp.stack(convs_l)
    return (y_prompt, y_sample, k_new_prompt, v_new_prompt, pool_new_prompt, conv_new_prompt,
            k_new_sample, v_new_sample, pool_new_sample, conv_new_sample)


_drawn_inputs = setup_inputs


def setup_inputs(seed=0):
    import zlib

    import numpy as np

    out = dict(_drawn_inputs(seed))
    spreads = {}
    factors = {'subln_g': 4.849, 'conv_b': 21.941, 'final_g': 8.065, 'norm2_g': 2.806}
    for name, (base, spread) in spreads.items():
        noise = np.random.default_rng([zlib.crc32(name.encode()), seed]).standard_normal(out[name].shape)
        drawn = base * np.exp(spread * noise) if base else spread * noise
        out[name] = __import__('jax').numpy.asarray(drawn.astype(out[name].dtype))
    for name, factor in factors.items():
        out[name] = (out[name] * factor).astype(out[name].dtype)
    return out
```

```python
import math
from contextlib import ExitStack

import numpy as np

import concourse.bass as bass
from concourse import mybir

F32 = mybir.dt.float32
F32R = mybir.dt.float32r
I32 = mybir.dt.int32
ALU = mybir.AluOpType
ACT = mybir.ActivationFunctionType
AX_X = mybir.AxisListType.X

P = 128
D_MODEL, SEQ, DEPTH, DEC_BATCH = 1024, 1024, 2, 8
PAST_LEN, PAGE_SIZE = 1024, 128
N_PAGES = PAST_LEN // PAGE_SIZE
RUN = 8
GROUPS = PAGE_SIZE // RUN
assert GROUPS * N_PAGES == P and RUN == N_PAGES
POOL_W, POOL_WINDOWS, POOL_HIST = 512, (2, 4, 8, 16), 15
N_HEADS, HEAD_DIM = 4, 64
VDIM = 2 * HEAD_DIM
D_FF = 2816
EPS = 1e-6
ROPE_THETA = 10000.0
NEG = -1e30

T = SEQ + DEC_BATCH
NT = 3
TW = T // NT
KC = D_MODEL // P
FC = D_FF // P
QT_N = SEQ // P
CONV_TAPS = 3

SLOTS = 3
U_HEAD = 6
U_FFN0 = U_HEAD * N_HEADS
U_LAYER = U_FFN0 + 3 * FC

ORDER = [7, 0, 6, 1, 5, 2, 4, 3]
SOFTMAX_STEP = 0
VALUES_STEP = 2


def rounds(i):
    return [list(range(a, min(a + 4, i + 1))) for a in range(0, i + 1, 4)]


def head_uses():
    g, t = [("u",), ("q",), ("k",), ("qb", 0), ("qb", 1), ("v",), ("y",)], ["state", "uout"]
    t += [("k", 0), ("k", 1), "small"]
    g += [("wg", m) for m in range(KC)]
    t += [("v", 0), ("v", 1)]
    g += [("s", 0, 0), ("s", 0, 1)]
    for s in range(QT_N):
        if s + 1 < QT_N:
            g += [("s", s + 1, 0), ("s", s + 1, 1)]
        if s == VALUES_STEP:
            t.append("soft")
        t += [("p", s)] * (len(rounds(ORDER[s])) - 1)
        if s >= 1:
            t.append(("o", s - 1))
        if s == SOFTMAX_STEP:
            g.append(("soft",))
    t += [("o", QT_N - 1), ("o", QT_N)]
    g += [("wh", m) for m in range(KC)]
    return {k: n for n, k in enumerate(g)}, {k: n for n, k in enumerate(t)}


HG, HT = head_uses()
G_HEAD, T_HEAD, O_HEAD = len(HG), len(HT), QT_N + 1
assert G_HEAD % 2 == 0
G_SETUP = 10
G_FFN = 2 + KC
G0_HEADS = 1
G0_NORM2 = G0_HEADS + G_HEAD * N_HEADS
G0_A0 = G0_NORM2 + 1
G0_FFN = G0_A0 + 1
G_LAYER = G0_FFN + G_FFN * (FC - 1) + G_FFN - 1
assert G_LAYER % 2 == 0
T0_HEADS = 1
T0_NORM2 = T0_HEADS + T_HEAD * N_HEADS
T0_FFN = T0_NORM2 + 1
T_LAYER = T0_FFN + 2 * FC
W_CREDIT, K_CREDIT, V_CREDIT = SLOTS, 2, 2

CON = {}
for _name, _width in (("ident", P), ("ones", P), ("causal", P), ("delta", 64), ("rowsel", 8), ("sign", 2),
                      ("compsel", 2), ("group", 1), ("neghalf", 1), ("eps", 1), ("poolstep", 16), ("poolinv", 4), ("poolhead", 64), ("lam_init", DEPTH),
                      ("one_minus", DEPTH), ("cos", T), ("sin", T)):
    _at = sum(w for _, w in CON.values())
    CON[_name] = (_at, _width)
CON_W = sum(w for _, w in CON.values())

PAR = {}
for _name, _n in (("conv_w", CONV_TAPS * FC), ("conv_b", FC), ("norm1_g", KC), ("norm2_g", KC), ("pool_scale", 4),
                  ("subln_g", 1), ("final_g", KC)):
    PAR[_name] = (sum(n for _, n in PAR.values()), _n)
PAR_W = sum(n for _, n in PAR.values())


def constants():
    c = np.zeros((P, CON_W), np.float32)

    def put(name, value, rows=slice(None)):
        a, w = CON[name]
        c[rows, a:a + w] = np.asarray(value, np.float32).reshape(-1, w) if np.ndim(value) else value

    put("ident", np.eye(P))
    put("ones", 1.0)
    put("causal", np.where(np.arange(P)[None, :] > np.arange(P)[:, None], NEG, 0.0))
    put("delta", np.broadcast_to(np.eye(8).reshape(1, 64), (P, 64)))
    put("rowsel", np.tile(np.eye(8), (2, 1)), slice(0, 16))
    put("sign", np.repeat([[1.0, 0.0], [0.0, -1.0]], 8, axis=0), slice(0, 16))
    put("compsel", np.repeat(np.eye(2), 64, axis=0))
    put("group", (np.arange(P) % GROUPS).reshape(P, 1))
    put("neghalf", -0.5)
    put("eps", VDIM * EPS)
    put("poolstep", np.broadcast_to([[1.0 if k <= g else 0.0 for g in range(4) for k in range(4)]], (P, 16)))
    put("poolinv", np.broadcast_to([[1.0 / w for w in POOL_WINDOWS]], (P, 4)))
    put("poolhead", np.broadcast_to([[1.0 / min(t + 1, w) for w in POOL_WINDOWS for t in range(16)]], (P, 64)))
    li = [0.8 - 0.6 * math.exp(-0.3 * n) for n in range(DEPTH)]
    put("lam_init", np.broadcast_to([li], (P, DEPTH)))
    put("one_minus", np.broadcast_to([[1.0 - x for x in li]], (P, DEPTH)))
    half = HEAD_DIM // 2
    inv = (1.0 / (np.float32(ROPE_THETA) ** (np.arange(half, dtype=np.float32) * np.float32(2.0 / HEAD_DIM)))
           ).astype(np.float32)
    pos = np.concatenate([np.arange(SEQ), np.full(DEC_BATCH, PAST_LEN)]).astype(np.float32)
    ang = (pos[None, :] * inv[:, None]).astype(np.float32).astype(np.float64)
    cos, sin = np.cos(ang), np.sin(ang)
    put("cos", np.tile(cos, (4, 1)))
    put("sin", np.concatenate([-sin, sin, -sin, sin]))
    return c


def hybrid_decoder_kernel(nc, x_prompt, x_sample, cache_k, cache_v, state_pool, state_conv, page_table, norm1_g, w_in,
                          pool_w, pool_scale, lam_q1, lam_k1, lam_q2, lam_k2, subln_g, w_out, norm2_g, w_up, conv_w,
                          conv_b, w_down, final_g, table, y_prompt, y_sample, k_new_prompt, v_new_prompt,
                          pool_new_prompt, conv_new_prompt, k_new_sample, v_new_sample, pool_new_sample,
                          conv_new_sample):
    with ExitStack() as ctx:
        def sb(name, shape, dt=F32):
            return ctx.enter_context(nc.sbuf_tensor(name, shape, dt))

        def sem(name):
            return ctx.enter_context(nc.semaphore(name))

        resid = sb("resid", [P, KC, T])
        act_hi = sb("act_hi", [P, KC, T], F32R)
        act_lo = sb("act_lo", [P, KC, T], F32R)
        w_raw = sb("w_raw", [P, SLOTS, 1024])
        w_hi = sb("w_hi", [P, SLOTS, 1024], F32R)
        w_lo = sb("w_lo", [P, SLOTS, 1024], F32R)
        con = sb("con", [P, CON_W])
        par = sb("par", [P, DEPTH, P])
        scratch = sb("scratch", [P, 3104])
        rot = sb("rot", [P, 1168])
        bq = sb("bq", [P, T])
        qT = sb("qT", [P, T])
        kT = sb("kT", [P, T])
        v_tok = sb("v_tok", [P, QT_N, P])
        k_tok = v_tok
        mix_hi = sb("mix_hi", [P, T], F32R)
        mix_lo = sb("mix_lo", [P, T], F32R)
        a_T = sb("a_T", [P, 2, 512])
        k_page = sb("k_page", [P, 2, N_PAGES, P])
        v_page = sb("v_page", [P, 2, N_PAGES, P])
        stat = sb("stat", [P, 2, 8])
        small = sb("small", [P, 48])
        rs = sb("rs", [P, QT_N + 1])
        pw = sb("pw", [P, P])
        state_in = sb("state_in", [120, P])
        rows_out = sb("rows_out", [P, P])
        v_dup = sb("v_dup", [16, P])
        lam = sb("lam", [P, 16])
        pages = sb("pages", [P, DEC_BATCH], I32)
        idx_k = sb("idx_k", [P, DEC_BATCH], I32)
        idx_v = sb("idx_v", [P, DEC_BATCH], I32)
        idx_now = sb("idx_now", [P, 1], I32)
        idx_inc = sb("idx_inc", [P, DEC_BATCH], I32)

        bank = ctx.enter_context(nc.psum_tensor("bank", [P, 8, 512], F32))
        t_bank = bank[:, 6, :]
        o_bank = bank[:, 7, :]
        p_bank = bank[:, 2, :]
        s_bank = bank[:, 5, :]

        table_in, params_in, lam_in_s, pages_in = sem("table_in"), sem("params_in"), sem("lam_landed"), sem("pages_in")
        x_in = [sem(f"x_in{i}") for i in range(3)]
        w_in_s = [sem(f"w_landed{i}") for i in range(SLOTS)]
        k_in = [sem(f"k_landed{i}") for i in range(2)]
        v_in = [sem(f"v_landed{i}") for i in range(2)]
        pw_in, sp_in, sc_in = sem("pool_w_landed"), sem("state_pool_landed"), sem("state_conv_landed")
        k_out_s, v_out_s, small_out, u_out_s = sem("k_stored"), sem("v_stored"), sem("small_stored"), sem("u_stored")
        conv_out_s, pool_copy, y_out = sem("conv_stored"), sem("pool_copied"), [sem("y_stored0"), sem("y_stored1")]
        g_full, g_free = [sem("group0_full"), sem("group1_full")], [sem("group0_free"), sem("group1_free")]
        t_full, t_free = sem("tbank_full"), sem("tbank_free")
        p_full, p_free = sem("pbank_full"), sem("pbank_free")
        o_full, o_free = sem("obank_full"), sem("obank_free")
        w_hi_done, w_lo_done = sem("w_hi_done"), sem("w_lo_done")
        sq_done, acc_done, y_done, hi_done = sem("sq_done"), sem("acc_done"), sem("y_done"), sem("act_hi_done")
        lo_pool, lo_dve = sem("act_lo_pool"), sem("act_lo_dve")
        pool_d, roped, diag_done = sem("pool_d_done"), sem("roped"), sem("diag_done")
        y_hi_done, k_mul, k_red = sem("pool_y_hi_done"), sem("k_multiplied"), sem("k_reduced")
        att_bias, att_a, att_sq, mix_hi_done = sem("att_bias"), sem("att_weights"), sem("att_squares"), sem("mix_hi_done")
        idx_ready, idx_step = sem("idx_ready"), sem("idx_step")
        att_rms, pool_step, norm_diag, norm_rs = sem("att_rms"), sem("pool_step"), sem("norm_diag"), sem("norm_rs")
        soft_bias, soft_sel, v_used = sem("soft_bias"), sem("soft_sel"), sem("v_used")
        taps0, conv_done, silu_done, g_hi_done, g_lo_done = (sem("tap2_done"), sem("conv_done"), sem("silu_done"),
                                                             sem("gate_hi_done"), sem("gate_lo_done"))
        dve_step, act_step, lam_sum, lam_exp = sem("dve_step"), sem("act_step"), sem("lam_sum"), sem("lam_exp")

        def c_(name, rows=slice(None)):
            a, w = CON[name]
            return con[rows, a:a + w]

        def sl(n, width):
            return slice(n, n + width) if isinstance(n, int) else bass.ds(n, width)

        def c_at(name, n, width=1, rows=slice(None)):
            a, _ = CON[name]
            return con[rows, sl(n + a, width)]

        def p_at(name, layer, n, width=1):
            a, _ = PAR[name]
            return par[:, layer, sl(n + a, width)]

        ident, ones = c_("ident"), c_("ones")

        def grp(p):
            return bank[:, 3 * p:3 * p + 3, :]

        def grp3(p):
            return bank[:, 3 * p:3 * p + 3, 0:TW]

        def tiles(ap):
            return ap.rearrange("p (a b) -> p a b", a=NT)

        sq_ring = [scratch[:, i * T:(i + 1) * T] for i in range(3)]
        ue, pool_a, pool_b = scratch[:, 0:1167], scratch[:, 1167:2334], rot[:, 0:1167]
        pool_dd = scratch[:, 1167:1167 + T]
        v_T = rot[:, 0:T]
        ext, conv_c = scratch[:, 0:1050], scratch[:, 1050:2098]
        ext_tail = ext[:, 1024:1050]
        gate = rot[:, 0:T]
        spread = rot[:, 0:512].rearrange("p (j b a) -> p j b a", j=N_PAGES, b=8)
        o_norm = rot[:, 512:768].rearrange("p (s d) -> p s d", s=2)
        junk = rot[:, 768:896]
        s_score = rot[:, T + 8:T + 136].rearrange("p (c b j) -> p c b j", c=2, b=8)
        u_out, us_out, ks_out, conv_out = (rows_out[0:POOL_HIST, :], rows_out[32:40, :], rows_out[64:72, :],
                                           rows_out[96:122, :])
        lam_in = a_T[:, 0, :].rearrange("p (n d) -> p n d", n=4)
        soft = bq[0:16, 0:1025]
        probs = [scratch[:, 0:2048].rearrange("p (c k) -> p c k", c=2),
                 scratch[:, 2048:3072].rearrange("p (c k) -> p c k", c=2)]
        u_hist = ue[:, 1039:1167].rearrange("p (b j) -> p b j", b=8)
        qk8, comp8 = small[:, 0:8], small[:, 8:24].rearrange("p (c b) -> p c b", c=2)
        sel8, diag8 = small[0:16, 24:32], small[0:16, 32:40]
        soft_m, soft_nb, soft_l, soft_cf = (small[0:16, 40:41], small[0:16, 41:42], small[0:16, 42:43],
                                            small[0:16, 43:44])
        sub_gain = small[:, 44:45]
        soft_sign = lam[0:16, 8:10]

        def use(half, j):
            return j % 2, half + j // 2

        def use_head(l, h, name):
            return use(G_SETUP // 2 + l * (G_LAYER // 2) + h * (G_HEAD // 2), G0_HEADS + HG[name])

        def use_ffn(l, i, j):
            return use(G_SETUP // 2 + l * (G_LAYER // 2) + i * (G_FFN // 2), G0_FFN + j)

        def use_layer(l, j):
            return use(G_SETUP // 2 + l * (G_LAYER // 2), j)

        def full(eng, u):
            eng.wait_ge(g_full[u[0]], u[1] + 1)

        def released(eng, u):
            eng.wait_ge(g_free[u[0]], u[1] + 2)

        def t_head(l, h, name):
            return l * T_LAYER + h * T_HEAD + (T0_HEADS + HT[name])

        def t_ffn(l, i, j):
            return l * T_LAYER + i * 2 + (T0_FFN + j)

        def w_landed(eng, l, h_or_i, off, per):
            eng.wait_ge(w_in_s[off % SLOTS], (l * (U_LAYER // SLOTS) + h_or_i * per + off // SLOTS) * 16 + 16)

        N_POOL = cache_k.shape[0] // (DEPTH * N_HEADS * GROUPS)

        block = ctx.enter_context(nc.Block())

        @block.sync
        def _(sp):
            sp.dma_start(con[:, :], table).then_inc(table_in, 16)
            for j in range(N_PAGES):
                sp.dma_start(pages[j * GROUPS:(j + 1) * GROUPS, :],
                             page_table[j:j + 1, :].broadcast_to([GROUPS, DEC_BATCH])).then_inc(pages_in, 16)
            for l in range(DEPTH):
                rows = [("conv_w", conv_w[l].rearrange("j (c p) -> (j c) p", p=P)),
                        ("conv_b", conv_b[l].rearrange("(c p) -> c p", p=P)),
                        ("norm1_g", norm1_g[l].rearrange("(c p) -> c p", p=P)),
                        ("norm2_g", norm2_g[l].rearrange("(c p) -> c p", p=P)),
                        ("pool_scale", pool_scale[l].rearrange("(c p) -> c p", p=P)),
                        ("subln_g", subln_g[l].rearrange("(c p) -> c p", p=P)),
                        ("final_g", final_g.rearrange("(c p) -> c p", p=P))]
                for name, src in rows:
                    a, n = PAR[name]
                    sp.dma_start(k_tok[a:a + n, l, :], src).then_inc(params_in, 16)
            for n, v in enumerate((lam_q1, lam_k1, lam_q2, lam_k2)):
                src = v.rearrange("l d -> (l d)").rearrange("(a n) -> a n", a=1).broadcast_to([P, DEPTH * HEAD_DIM])
                sp.dma_start(lam_in[:, n, :], src).then_inc(lam_in_s, 16)
            for t in range(QT_N + 1):
                if t >= 3:
                    released(sp, use(0, t - 3))
                if t < QT_N:
                    sp.dma_start(scratch[:, 1024 * (t % 3):1024 * (t % 3) + 1024], x_prompt[0, t * P:(t + 1) * P, :]
                                 ).then_inc(x_in[t % 3], 16)
                else:
                    sp.dma_start(scratch[0:8, 1024 * (t % 3):1024 * (t % 3) + 1024],
                                 x_sample.rearrange("b a d -> (b a) d")).then_inc(x_in[t % 3], 16)

            def load_unit(n, slot, src):
                sp.wait_ge(w_lo_done, n + 1)
                sp.dma_start(w_raw[:, slot, :], src).then_inc(w_in_s[slot], 16)

            def head_loads(l, h, next_units):
                it = l * N_HEADS + h
                sp.wait_ge(y_hi_done, it + 1)
                sp.dma_start(pw[:, :], pool_w[l, h]).then_inc(pw_in, 16)
                sp.wait_ge(t_full, l * T_LAYER)
                sp.dma_start(state_in[:, :], state_pool[l].rearrange("b j c -> (b j) c")[:, sl(h * P, P)]
                             ).then_inc(sp_in, 16)
                n0 = l * U_LAYER + h * U_HEAD
                load_unit(n0 + 2, 2, w_in[l, h + 8])
                load_unit(n0 + 3, 0, w_in[l, h + 12])
                load_unit(n0 + 4, 1, w_out[l, sl(h * P, P), :])
                load_unit(n0 + 5, 2, w_out[l, sl(h * P + POOL_W, P), :])

                next_units(n0 + U_HEAD)

            with sp.Fori(0, DEPTH) as l:
                def load_u_q(h, n0):
                    load_unit(n0, 0, w_in[l, h])
                    load_unit(n0 + 1, 1, w_in[l, h + 4])

                def load_a_b(n0):
                    load_unit(n0, 0, w_up[l, 0])
                    load_unit(n0 + 1, 1, w_up[l, FC])

                load_u_q(0, l * U_LAYER)
                with sp.Fori(0, N_HEADS - 1) as h:
                    head_loads(l, h, lambda n0: load_u_q(h + 1, n0))
                head_loads(l, N_HEADS - 1, load_a_b)

                def load_state(c):
                    sp.wait_ge(t_full, l * T_LAYER + c * 2 + (T0_FFN - 1))
                    sp.dma_start(state_in[0:16, :],
                                 state_conv[l].rearrange("b j c -> (b j) c")[:, sl(c * P, P)]
                                 ).then_inc(sc_in, 16)

                def load_a(i, n, slot):
                    load_unit(n, slot, w_up[l, i])

                def load_b(i, n, slot):
                    load_unit(n, slot, w_up[l, i + FC])

                def load_d(i, n, slot):
                    load_unit(n, slot, w_down[l, sl(i * P, P), :])

                f0 = l * U_LAYER + U_FFN0
                load_state(0)
                with sp.Fori(0, FC - 1) as i:
                    load_a(i + 1, f0 + i * 3 + 2, 2)
                    load_state(i + 1)
                    load_d(i, f0 + i * 3 + 3, 0)
                    load_b(i + 1, f0 + i * 3 + 4, 1)
                load_d(FC - 1, f0 + 3 * FC - 1, 2)

        @block.gpsimd
        def _(pool):
            for l in range(DEPTH):
                pool.dma_start(pool_new_sample[l, :, 0:POOL_HIST - 1, :], state_pool[l, :, 1:POOL_HIST, :]
                               ).then_inc(pool_copy, 16)

            def split_lo(n, slot):
                pool.wait_ge(w_hi_done, n + 1)
                pool.tensor_tensor(w_lo[:, slot, :], w_raw[:, slot, :], w_hi[:, slot, :].bitcast(F32), ALU.subtract
                                   ).then_inc(w_lo_done, 1)

            pool.memset(junk[:, :], 0.0).then_inc(w_lo_done, W_CREDIT)
            pool.wait_ge(w_lo_done, W_CREDIT)

            neghalf = c_("neghalf")
            IDX_STEPS = 2 * DEC_BATCH + 2
            pool.wait_ge(idx_ready, 1)

            def norm_lo(ni, t_use):
                norm_rms(ni, t_use)
                for k in range(0, KC, 2):
                    pool.wait_ge(hi_done, ni * KC + k + 1)
                    pool.tensor_tensor(act_lo[:, k, :], sq_ring[k % 3], act_hi[:, k, :].bitcast(F32), ALU.subtract
                                       ).then_inc(lo_pool, 1)

            def norm_rms(ni, t_use):
                pool.wait_ge(t_free, t_use + 2)
                pool.tensor_tensor(rs[:, :], rs[:, :], neghalf.broadcast_to([P, QT_N + 1]), ALU.pow
                                   ).then_inc(norm_rs, 1)

            def head_rms(l, it, s):
                rows = P if s < QT_N else 8
                ss = stat[0:rows, s % 2, 6:7]
                pool.wait_ge(att_sq, it * O_HEAD + s + 1)
                pool.tensor_tensor(ss, ss, c_("eps")[0:rows], ALU.add).then_inc(pool_step, 1)
                pool.wait_ge(pool_step, it * O_HEAD + s + 1)
                pool.tensor_tensor(ss, ss, neghalf[0:rows], ALU.pow).then_inc(att_rms, 1)

            with pool.Fori(0, DEPTH) as l:
                n0 = l * U_LAYER
                split_lo(n0, 0)
                split_lo(n0 + 1, 1)
                norm_lo(l * 2, l * T_LAYER)
                with pool.Fori(0, N_HEADS) as h:
                    it = l * N_HEADS + h
                    n = l * U_LAYER + h * U_HEAD

                    def k_product(b):
                        pool.wait_ge(k_in[b % 2], (it * 4 + b // 2 + 1) * 16)
                        kp = k_page[:, b % 2, :, :]
                        q_row = bq[:, None, b * P:(b + 1) * P].broadcast_to([P, N_PAGES, P])
                        pool.tensor_tensor(kp, kp, q_row, ALU.mult).then_inc(k_mul, 1)

                    steps = 0

                    def index_step(out, in0, in1):
                        nonlocal steps
                        pool.wait_ge(idx_step, it * IDX_STEPS + steps)
                        pool.tensor_tensor(out, in0, in1, ALU.add).then_inc(idx_step, 1)
                        steps += 1

                    def load(b, cache, dst, rows, landed, used):
                        pool.wait_ge(used, it * DEC_BATCH + b + 1)
                        index_step(idx_now[:, :], rows[:, b:b + 1], idx_inc[:, 0:1])
                        pool.indirect_dma_start(dst[:, b % 2, :, :].rearrange("p t d -> p (t d)"), None, cache,
                                                bass.IndirectOffsetOnAxis(rows[:, b:b + 1], 0)
                                                ).then_inc(landed[b % 2], 16)

                    def k_load(b):
                        load(b, cache_k, k_page, idx_k, k_in, k_red)

                    def v_load(b):
                        load(b, cache_v, v_page, idx_v, v_in, v_used)

                    k_load(0)
                    k_load(1)
                    v_load(0)
                    v_load(1)
                    split_lo(n + 2, 2)
                    split_lo(n + 3, 0)
                    split_lo(n + 4, 1)
                    released(pool, use_head(l, h, ("qb", 1)))
                    k_product(0)
                    k_product(1)
                    k_load(2)
                    split_lo(n + 5, 2)
                    for b in range(2, DEC_BATCH):
                        if b + 1 < DEC_BATCH:
                            k_load(b + 1)
                        k_product(b)
                    index_step(idx_k[:, :], idx_k[:, :], idx_inc[:, :])
                    split_lo(n + 6, 0)
                    split_lo(n + 7, 1)
                    for s in range(QT_N + 1):
                        head_rms(l, it, s)
                        if VALUES_STEP <= s < VALUES_STEP + DEC_BATCH - 2:
                            v_load(s - VALUES_STEP + 2)
                    for s in range(2):
                        pool.wait_ge(v_in[s], (it + 1) * 16 * (DEC_BATCH // 2))
                    index_step(idx_v[:, :], idx_v[:, :], idx_inc[:, :])
                    assert steps == IDX_STEPS
                norm_lo(l * 2 + 1, l * T_LAYER + T0_NORM2)
                f0 = l * U_LAYER + U_FFN0
                split_lo(f0 + 2, 2)
                with pool.Fori(0, FC - 1) as i:
                    split_lo(f0 + i * 3 + 3, 0)
                    split_lo(f0 + i * 3 + 4, 1)
                    split_lo(f0 + i * 3 + 5, 2)
            norm_rms(2 * DEPTH, DEPTH * T_LAYER)
            pool.wait_ge(pool_copy, 16 * DEPTH)

        def act_y(t):
            n = t // 2
            return [scratch[:, 0:1024], scratch[:, 2048:3072], qT[:, 0:1024], kT[:, 0:1024], bq[:, 0:1024]][n]

        @block.scalar
        def _(act):
            def split_hi(l, idx, off, per, last_use):
                w_landed(act, l, idx, off, per)
                full(act, last_use)
                act.activation(w_hi[:, off % SLOTS, :], w_raw[:, off % SLOTS, :], ACT.Copy).then_inc(w_hi_done, 1)

            def norm_sums(ni, t_use):
                act.wait_ge(t_full, t_use + 1)
                act.wait_ge(norm_diag, ni * 2)
                act.activation(rs[:, 0:QT_N], t_bank[:, 0:QT_N], ACT.Copy).then_inc(act_step, 1)
                act.activation(rs[0:8, QT_N:QT_N + 1], t_bank[0:8, QT_N:QT_N + 1], ACT.Copy).then_inc(t_free, 1)

            def norm(ni, last_add, t_use):
                released(act, last_add)
                act.activation(rot[:, 0:T], resid[:, 0, :], ACT.Square).then_inc(sq_done, 1)
                for k in range(1, KC):
                    if k >= 3:
                        act.wait_ge(acc_done, ni * (KC - 1) + k - 2)
                    act.activation(sq_ring[k % 2], resid[:, k, :], ACT.Square).then_inc(sq_done, 1)
                norm_sums(ni, t_use)
                for k in range(KC):
                    act.wait_ge(y_done, ni * KC + k + 1)
                    act.activation(act_hi[:, k, :], sq_ring[k % 3], ACT.Copy).then_inc(hi_done, 1)

            act.wait_ge(lam_sum, 1)
            act.activation(lam[:, 4:8], lam[:, 0:4], ACT.Exp).then_inc(lam_exp, 1)

            with act.Fori(0, DEPTH) as l:
                split_hi(l, 0, 0, 0, (0, l * (G_LAYER // 2)))
                split_hi(l, 0, 1, 0, (1, l * (G_LAYER // 2)))
                norm(l * 2, (1, G_SETUP // 2 - 1 + l * (G_LAYER // 2)), l * T_LAYER)

                with act.Fori(0, N_HEADS) as h:
                    it = l * N_HEADS + h
                    ug = lambda name: use_head(l, h, name)
                    ta = lambda name: t_head(l, h, name)

                    def hi(off, last_use):
                        split_hi(l, h, off, 2, last_use)

                    hi(2, use(G_SETUP // 2 + l * (G_LAYER // 2) + h * (G_HEAD // 2), 0))
                    full(act, ug(("u",)))
                    act.wait_ge(t_full, ta("state") + 1)
                    act.activation(u_hist[:, :, 0:POOL_HIST],
                                   t_bank[:, 0:120].rearrange("p (b j) -> p b j", b=8), ACT.Copy).then_inc(t_free, 1)
                    g = grp(ug(("u",))[0])
                    act.activation(ue[:, 15:15 + 2 * TW].rearrange("p (a b) -> p a b", a=2), g[:, 0:2, 0:TW], ACT.Copy
                                   ).then_inc(act_step, 1)
                    act.activation(ue[:, 15 + 2 * TW:15 + SEQ], g[:, 2, 0:TW - 8], ACT.Copy).then_inc(act_step, 1)
                    act.activation(u_hist[:, :, POOL_HIST], g[:, 2, TW - 8:TW], ACT.Copy
                                   ).then_inc(g_free[ug(("u",))[0]], 1)
                    hi(3, ug(("u",)))

                    def raw(name, dst):
                        u = ug(name)
                        full(act, u)
                        act.activation(tiles(dst[:, :]), grp3(u[0]), ACT.Copy).then_inc(g_free[u[0]], 1)

                    raw(("q",), qT)
                    act.wait_ge(t_full, ta("uout") + 1)
                    act.wait_ge(u_out_s, it * 32)
                    act.activation(u_out[:, :], t_bank[0:POOL_HIST, 0:P], ACT.Copy).then_inc(act_step, 1)
                    act.activation(us_out[:, :], t_bank[0:8, P:2 * P], ACT.Copy).then_inc(t_free, 1)
                    act.wait_ge(t_free, ta("uout") + 2)
                    act.dma_start(pool_new_prompt[l, 0, :, bass.ds(h * P, P)], u_out[:, :]).then_inc(u_out_s, 16)
                    act.dma_start(pool_new_sample[l, :, POOL_HIST - 1, bass.ds(h * P, P)], us_out[:, :]
                                  ).then_inc(u_out_s, 16)
                    hi(4, ug(("q",)))
                    raw(("k",), kT)
                    for n in range(2):
                        full(act, ug(("qb", n)))
                        act.activation(bq[:, n * 512:(n + 1) * 512], grp(ug(("qb", n))[0])[:, 0, :], ACT.Copy
                                       ).then_inc(g_free[ug(("qb", n))[0]], 1)
                    hi(5, ug(("k",)))
                    full(act, ug(("v",)))
                    act.wait_ge(roped, it * 2 + 2)
                    act.activation(rot[:, T:T + 8], grp(ug(("v",))[0])[:, NT - 1, TW - 8:TW], ACT.Copy
                                   ).then_inc(act_step, 1)
                    act.activation(tiles(v_T), grp3(ug(("v",))[0]), ACT.Copy).then_inc(g_free[ug(("v",))[0]], 1)
                    act.wait_ge(v_out_s, it * 16)
                    for r in range(2):
                        act.wait_ge(t_full, ta(("k", r)) + 1)
                        act.activation(k_tok[:, 4 * r:4 * r + 4, :], t_bank.rearrange("p (a b) -> p a b", a=4), ACT.Copy
                                       ).then_inc(t_free, 1)
                    act.wait_ge(t_free, ta(("k", 1)) + 2)
                    act.dma_start(k_new_prompt[l, 0, :, :, h, :].rearrange("t p d -> p t d"), k_tok[:, :, :]
                                  ).then_inc(k_out_s, 16)
                    act.wait_ge(t_full, ta("small") + 1)
                    act.wait_ge(small_out, it * 32)
                    act.activation(ks_out[:, :], t_bank[0:8, 0:P], ACT.Copy).then_inc(act_step, 1)
                    act.activation(v_dup[:, :], t_bank[0:16, P:2 * P], ACT.Copy).then_inc(t_free, 1)
                    act.wait_ge(t_free, ta("small") + 2)
                    act.dma_start(k_new_sample[l, :, 0, h, :], ks_out[:, :]).then_inc(small_out, 16)
                    act.dma_start(v_new_sample[l, :, 0, h, :], v_dup[0:8, :]).then_inc(small_out, 16)
                    full(act, ug(("y",)))
                    act.activation(tiles(mix_hi[:, :]), grp3(ug(("y",))[0]), ACT.Copy,
                                   scale=p_at("pool_scale", l, h)).then_inc(y_hi_done, 1)
                    hi(6, ug(("v",)))
                    act.wait_ge(k_out_s, it * 16 + 16)
                    for r in range(2):
                        act.wait_ge(t_full, ta(("v", r)) + 1)
                        act.activation(v_tok[:, 4 * r:4 * r + 4, :], t_bank.rearrange("p (a b) -> p a b", a=4), ACT.Copy
                                       ).then_inc(t_free, 1)
                    act.wait_ge(t_free, ta(("v", 1)) + 2)
                    act.dma_start(v_new_prompt[l, 0, :, :, h, :].rearrange("t p d -> p t d"), v_tok[:, :, :]
                                  ).then_inc(v_out_s, 16)
                    hi(7, ug(("wg", KC - 1)))

                    def exps(s):
                        width = (ORDER[s] + 1) * P
                        for c in range(2):
                            act.wait_ge(att_bias, it * 2 * QT_N + 2 * s + c + 1)
                            p = ug(("s", s, c))[0]
                            src = bank[:, 3 * p:3 * p + 2, :].rearrange("p a b -> p (a b)")[:, 0:width]
                            act.activation(probs[s % 2][:, c, 0:width], src, ACT.Exp,
                                           bias=stat[:, s % 2, 2 + c:3 + c], scale=HEAD_DIM ** -0.5,
                                           accum_out=stat[:, s % 2, 4 + c:5 + c]).then_inc(g_free[p], 1)

                    def squares(s):
                        rows = P if s < QT_N else 8
                        act.wait_ge(o_full, it * O_HEAD + s + 1)
                        src = o_bank if s < QT_N else s_bank
                        act.activation(junk[0:rows, :], src[0:rows, 0:P], ACT.Square,
                                       accum_out=stat[0:rows, s % 2, 6:7]).then_inc(att_sq, 1)

                    def mix(s):
                        at, n = (ORDER[s] * P, P) if s < QT_N else (SEQ, 8)
                        act.wait_ge(t_full, ta(("o", s)) + 1)
                        act.activation(mix_hi[:, at:at + n], t_bank[:, 0:n], ACT.Copy, scale=sub_gain
                                       ).then_inc(mix_hi_done, 1)

                    exps(0)
                    for s in range(QT_N):
                        if s >= 2:
                            mix(s - 2)
                        if s >= 1:
                            squares(s - 1)
                        for r, blocks in enumerate(rounds(ORDER[s])):
                            if r == 0:
                                act.wait_ge(p_full, it * QT_N + s + 1)
                                act.activation(a_T[:, 0, 0:P * len(blocks)], p_bank[:, 0:P * len(blocks)], ACT.Copy
                                               ).then_inc(p_free, 1)
                            else:
                                act.wait_ge(t_full, ta(("p", s)) + 1)
                                act.activation(a_T[:, 1, 0:P * len(blocks)], t_bank[:, 0:P * len(blocks)], ACT.Copy
                                               ).then_inc(t_free, 1)
                        if s + 1 < QT_N:
                            exps(s + 1)
                        if s == SOFTMAX_STEP:
                            act.wait_ge(soft_bias, it + 1)
                            p = ug(("soft",))[0]
                            act.activation(soft[:, 0:PAST_LEN],
                                           bank[0:16, 3 * p:3 * p + 2, :].rearrange("p a b -> p (a b)"), ACT.Exp,
                                           bias=soft_nb, scale=HEAD_DIM ** -0.5, accum_out=soft_l
                                           ).then_inc(act_step, 1)
                            act.activation(soft[:, PAST_LEN:PAST_LEN + 1], bank[0:16, 3 * p + 2, 0:1], ACT.Exp,
                                           bias=soft_nb, scale=HEAD_DIM ** -0.5).then_inc(g_free[p], 1)
                    mix(QT_N - 2)
                    squares(QT_N - 1)
                    mix(QT_N - 1)
                    squares(QT_N)
                    mix(QT_N)

                norm(l * 2 + 1, use_layer(l, G0_NORM2 - 1), l * T_LAYER + T0_NORM2)

                def evacuate_a(c, u):
                    full(act, u)
                    act.wait_ge(t_full, t_ffn(l, c, 0) + 1)
                    act.wait_ge(conv_done, l * FC + c)
                    rows = ext[:, 1026:1050].rearrange("p (b j) -> p b j", b=8)
                    act.activation(rows[:, :, 0:2], t_bank[:, 0:16].rearrange("p (b j) -> p b j", b=8), ACT.Copy
                                   ).then_inc(t_free, 1)
                    g = grp(u[0])
                    act.activation(ext[:, 2:2 + 2 * TW].rearrange("p (a b) -> p a b", a=2), g[:, 0:2, 0:TW], ACT.Copy
                                   ).then_inc(act_step, 1)
                    act.activation(ext[:, 2 + 2 * TW:2 + SEQ], g[:, 2, 0:TW - 8], ACT.Copy).then_inc(act_step, 1)
                    act.activation(rows[:, :, 2], g[:, 2, TW - 8:TW], ACT.Copy).then_inc(g_free[u[0]], 1)
                    released(act, u)
                    act.activation(conv_c[:, :], ext[:, 2:1050], ACT.Identity, bias=p_at("conv_b", l, c),
                                   scale=p_at("conv_w", l, c + 2 * FC)).then_inc(taps0, 1)

                def silu(c):
                    act.wait_ge(conv_done, l * FC + c + 1)
                    act.wait_ge(g_lo_done, l * FC + c)
                    act.activation(gate[:, 0:SEQ], conv_c[:, 0:SEQ], ACT.Silu).then_inc(act_step, 1)
                    act.activation(gate[:, SEQ:T], conv_c[:, 1026:1048:3], ACT.Silu).then_inc(silu_done, 1)

                def store_conv(c):
                    act.wait_ge(t_full, t_ffn(l, c, 1) + 1)
                    act.wait_ge(conv_out_s, (l * FC + c) * 48)
                    act.activation(conv_out[:, :], t_bank[0:26, 0:P], ACT.Copy).then_inc(t_free, 1)
                    act.wait_ge(t_free, t_ffn(l, c, 1) + 2)
                    act.dma_start(conv_new_prompt[l, 0, :, sl(c * P, P)], conv_out[0:2, :]
                                  ).then_inc(conv_out_s, 16)
                    for j in range(2):
                        act.dma_start(conv_new_sample[l, :, j, sl(c * P, P)], rows_out[99 + j:122:3, :]
                                      ).then_inc(conv_out_s, 16)

                def gate_hi(c, u):
                    released(act, u)
                    act.activation(mix_hi[:, :], gate[:, :], ACT.Copy).then_inc(g_hi_done, 1)

                split_hi(l, 0, U_FFN0 + 2, 0, use_layer(l, G0_NORM2 - 1))
                evacuate_a(0, use_layer(l, G0_A0))
                silu(0)
                with act.Fori(0, FC - 1) as i:
                    split_hi(l, i, U_FFN0 + 3, 1, use_ffn(l, i, -1))
                    store_conv(i)
                    gate_hi(i, use_ffn(l, i, 0))
                    split_hi(l, i, U_FFN0 + 4, 1, use_ffn(l, i, 0))
                    evacuate_a(i + 1, use_ffn(l, i, 1))
                    split_hi(l, i, U_FFN0 + 5, 1, use_ffn(l, i, 1))
                    silu(i + 1)
                store_conv(FC - 1)
                gate_hi(FC - 1, use_ffn(l, FC - 1, 0))

            last = DEPTH * (G_LAYER // 2)
            released(act, (1, G_SETUP // 2 - 1 + last))
            act.activation(rot[:, 0:T], resid[:, 0, :], ACT.Square).then_inc(sq_done, 1)
            for k in range(1, KC):
                if k >= 3:
                    act.wait_ge(acc_done, 2 * DEPTH * (KC - 1) + k - 2)
                act.activation(sq_ring[k % 2], resid[:, k, :], ACT.Square).then_inc(sq_done, 1)
            norm_sums(2 * DEPTH, DEPTH * T_LAYER)
            for t in range(1, QT_N + 1):
                if t % 2 == 0:
                    continue
                u = use(G_SETUP // 2 + last, 1 + t)
                full(act, u)
                if t >= 2:
                    act.wait_ge(y_out[1], 16 * (t // 2))
                src = bank[:, 3 * u[0]:3 * u[0] + 2, :].rearrange("p a b -> p (a b)")
                act.activation(scratch[:, 1024:2048], src, ACT.Copy).then_inc(g_free[u[0]], 1)
                released(act, u)
                act.dma_start(y_prompt[0, t * P:(t + 1) * P, :], scratch[:, 1024:2048]).then_inc(y_out[1], 16)
            for t in range(0, QT_N + 1, 2):
                rows = P if t < QT_N else 8
                dst = y_prompt[0, t * P:(t + 1) * P, :] if t < QT_N else y_sample.rearrange("b a d -> (b a) d")
                released(act, use(G_SETUP // 2 + last, 1 + t))
                act.dma_start(dst, act_y(t)[0:rows, :]).then_inc(y_out[0], 16)
            act.wait_ge(k_out_s, 16 * DEPTH * N_HEADS)
            act.wait_ge(v_out_s, 16 * DEPTH * N_HEADS)
            act.wait_ge(small_out, 32 * DEPTH * N_HEADS)
            act.wait_ge(u_out_s, 32 * DEPTH * N_HEADS)
            act.wait_ge(conv_out_s, 48 * DEPTH * FC)
            act.wait_ge(y_out[0], 16 * (QT_N // 2 + 1))
            act.wait_ge(y_out[1], 16 * (QT_N // 2))

        @block.tensor
        def _(pe):
            def wait_free(u):
                pe.wait_ge(g_free[u[0]], u[1] + 1)

            def wait_t(seq):
                pe.wait_ge(t_free, seq + 1)

            def unit_ready(n):
                pe.wait_ge(w_lo_done, n + (1 + W_CREDIT))

            def up_unit(n, slot, u, norm_index=None):
                unit_ready(n)
                wait_free(u)
                g = grp(u[0])
                for k in range(KC):
                    if norm_index is not None:
                        pe.wait_ge((lo_pool, lo_dve)[k % 2], norm_index * (KC // 2) + k // 2 + 1)
                    for n_, (w, x) in enumerate(((w_hi, act_hi), (w_hi, act_lo), (w_lo, act_hi))):
                        for t in range(NT):
                            ins = pe.matmul(g[:, t, 0:TW], w[:, slot, k * P:(k + 1) * P],
                                            x[:, k, t * TW:(t + 1) * TW], start=(k == 0 and n_ == 0),
                                            stop=(k == KC - 1 and n_ == 2))
                ins.then_inc(g_full[u[0]], 1)

            def down_unit(n, slot, uses):
                unit_ready(n)
                for m in range(KC):
                    u = uses(m)
                    wait_free(u)
                    g = grp(u[0])
                    for n_, (w, x) in enumerate(((w_hi, mix_hi), (w_hi, mix_lo), (w_lo, mix_hi))):
                        for t in range(NT):
                            ins = pe.matmul(g[:, t, 0:TW], w[:, slot, m * P:(m + 1) * P], x[:, t * TW:(t + 1) * TW],
                                            start=(n_ == 0), stop=(n_ == 2))
                    ins.then_inc(g_full[u[0]], 1)

            pe.wait_ge(table_in, 16)
            for t in range(QT_N + 1):
                u = use(0, t)
                wait_free(u)
                pe.wait_ge(x_in[t % 3], 16 * (t // 3 + 1))
                rows = P if t < QT_N else 8
                g = bank[:, 3 * u[0]:3 * u[0] + 2, :].rearrange("p a b -> p (a b)")
                for k in range(KC):
                    at = 1024 * (t % 3) + k * P
                    ins = pe.transpose(g[:, k * P:k * P + rows], scratch[0:rows, at:at + P], ident[0:rows, 0:rows])
                ins.then_inc(g_full[u[0]], 1)
            u = use(0, QT_N + 1)
            wait_free(u)
            pe.wait_ge(params_in, 16 * len(PAR) * DEPTH)
            for l in range(DEPTH):
                ins = pe.transpose(bank[:, 3 * u[0], l * P:l * P + PAR_W], k_tok[0:PAR_W, l, :],
                                   ident[0:PAR_W, 0:PAR_W])
            ins.then_inc(g_full[u[0]], 1)

            def norm_sum(ni, u, t_use):
                wait_t(t_use)
                pe.wait_ge(acc_done, (ni + 1) * (KC - 1))
                for t in range(QT_N + 1):
                    rows = P if t < QT_N else 8
                    ins = pe.matmul(t_bank[0:rows, t:t + 1], rot[:, t * P:t * P + rows], ones[:, 0:1], start=True,
                                    stop=True)
                ins.then_inc(t_full, 1)
                wait_free(u)
                pe.wait_ge(norm_diag, (ni + 1) * 2)
                g = grp(u[0])
                for t in range(NT):
                    ins = pe.matmul(g[:, t, 0:TW], ones, bq[:, t * TW:(t + 1) * TW], start=True, stop=True)
                ins.then_inc(g_full[u[0]], 1)

            with pe.Fori(0, DEPTH) as l:
                norm_sum(l * 2, use_layer(l, 0), l * T_LAYER)
                with pe.Fori(0, N_HEADS) as h:
                    it = l * N_HEADS + h
                    n0 = l * U_LAYER + h * U_HEAD
                    ug = lambda name: use_head(l, h, name)
                    ta = lambda name: t_head(l, h, name)
                    pe.wait_ge(sp_in, (it + 1) * 16)
                    wait_t(ta("state"))
                    pe.transpose(t_bank[:, 0:120], state_in[:, :], ident[0:120, 0:120]).then_inc(t_full, 1)
                    up_unit(n0, 0, ug(("u",)), norm_index=l * 2)
                    up_unit(n0 + 1, 1, ug(("q",)))
                    released(pe, ug(("u",)))
                    wait_t(ta("uout"))
                    pe.transpose(t_bank[0:POOL_HIST, 0:P], ue[:, SEQ:SEQ + POOL_HIST], ident)
                    pe.transpose(t_bank[0:8, P:2 * P], u_hist[:, :, POOL_HIST], ident).then_inc(t_full, 1)
                    up_unit(n0 + 2, 2, ug(("k",)))
                    pe.wait_ge(diag_done, it + 1)
                    for n in range(2):
                        u = ug(("qb", n))
                        wait_free(u)
                        pe.matmul(grp(u[0])[:, 0, :], ones, bq[:, n * 512:(n + 1) * 512], start=True, stop=True
                                  ).then_inc(g_full[u[0]], 1)
                    up_unit(n0 + 3, 0, ug(("v",)))
                    pe.wait_ge(roped, it * 2 + 2)
                    for r in range(2):
                        wait_t(ta(("k", r)))
                        for a in range(4):
                            i = 4 * r + a
                            ins = pe.transpose(t_bank[:, a * P:(a + 1) * P], kT[:, i * P:(i + 1) * P], ident)
                        ins.then_inc(t_full, 1)
                    wait_t(ta("small"))
                    released(pe, ug(("v",)))
                    pe.transpose(t_bank[0:8, 0:P], kT[:, SEQ:T], ident)
                    pe.transpose(t_bank[0:16, P:2 * P], rot[:, SEQ:T + 8], ident
                                 ).then_inc(t_full, 1)
                    u = ug(("y",))
                    wait_free(u)
                    pe.wait_ge(pool_d, it + 1)
                    pe.wait_ge(pw_in, (it + 1) * 16)
                    for t in range(NT):
                        ins = pe.matmul(grp(u[0])[:, t, 0:TW], pw[:, :], pool_dd[:, t * TW:(t + 1) * TW],
                                        start=True, stop=True)
                    ins.then_inc(g_full[u[0]], 1)
                    released(pe, u)
                    down_unit(n0 + 4, 1, lambda m: ug(("wg", m)))
                    for r in range(2):
                        wait_t(ta(("v", r)))
                        for a in range(4):
                            i = 4 * r + a
                            ins = pe.transpose(t_bank[:, a * P:(a + 1) * P], v_T[:, i * P:(i + 1) * P], ident)
                        ins.then_inc(t_full, 1)

                    def scores(s):
                        i = ORDER[s]
                        width = (i + 1) * P
                        for c in range(2):
                            u = ug(("s", s, c))
                            wait_free(u)
                            rows = slice(c * HEAD_DIM, (c + 1) * HEAD_DIM)
                            for n, at in enumerate(range(0, i * P, 512)):
                                w = min(512, i * P - at)
                                pe.matmul(bank[:, 3 * u[0] + n, 0:w], qT[rows, i * P:(i + 1) * P],
                                          kT[rows, at:at + w], start=True, stop=True)
                            last = bank[:, 3 * u[0] + i // 4, (i % 4) * P:(i % 4 + 1) * P]
                            pe.matmul(last, qT[rows, i * P:(i + 1) * P], kT[rows, i * P:(i + 1) * P],
                                      start=True, stop=False)
                            ins = pe.matmul(last, ident, c_("causal"), start=False, stop=True)
                            ins.then_inc(g_full[u[0]], 1)

                    def weigh(s):
                        i = ORDER[s]
                        rr = rounds(i)
                        pe.wait_ge(att_a, it * QT_N + s + 1)
                        for r, blocks in enumerate(rr):
                            to = (p_bank, t_bank)[r]
                            if r == 0:
                                pe.wait_ge(p_free, it * QT_N + s)
                            else:
                                wait_t(ta(("p", s)))
                            for n, b in enumerate(blocks):
                                ins = pe.transpose(to[:, n * P:(n + 1) * P], probs[s % 2][:, 0, b * P:(b + 1) * P],
                                                   ident)
                            ins.then_inc((p_full, t_full)[r], 1)
                        pe.wait_ge(o_free, it * O_HEAD + s + 1)
                        for r, blocks in enumerate(rr):
                            if r == 0:
                                pe.wait_ge(p_free, it * QT_N + s + 1)
                            else:
                                pe.wait_ge(t_free, ta(("p", s)) + 2)
                            for n, b in enumerate(blocks):
                                ins = pe.matmul(o_bank[:, 0:P], a_T[:, r, n * P:(n + 1) * P],
                                                v_tok[:, b, :], start=(b == 0), stop=(b == i))
                        ins.then_inc(o_full, 1)

                    def turn_out(s):
                        rows = P if s < QT_N else 8
                        pe.wait_ge(o_free, it * O_HEAD + s + 2)
                        wait_t(ta(("o", s)))
                        pe.matmul(t_bank[:, 0:rows], o_norm[0:rows, s % 2, :], ident[0:rows, 0:rows], start=True,
                                  stop=True).then_inc(t_full, 1)

                    def values(b):
                        if b == 0:
                            pe.wait_ge(t_free, ta("soft") + 2)
                            pe.wait_ge(o_free, it * O_HEAD + 1)
                        pe.wait_ge(v_in[b % 2], (it * 4 + b // 2 + 1) * 16)
                        for t in range(RUN):
                            ins = pe.matmul(s_bank[0:8, 0:P], spread[:, t, b, :], v_page[:, b % 2, t, :],
                                            start=(b == 0 and t == 0), stop=False)
                        ins.then_inc(v_used, 1)

                    pe.wait_ge(t_free, ta(("v", 1)) + 2)
                    scores(0)
                    for s in range(QT_N):
                        if s + 1 < QT_N:
                            scores(s + 1)
                        if s == VALUES_STEP:
                            pe.wait_ge(soft_sel, it + 1)
                            wait_t(ta("soft"))
                            for j in range(N_PAGES):
                                ins = pe.matmul(t_bank[:, j * 8:j * 8 + 8], soft[:, j * P:(j + 1) * P], sel8,
                                                start=True, stop=True)
                            ins.then_inc(t_full, 1)
                        weigh(s)
                        if s >= 1:
                            turn_out(s - 1)
                        if s >= VALUES_STEP:
                            values(s - VALUES_STEP)
                        if s == SOFTMAX_STEP:
                            u = ug(("soft",))
                            wait_free(u)
                            pe.wait_ge(k_red, (it + 1) * DEC_BATCH + K_CREDIT)
                            for j in range(N_PAGES):
                                pe.transpose(bank[0:16, 3 * u[0] + j // 4, (j % 4) * P:(j % 4 + 1) * P],
                                             s_score[:, :, :, j], ident)
                            pe.matmul(bank[0:16, 3 * u[0] + 2, 0:1], comp8, ones[:, 0:1], start=True, stop=True
                                      ).then_inc(g_full[u[0]], 1)
                    for b in range(QT_N - VALUES_STEP, DEC_BATCH):
                        values(b)
                    pe.matmul(s_bank[0:8, 0:P], diag8, v_dup[:, :], start=False, stop=True).then_inc(o_full, 1)
                    turn_out(QT_N - 1)
                    turn_out(QT_N)
                    pe.wait_ge(t_free, ta(("o", QT_N)) + 2)
                    down_unit(n0 + 5, 2, lambda m: ug(("wh", m)))

                norm_sum(l * 2 + 1, use_layer(l, G0_NORM2), l * T_LAYER + T0_NORM2)
                f0 = l * U_LAYER + U_FFN0

                def state_rows(c):
                    pe.wait_ge(sc_in, (l * FC + c + 1) * 16)
                    wait_t(t_ffn(l, c, 0))
                    pe.matmul(t_bank[:, 0:16], state_in[0:16, :], ident[0:16, 0:16], start=True, stop=True
                              ).then_inc(t_full, 1)

                def new_rows(c):
                    pe.wait_ge(taps0, l * FC + c + 1)
                    wait_t(t_ffn(l, c, 1))
                    pe.transpose(t_bank[0:26, 0:P], ext_tail, ident).then_inc(t_full, 1)

                def down(c, n, slot, first_use):
                    pe.wait_ge(g_lo_done, l * FC + c + 1)
                    down_unit(n, slot, lambda m: use_ffn(l, c, first_use + m))

                state_rows(0)
                up_unit(f0, 0, use_layer(l, G0_A0), norm_index=l * 2 + 1)
                with pe.Fori(0, FC - 1) as i:
                    up_unit(f0 + i * 3 + 1, 1, use_ffn(l, i, 0))
                    new_rows(i)
                    up_unit(f0 + i * 3 + 2, 2, use_ffn(l, i, 1))
                    state_rows(i + 1)
                    down(i, f0 + i * 3 + 3, 0, 2)
                up_unit(f0 + 3 * FC - 2, 1, use_ffn(l, FC - 1, 0))
                new_rows(FC - 1)
                down(FC - 1, f0 + 3 * FC - 1, 2, 1)

            norm_sum(2 * DEPTH, use(G_SETUP // 2 + DEPTH * (G_LAYER // 2), 0), DEPTH * T_LAYER)
            pe.wait_ge(y_done, 2 * DEPTH * KC + KC)
            for t in range(QT_N + 1):
                u = use(G_SETUP // 2 + DEPTH * (G_LAYER // 2), 1 + t)
                wait_free(u)
                rows = P if t < QT_N else 8
                g = bank[:, 3 * u[0]:3 * u[0] + 2, :].rearrange("p a b -> p (a b)")
                for k in range(KC):
                    ins = pe.transpose(g[0:rows, k * P:(k + 1) * P], resid[:, k, t * P:t * P + rows], ident)
                ins.then_inc(g_full[u[0]], 1)

        @block.vector
        def _(dve):
            class Chain:

                def __init__(self, base):
                    self.base, self.n = base, 0

                def __call__(self, ins):
                    self.n += 1
                    ins.then_inc(dve_step, 1)
                    dve.wait_ge(dve_step, self.base + self.n)

            STEP_SETUP, STEP_HEAD, STEP_FFN = 24, 61, 1
            STEP_LAYER = STEP_HEAD * N_HEADS + 1 + STEP_FFN * FC

            for p in range(2):
                dve.memset(small[:, p:p + 1], 0.0).then_inc(g_free[p], 1)
            dve.memset(small[:, 2:3], 0.0).then_inc(t_free, 1)
            dve.memset(small[:, 3:4], 0.0).then_inc(o_free, 1)
            dve.memset(small[:, 4:5], 0.0).then_inc(k_red, K_CREDIT)
            dve.memset(small[:, 5:6], 0.0).then_inc(v_used, V_CREDIT)
            dve.memset(small[:, 6:7], 0.0).then_inc(y_hi_done, 1)
            step = Chain(0)
            dve.wait_ge(table_in, 16)
            step(dve.memset(rs[:, :], 1.0))
            dve.wait_ge(pages_in, 16 * N_PAGES)
            page_f, idx_f = small[:, 8:16], small[:, 16:24]
            step(dve.tensor_copy(page_f, pages[:, :]))
            step(dve.tensor_scalar(idx_f, page_f, float(GROUPS), None, ALU.mult))
            step(dve.tensor_scalar(idx_f, idx_f, c_("group"), None, ALU.add))
            step(dve.tensor_copy(idx_k[:, :], idx_f))
            step(dve.tensor_copy(idx_v[:, :], idx_f))
            step(dve.memset(page_f, float(GROUPS * N_POOL)))
            dve.tensor_copy(idx_inc[:, :], page_f).then_inc(idx_ready, 1)
            dve.wait_ge(lam_in_s, 64)
            for n in range(2):
                step(dve.tensor_tensor(lam_in[:, 2 * n, :], lam_in[:, 2 * n, :], lam_in[:, 2 * n + 1, :], ALU.mult))
            step(dve.tensor_reduce(lam[:, 0:2], lam_in[:, 0, :].rearrange("p (l d) -> p l d", l=DEPTH), AX_X, ALU.add))
            dve.tensor_reduce(lam[:, 2:4], lam_in[:, 2, :].rearrange("p (l d) -> p l d", l=DEPTH), AX_X, ALU.add
                              ).then_inc(lam_sum, 1)
            dve.wait_ge(lam_exp, 1)
            step(dve.tensor_tensor(lam[:, 0:2], lam[:, 4:6], lam[:, 6:8], ALU.subtract))
            step(dve.tensor_tensor(lam[:, 0:2], lam[:, 0:2], c_("lam_init"), ALU.add))
            for l in range(DEPTH):
                step(dve.scalar_tensor_tensor(out=lam[0:16, 8 + l:9 + l], in0=c_("sign", slice(0, 16))[:, 1:2],
                                              scalar=lam[0:16, l:l + 1], in1=c_("sign", slice(0, 16))[:, 0:1],
                                              op0=ALU.mult, op1=ALU.add))
            for t in range(QT_N + 1):
                u = use(0, t)
                full(dve, u)
                rows = P if t < QT_N else 8
                g = bank[:, 3 * u[0]:3 * u[0] + 2, :].rearrange("p a b -> p (a b)").rearrange("p (k r) -> p k r", k=KC)
                dve.tensor_copy(resid[:, :, t * P:t * P + rows], g[:, :, 0:rows]).then_inc(g_free[u[0]], 1)
            u = use(0, QT_N + 1)
            full(dve, u)
            for l in range(DEPTH):
                step(dve.tensor_copy(par[:, l, 0:PAR_W], bank[:, 3 * u[0], l * P:l * P + PAR_W]))
            for l in range(DEPTH):
                a, _ = PAR["norm1_g"]
                step(dve.tensor_scalar(par[:, l, a:a + 2 * KC], par[:, l, a:a + 2 * KC], math.sqrt(D_MODEL), None,
                                       ALU.mult))
                a, _ = PAR["final_g"]
                step(dve.tensor_scalar(par[:, l, a:a + KC], par[:, l, a:a + KC], math.sqrt(D_MODEL), None, ALU.mult))
                a, _ = PAR["subln_g"]
                one = CON["one_minus"][0]
                ins = dve.tensor_scalar(par[:, l, a:a + 1], par[:, l, a:a + 1], con[:, one + l:one + l + 1],
                                        math.sqrt(VDIM), ALU.mult, ALU.mult)
                if l == 0:
                    step(ins)
            ins.then_inc(g_free[u[0]], 1)
            released(dve, u)
            assert step.n <= STEP_SETUP, step.n
            base0 = step.n

            def norm_scale(ni, u, t_use):
                for k in range(1, KC):
                    dve.wait_ge(sq_done, ni * KC + k + 1)
                    if k == 1:
                        dve.scalar_tensor_tensor(out=rot[:, 0:T], in0=rot[:, 0:T], scalar=D_MODEL * EPS / P,
                                                 in1=sq_ring[1], op0=ALU.add, op1=ALU.add).then_inc(acc_done, 1)
                    else:
                        dve.wait_ge(acc_done, ni * (KC - 1) + k - 1)
                        dve.tensor_tensor(rot[:, 0:T], rot[:, 0:T], sq_ring[k % 2], ALU.add).then_inc(acc_done, 1)
                dve.wait_ge(norm_rs, ni + 1)
                dve.tensor_tensor(bq[:, 0:SEQ].rearrange("p (b f) -> p b f", b=QT_N),
                                  ident[:, None, :].broadcast_to([P, QT_N, P]),
                                  rs[:, 0:QT_N].rearrange("p (b a) -> p b a", a=1).broadcast_to([P, QT_N, P]), ALU.mult
                                  ).then_inc(norm_diag, 1)
                dve.tensor_scalar(bq[:, SEQ:T], ident[:, 0:8], rs[:, QT_N:QT_N + 1], None, ALU.mult
                                  ).then_inc(norm_diag, 1)
                full(dve, u)
                dve.tensor_copy(tiles(bq[:, 0:T]), grp3(u[0])).then_inc(g_free[u[0]], 1)
                released(dve, u)

            def norm(ni, u, t_use, gains):
                norm_scale(ni, u, t_use)
                for k in range(KC + 1):
                    if k < KC:
                        if k >= 3:
                            j = k - 3
                            dve.wait_ge((lo_pool, lo_dve)[j % 2], ni * (KC // 2) + j // 2 + 1)
                        dve.scalar_tensor_tensor(out=sq_ring[k % 3], in0=resid[:, k, :], scalar=gains(k),
                                                 in1=bq[:, 0:T], op0=ALU.mult, op1=ALU.mult).then_inc(y_done, 1)
                    j = k - 1
                    if j >= 1 and j % 2 == 1:
                        dve.wait_ge(hi_done, ni * KC + j + 1)
                        dve.tensor_tensor(act_lo[:, j, :], sq_ring[j % 3], act_hi[:, j, :].bitcast(F32), ALU.subtract
                                          ).then_inc(lo_dve, 1)

            def add_rows(uses, ms=range(KC)):
                for m in ms:
                    u = uses(m)
                    full(dve, u)
                    dve.tensor_tensor(tiles(resid[:, m, :]), grp3(u[0]), tiles(resid[:, m, :]), ALU.add
                                      ).then_inc(g_free[u[0]], 1)

            with dve.Fori(0, DEPTH) as l:
                norm(l * 2, use_layer(l, 0), l * T_LAYER, lambda k: p_at("norm1_g", l, k))
                with dve.Fori(0, N_HEADS) as h:
                    it = l * N_HEADS + h
                    ug = lambda name: use_head(l, h, name)
                    ta = lambda name: t_head(l, h, name)
                    step = Chain(l * STEP_LAYER + h * STEP_HEAD + base0)
                    step(dve.tensor_copy(sub_gain, p_at("subln_g", l, 0)))
                    released(dve, ug(("u",)))
                    step(dve.memset(ue[:, 0:POOL_HIST], 0.0))
                    src, dst = ue, pool_a
                    for k in range(4):
                        back, lo = 1 << k, (2 << k) - 1
                        step(dve.scalar_tensor_tensor(out=dst[:, lo:1167], in0=src[:, lo - back:1167 - back],
                                                      scalar=c_at("poolstep", h * 4 + k), in1=src[:, lo:1167],
                                                      op0=ALU.mult, op1=ALU.add))
                        src, dst = dst, (pool_b if k % 2 == 0 else pool_a)
                    step(dve.scalar_tensor_tensor(out=pool_dd[:, 0:SEQ], in0=pool_b[:, 15:15 + SEQ],
                                                  scalar=c_at("poolinv", h), in1=ue[:, 15:15 + SEQ],
                                                  op0=ALU.mult, op1=ALU.subtract))
                    step(dve.tensor_tensor(pool_dd[:, 0:16], pool_b[:, 15:31], c_at("poolhead", h * 16, 16), ALU.mult))
                    step(dve.tensor_tensor(pool_dd[:, 0:16], pool_dd[:, 0:16], ue[:, 15:31], ALU.subtract))
                    dve.scalar_tensor_tensor(out=pool_dd[:, SEQ:T], in0=pool_b[:, 1039 + 15:1167:16],
                                             scalar=c_at("poolinv", h), in1=ue[:, 1039 + 15:1167:16],
                                             op0=ALU.mult, op1=ALU.subtract).then_inc(pool_d, 1)

                    def rope(n, name, dst):
                        released(dve, ug(name))
                        for a in range(4):
                            to = 32 * (a ^ 1)
                            dve.tensor_copy(rot[to:to + 32, 0:T], dst[32 * a:32 * a + 32, :]).then_inc(dve_step, 1)
                        step.n += 4
                        dve.wait_ge(dve_step, step.base + step.n)
                        dve.tensor_tensor(dst[:, :], dst[:, :], c_("cos"), ALU.mult).then_inc(dve_step, 1)
                        dve.tensor_tensor(rot[:, 0:T], rot[:, 0:T], c_("sin"), ALU.mult).then_inc(dve_step, 1)
                        step.n += 2
                        dve.wait_ge(dve_step, step.base + step.n)
                        dve.tensor_tensor(dst[:, :], dst[:, :], rot[:, 0:T], ALU.add).then_inc(roped, 1)
                        dve.wait_ge(roped, it * 2 + n + 1)

                    rope(0, ("q",), qT)
                    dve.tensor_tensor(bq[:, 0:1024].rearrange("p (b f) -> p b f", b=8),
                                      ident[:, None, :].broadcast_to([P, 8, P]),
                                      qT[:, SEQ:T].rearrange("p (b a) -> p b a", a=1).broadcast_to([P, 8, P]), ALU.mult
                                      ).then_inc(diag_done, 1)
                    rope(1, ("k",), kT)
                    step(dve.tensor_tensor(qk8, qT[:, SEQ:T], kT[:, SEQ:T], ALU.mult))
                    step(dve.tensor_tensor(comp8, qk8[:, None, :].broadcast_to([P, 2, 8]),
                                           c_("compsel").rearrange("p (c a) -> p c a", a=1).broadcast_to([P, 2, 8]),
                                           ALU.mult))

                    def k_sum(b):
                        dve.wait_ge(k_mul, it * DEC_BATCH + b + 1)
                        src = k_page[:, b % 2, :, :].rearrange("p j (c d) -> p j c d", c=2)
                        dve.tensor_reduce(s_score[:, :, b, :].rearrange("p c j -> p j c"), src, AX_X, ALU.add
                                          ).then_inc(k_red, 1)

                    for b in range(4):
                        k_sum(b)
                    u = ug(("y",))
                    dve.wait_ge(y_hi_done, it + 2)
                    dve.scalar_tensor_tensor(out=tiles(mix_lo[:, :]), in0=grp3(u[0]), scalar=p_at("pool_scale", l, h),
                                             in1=tiles(mix_hi[:, :].bitcast(F32)), op0=ALU.mult, op1=ALU.subtract
                                             ).then_inc(g_free[u[0]], 1)
                    for b in range(4, DEC_BATCH):
                        add_rows(lambda m: ug(("wg", m)), range(2 * b - 8, 2 * b - 6))
                        k_sum(b)

                    def maxima(s):
                        width = (ORDER[s] + 1) * P
                        for c in range(2):
                            u = ug(("s", s, c))
                            full(dve, u)
                            src = bank[:, 3 * u[0]:3 * u[0] + 2, :].rearrange("p a b -> p (a b)")[:, 0:width]
                            step(dve.tensor_reduce(stat[:, s % 2, c:c + 1], src, AX_X, ALU.max))
                            dve.tensor_scalar(stat[:, s % 2, 2 + c:3 + c], stat[:, s % 2, c:c + 1],
                                              -(HEAD_DIM ** -0.5), None, ALU.mult).then_inc(att_bias, 1)

                    def combine(s):
                        width = (ORDER[s] + 1) * P
                        released(dve, ug(("s", s, 0)))
                        released(dve, ug(("s", s, 1)))
                        sums = stat[:, s % 2, 4:6]
                        step(dve.reciprocal(sums, sums))
                        pr = probs[s % 2]
                        step(dve.tensor_scalar(pr[:, 1, 0:width], pr[:, 1, 0:width], stat[:, s % 2, 5:6],
                                               lam[:, bass.ds(l, 1)], ALU.mult, ALU.mult))
                        dve.scalar_tensor_tensor(out=pr[:, 0, 0:width], in0=pr[:, 0, 0:width],
                                                 scalar=stat[:, s % 2, 4:5], in1=pr[:, 1, 0:width], op0=ALU.mult,
                                                 op1=ALU.subtract).then_inc(att_a, 1)

                    def normalise(s):
                        rows = P if s < QT_N else 8
                        dve.wait_ge(att_rms, it * O_HEAD + s + 1)
                        ss = stat[0:rows, s % 2, 6:7]
                        src = o_bank if s < QT_N else s_bank
                        dve.tensor_scalar(o_norm[0:rows, s % 2, :], src[0:rows, 0:P], ss, None, ALU.mult
                                          ).then_inc(o_free, 1)

                    def mix(s):
                        at, n = (ORDER[s] * P, P) if s < QT_N else (SEQ, 8)
                        dve.wait_ge(mix_hi_done, it * O_HEAD + s + 1)
                        dve.scalar_tensor_tensor(out=mix_lo[:, at:at + n], in0=t_bank[:, 0:n],
                                                 scalar=sub_gain, in1=mix_hi[:, at:at + n].bitcast(F32),
                                                 op0=ALU.mult, op1=ALU.subtract).then_inc(t_free, 1)

                    maxima(0)
                    for s in range(QT_N):
                        if s >= 2:
                            mix(s - 2)
                        if s >= 1:
                            normalise(s - 1)
                        if s == VALUES_STEP:
                            dve.wait_ge(t_full, ta("soft") + 1)
                            w = t_bank[:, 0:64].rearrange("p (j b a) -> p j b a", j=8, a=1).broadcast_to([P, 8, 8, 8])
                            d = c_("delta").rearrange("p (o b a) -> p o b a", o=1, b=8).broadcast_to([P, 8, 8, 8])
                            dve.tensor_tensor(spread[:, :, :, :], w, d, ALU.mult).then_inc(t_free, 1)
                        combine(s)
                        if s + 1 < QT_N:
                            maxima(s + 1)
                        if s == SOFTMAX_STEP:
                            u = ug(("soft",))
                            full(dve, u)
                            src = bank[0:16, 3 * u[0]:3 * u[0] + 2, :].rearrange("p a b -> p (a b)")
                            step(dve.tensor_reduce(soft_m, src, AX_X, ALU.max))
                            step(dve.tensor_tensor(soft_m, bank[0:16, 3 * u[0] + 2, 0:1], soft_m, ALU.max))
                            dve.tensor_scalar(soft_nb, soft_m, -(HEAD_DIM ** -0.5), None, ALU.mult
                                              ).then_inc(soft_bias, 1)
                            released(dve, u)
                            own = soft[:, PAST_LEN:PAST_LEN + 1]
                            step(dve.tensor_tensor(soft_l, soft_l, own, ALU.add))
                            step(dve.reciprocal(soft_l, soft_l))
                            step(dve.tensor_tensor(soft_cf, soft_l, lam[0:16, bass.ds(l + 8, 1)], ALU.mult))
                            step(dve.tensor_scalar(sel8, c_("rowsel", slice(0, 16)), soft_cf, None, ALU.mult))
                            dve.tensor_scalar(diag8, sel8, own, None, ALU.mult).then_inc(soft_sel, 1)
                    mix(QT_N - 2)
                    normalise(QT_N - 1)
                    mix(QT_N - 1)
                    normalise(QT_N)
                    mix(QT_N)
                    add_rows(lambda m: ug(("wh", m)))
                    assert step.n == STEP_HEAD, step.n

                norm(l * 2 + 1, use_layer(l, G0_NORM2), l * T_LAYER + T0_NORM2,
                     lambda k: p_at("norm2_g", l, k))
                fstep = l * STEP_LAYER + (N_HEADS * STEP_HEAD + 1 + base0)

                def taps(c):
                    dve.wait_ge(taps0, l * FC + c + 1)
                    dve.scalar_tensor_tensor(out=conv_c[:, :], in0=ext[:, 1:1049], scalar=p_at("conv_w", l, c + FC),
                                             in1=conv_c[:, :], op0=ALU.mult, op1=ALU.add).then_inc(dve_step, 1)
                    dve.wait_ge(dve_step, fstep + c + 1)
                    dve.scalar_tensor_tensor(out=conv_c[:, :], in0=ext[:, 0:1048], scalar=p_at("conv_w", l, c),
                                             in1=conv_c[:, :], op0=ALU.mult, op1=ALU.add).then_inc(conv_done, 1)

                def gate_b(c, u):
                    full(dve, u)
                    dve.wait_ge(silu_done, l * FC + c + 1)
                    dve.tensor_tensor(tiles(gate[:, :]), grp3(u[0]), tiles(gate[:, :]), ALU.mult
                                      ).then_inc(g_free[u[0]], 1)
                    dve.wait_ge(g_hi_done, l * FC + c + 1)
                    dve.tensor_tensor(mix_lo[:, :], gate[:, :], mix_hi[:, :].bitcast(F32), ALU.subtract
                                      ).then_inc(g_lo_done, 1)

                dve.wait_ge(taps0, l * FC + 1)
                dve.memset(ext[:, 0:2], 0.0).then_inc(dve_step, 1)
                dve.wait_ge(dve_step, fstep)
                taps(0)
                with dve.Fori(0, FC - 1) as i:
                    gate_b(i, use_ffn(l, i, 0))
                    add_rows(lambda m: use_ffn(l, i, 2 + m))
                    taps(i + 1)
                gate_b(FC - 1, use_ffn(l, FC - 1, 0))
                add_rows(lambda m: use_ffn(l, FC - 1, 1 + m))

            half = G_SETUP // 2 + DEPTH * (G_LAYER // 2)
            ni = 2 * DEPTH
            norm_scale(ni, use(half, 0), DEPTH * T_LAYER)
            for k in range(KC):
                dve.scalar_tensor_tensor(out=resid[:, k, :], in0=resid[:, k, :], scalar=p_at("final_g", 0, k),
                                         in1=bq[:, 0:T], op0=ALU.mult, op1=ALU.mult).then_inc(y_done, 1)
            dve.wait_ge(y_done, ni * KC + KC)
            for t in range(0, QT_N + 1, 2):
                u = use(half, 1 + t)
                full(dve, u)
                rows = P if t < QT_N else 8
                src = bank[0:rows, 3 * u[0]:3 * u[0] + 2, :].rearrange("p a b -> p (a b)")
                dve.tensor_copy(act_y(t)[0:rows, :], src).then_inc(g_free[u[0]], 1)


_INS = ["x_prompt", "x_sample", "cache_k", "cache_v", "state_pool", "state_conv", "page_table", "norm1_g", "w_in",
        "pool_w", "pool_scale", "lam_q1", "lam_k1", "lam_q2", "lam_k2", "subln_g", "w_out", "norm2_g", "w_up",
        "conv_w", "conv_b", "w_down", "final_g"]
_OUTS = [(1, SEQ, D_MODEL), (DEC_BATCH, 1, D_MODEL), (DEPTH, 1, SEQ // PAGE_SIZE, PAGE_SIZE, N_HEADS, VDIM),
         (DEPTH, 1, SEQ // PAGE_SIZE, PAGE_SIZE, N_HEADS, VDIM), (DEPTH, 1, POOL_HIST, POOL_W), (DEPTH, 1, 2, D_FF),
         (DEPTH, DEC_BATCH, 1, N_HEADS, VDIM), (DEPTH, DEC_BATCH, 1, N_HEADS, VDIM),
         (DEPTH, DEC_BATCH, POOL_HIST, POOL_W), (DEPTH, DEC_BATCH, 2, D_FF)]


def layouts(inputs):
    arrays = {f"in_{name}": np.asarray(inputs[name]) for name in _INS}
    for name in ("in_cache_k", "in_cache_v"):
        arrays[name] = arrays[name].transpose(0, 3, 1, 2, 4).reshape(-1, RUN * VDIM)
    for name in ("in_w_in", "in_w_up"):
        w = arrays[name].reshape(DEPTH, KC, P, -1, P)
        arrays[name] = w.transpose(0, 3, 2, 1, 4).reshape(DEPTH, -1, P, KC * P)
    arrays["in_page_table"] = arrays["in_page_table"].transpose(1, 0)
    arrays = {name: np.ascontiguousarray(a) for name, a in arrays.items()}
    arrays["in_table"] = constants()
    return arrays


def kernel(**inputs):
    import concourse.bacc as bacc
    from concourse.bass_utils import run_bass_kernel_spmd

    nc = bacc.Bacc("TRN2", target_bir_lowering=False, num_devices=1)
    arrays = layouts(inputs)
    args = [nc.dram_tensor(name, a.shape, mybir.dt.from_np(a.dtype), kind="ExternalInput").ap()
            for name, a in arrays.items()]
    args += [nc.dram_tensor(f"out_{i}", shape, F32, kind="ExternalOutput").ap() for i, shape in enumerate(_OUTS)]
    hybrid_decoder_kernel(nc, *args)
    r = run_bass_kernel_spmd(nc, [arrays], core_ids=[0])
    return tuple(r.results[0][f"out_{i}"] for i in range(len(_OUTS)))
```

```python
import math
from contextlib import ExitStack

import numpy as np

import concourse.bass as bass
from concourse import mybir

F32 = mybir.dt.float32
F32R = mybir.dt.float32r
I32 = mybir.dt.int32
BF16 = mybir.dt.bfloat16
ALU = mybir.AluOpType
ACT = mybir.ActivationFunctionType
AX_X = mybir.AxisListType.X

P = 128
D_MODEL, SEQ, DEPTH, DEC_BATCH = 1024, 1024, 2, 8
PAST_LEN, PAGE_SIZE = 1024, 128
N_PAGES = PAST_LEN // PAGE_SIZE
RUN = 8
GROUPS = PAGE_SIZE // RUN
assert GROUPS * N_PAGES == P and RUN == N_PAGES
POOL_W, POOL_WINDOWS, POOL_HIST = 512, (2, 4, 8, 16), 15
N_HEADS, HEAD_DIM = 4, 64
VDIM = 2 * HEAD_DIM
D_FF = 2816
EPS = 1e-6
ROPE_THETA = 10000.0
NEG = -2.0 ** 100

T = SEQ + DEC_BATCH
NT = 3
TW = T // NT
KC = D_MODEL // P
FC = D_FF // P
QT_N = SEQ // P
CONV_TAPS = 3

SLOTS = 3
U_HEAD = 6
U_FFN0 = U_HEAD * N_HEADS
U_LAYER = U_FFN0 + 3 * FC

ORDER = [7, 0, 6, 1, 5, 2, 4, 3]
SOFTMAX_STEP = 1
WEIGHTS_STEP = 3
VALUES_AT = {4: (0, 1), 5: (2, 3), 6: (4, 5), 7: (6, 7)}


def rounds(i):
    return [list(range(a, min(a + 4, i + 1))) for a in range(0, i + 1, 4)]


def head_uses():
    g, t = [("u",), ("q",), ("k",), ("qb", 0), ("qb", 1), ("y",), ("v",)], ["state", "uout"]
    t += [("k", 0), ("k", 1), "small"]
    g += [("wg", m) for m in range(KC)]
    t += [("v", 0), ("v", 1)]
    g += [("s", 0, 0), ("s", 0, 1)]
    for s in range(QT_N):
        if s + 1 < QT_N:
            g += [("s", s + 1, 0), ("s", s + 1, 1)]
        t += [("p", s)] * (len(rounds(ORDER[s])) - 1)
        if s >= 1:
            t.append(("o", s - 1))
        if s == SOFTMAX_STEP:
            g.append(("soft",))
    t += [("o", QT_N - 1), ("o", QT_N)]
    g += [("wh", m) for m in range(KC)]
    return {k: n for n, k in enumerate(g)}, {k: n for n, k in enumerate(t)}


HG, HT = head_uses()
G_HEAD, T_HEAD, O_HEAD = len(HG), len(HT), QT_N + 1
assert G_HEAD % 2 == 0
G_SETUP = 10
G_FFN = 2 + KC
G0_HEADS = 1
G0_NORM2 = G0_HEADS + G_HEAD * N_HEADS
G0_A0 = G0_NORM2 + 1
G0_FFN = G0_A0 + 1
G_LAYER = G0_FFN + G_FFN * (FC - 1) + G_FFN - 1
assert G_LAYER % 2 == 0
T0_HEADS = 1
T0_NORM2 = T0_HEADS + T_HEAD * N_HEADS
T0_FFN = T0_NORM2 + 1
T_LAYER = T0_FFN + 2 * FC
W_CREDIT, V_CREDIT = SLOTS, DEC_BATCH
SAMPLES = QT_N - 1


def out_rows(n):
    return (SEQ, DEC_BATCH) if n == SAMPLES else (ORDER[min(n, QT_N - 1)] * P, P)


CON = {}
for _name, _width in (("ident", P), ("ones", P), ("causal", P), ("delta", 64), ("rowsel", 8), ("sign", 2),
                      ("compsel", 2), ("group", 1), ("neghalf", 1), ("eps", 1), ("poolstep", 16), ("poolinv", 4), ("poolhead", 64), ("lam_init", DEPTH),
                      ("one_minus", DEPTH), ("cos", T), ("sin", T)):
    _at = sum(w for _, w in CON.values())
    CON[_name] = (_at, _width)
CON_W = sum(w for _, w in CON.values())
CON_SMALL = CON["cos"][0]

PAR = {}
for _name, _n in (("conv_w", CONV_TAPS * FC), ("conv_b", FC), ("norm1_g", KC), ("norm2_g", KC), ("pool_scale", 4),
                  ("subln_g", 1), ("final_g", KC)):
    PAR[_name] = (sum(n for _, n in PAR.values()), _n)
PAR_W = sum(n for _, n in PAR.values())


def constants():
    c = np.zeros((P, CON_W), np.float32)

    def put(name, value, rows=slice(None)):
        a, w = CON[name]
        c[rows, a:a + w] = np.asarray(value, np.float32).reshape(-1, w) if np.ndim(value) else value

    put("ident", np.eye(P))
    put("ones", 1.0)
    put("causal", np.where(np.arange(P)[None, :] > np.arange(P)[:, None], NEG, 0.0))
    put("delta", np.broadcast_to(np.eye(8).reshape(1, 64), (P, 64)))
    put("rowsel", np.tile(np.eye(8), (2, 1)), slice(0, 16))
    put("sign", np.repeat([[1.0, 0.0], [0.0, -1.0]], 8, axis=0), slice(0, 16))
    put("compsel", np.repeat(np.eye(2), 64, axis=0))
    put("group", (np.arange(P) % GROUPS).reshape(P, 1))
    put("neghalf", -0.5)
    put("eps", VDIM * EPS)
    put("poolstep", np.broadcast_to([[1.0 if k <= g else 0.0 for g in range(4) for k in range(4)]], (P, 16)))
    put("poolinv", np.broadcast_to([[1.0 / w for w in POOL_WINDOWS]], (P, 4)))
    put("poolhead", np.broadcast_to([[1.0 / min(t + 1, w) for w in POOL_WINDOWS for t in range(16)]], (P, 64)))
    li = [0.8 - 0.6 * math.exp(-0.3 * n) for n in range(DEPTH)]
    put("lam_init", np.broadcast_to([li], (P, DEPTH)))
    put("one_minus", np.broadcast_to([[1.0 - x for x in li]], (P, DEPTH)))
    half = HEAD_DIM // 2
    inv = (1.0 / (np.float32(ROPE_THETA) ** (np.arange(half, dtype=np.float32) * np.float32(2.0 / HEAD_DIM)))
           ).astype(np.float32)
    pos = np.concatenate([np.arange(SEQ), np.full(DEC_BATCH, PAST_LEN)]).astype(np.float32)
    ang = (pos[None, :] * inv[:, None]).astype(np.float32).astype(np.float64)
    cos, sin = np.cos(ang), np.sin(ang)
    put("cos", np.tile(cos, (4, 1)))
    put("sin", np.concatenate([-sin, sin, -sin, sin]))
    return c


def hybrid_decoder_kernel(nc, x_prompt, x_sample, cache_k, cache_v, state_pool, state_conv, page_table, norm1_g, w_in,
                          pool_w, pool_scale, lam_q1, lam_k1, lam_q2, lam_k2, subln_g, w_out, norm2_g, w_up, conv_w,
                          conv_b, w_down, final_g, table, y_prompt, y_sample, k_new_prompt, v_new_prompt,
                          pool_new_prompt, conv_new_prompt, k_new_sample, v_new_sample, pool_new_sample,
                          conv_new_sample):
    with ExitStack() as ctx:
        def sb(name, shape, dt=F32):
            return ctx.enter_context(nc.sbuf_tensor(name, shape, dt))

        def sem(name):
            return ctx.enter_context(nc.semaphore(name))

        resid = sb("resid", [P, KC, T])
        act_hi = sb("act_hi", [P, KC, T], F32R)
        act_lo = sb("act_lo", [P, KC, T], F32R)
        w_raw = sb("w_raw", [P, SLOTS, 1024])
        w_hi = sb("w_hi", [P, SLOTS, 1024], F32R)
        w_lo = sb("w_lo", [P, SLOTS, 1024], F32R)
        con = sb("con", [P, CON_W])
        par = sb("par", [P, DEPTH, P])
        mask = sb("mask", [P, 2, P], BF16)
        scratch = sb("scratch", [P, 3104])
        rot = sb("rot", [P, 1168])
        bq = sb("bq", [P, T])
        qT = sb("qT", [P, T])
        kT = sb("kT", [P, T])
        v_tok = sb("v_tok", [P, QT_N, P])
        k_tok = v_tok
        mix_hi = sb("mix_hi", [P, T], F32R)
        mix_lo = sb("mix_lo", [P, T], F32R)
        a_T = sb("a_T", [P, 2, 512])
        page = sb("page", [P, 4, RUN, P])
        stat = sb("stat", [P, 2, 8])
        small = sb("small", [P, 48])
        rs = sb("rs", [P, QT_N + 1])
        pw = sb("pw", [P, P])
        state_in = sb("state_in", [120, P])
        rows_out = sb("rows_out", [P, P])
        v_dup = sb("v_dup", [16, P])
        lam = sb("lam", [P, 16])
        pages = sb("pages", [P, DEC_BATCH], I32)
        idx_k = sb("idx_k", [P, DEC_BATCH], I32)
        idx_v = sb("idx_v", [P, DEC_BATCH], I32)
        idx_now = sb("idx_now", [P, 1], I32)
        idx_inc = sb("idx_inc", [P, DEC_BATCH], I32)

        bank = ctx.enter_context(nc.psum_tensor("bank", [P, 8, 512], F32))
        t_bank = bank[:, 6, :]
        o_bank = bank[:, 7, :]
        p_bank = bank[:, 2, :]
        s_bank = bank[:, 5, :]

        table_in, rope_in, params_in, lam_in_s, pages_in = sem("table_in"), sem("rope_in"), sem("params_in"), sem("lam_landed"), sem("pages_in")
        x_in = [sem(f"x_in{i}") for i in range(QT_N + 1)]
        w_in_s = [sem(f"w_landed{i}") for i in range(SLOTS)]
        page_in = [sem(f"page_landed{i}") for i in range(4)]
        pw_in, sp_in, sc_in = sem("pool_w_landed"), sem("state_pool_landed"), sem("state_conv_landed")
        k_out_s, v_out_s, small_out, u_out_s = sem("k_stored"), sem("v_stored"), sem("small_stored"), sem("u_stored")
        conv_out_s, pool_copy, y_out = sem("conv_stored"), sem("pool_copied"), sem("y_stored")
        g_full, g_free = [sem("group0_full"), sem("group1_full")], [sem("group0_free"), sem("group1_free")]
        t_full, t_free = sem("tbank_full"), sem("tbank_free")
        p_full, p_free = sem("pbank_full"), sem("pbank_free")
        o_full, o_free = sem("obank_full"), sem("obank_free")
        w_hi_done, w_lo_done = sem("w_hi_done"), sem("w_lo_done")
        sq_done, acc_done, y_done, hi_done = sem("sq_done"), sem("acc_done"), sem("y_done"), sem("act_hi_done")
        lo_pool, lo_dve = sem("act_lo_pool"), sem("act_lo_dve")
        pool_d, roped, diag_done = sem("pool_d_done"), sem("roped"), sem("diag_done")
        y_hi_done, k_mul, k_red = sem("pool_y_hi_done"), sem("k_multiplied"), sem("k_reduced")
        att_bias, att_a, att_sq, mix_hi_done = sem("att_bias"), sem("att_weights"), sem("att_squares"), sem("mix_hi_done")
        inv_done = sem("inv_sum_done")
        idx_ready, idx_step = sem("idx_ready"), sem("idx_step")
        att_rms, pool_step, norm_diag, norm_rs = sem("att_rms"), sem("pool_step"), sem("norm_diag"), sem("norm_rs")
        weights_full, spread_done = sem("sample_weights_full"), sem("sample_weights_spread")
        soft_exp = sem("soft_exp_done")
        soft_bias, soft_sel, v_used = sem("soft_bias"), sem("soft_sel"), sem("v_used")
        taps0, conv_done, silu_done, g_hi_done, g_lo_done = (sem("tap2_done"), sem("conv_done"), sem("silu_done"),
                                                             sem("gate_hi_done"), sem("gate_lo_done"))
        dve_step, act_step, lam_sum, lam_exp = sem("dve_step"), sem("act_step"), sem("lam_sum"), sem("lam_exp")

        def c_(name, rows=slice(None)):
            a, w = CON[name]
            return con[rows, a:a + w]

        def sl(n, width):
            return slice(n, n + width) if isinstance(n, int) else bass.ds(n, width)

        def c_at(name, n, width=1, rows=slice(None)):
            a, _ = CON[name]
            return con[rows, sl(n + a, width)]

        def p_at(name, layer, n, width=1):
            a, _ = PAR[name]
            return par[:, layer, sl(n + a, width)]

        ident, ones = c_("ident"), c_("ones")

        def x_buf(t):
            if t < 3:
                return scratch[:, 1024 * t:1024 * t + 1024]
            if t < 7:
                return page[:, t - 3, :, :].rearrange("p t d -> p (t d)")
            return (qT, kT)[t - 7][:, 0:1024]

        def page_landed(eng, it, n):
            eng.wait_ge(page_in[n % 4], (it * (2 * DEC_BATCH // 4) + n // 4 + 1) * 16)

        def grp(p):
            return bank[:, 3 * p:3 * p + 3, :]

        def grp3(p):
            return bank[:, 3 * p:3 * p + 3, 0:TW]

        def tiles(ap):
            return ap.rearrange("p (a b) -> p a b", a=NT)

        sq_ring = [scratch[:, i * T:(i + 1) * T] for i in range(3)]
        ue, pool_a, pool_b = scratch[:, 0:1167], scratch[:, 1167:2334], rot[:, 0:1167]
        pool_dd = scratch[:, 1167:1167 + T]
        v_T = rot[:, 0:T]
        ext, conv_c = scratch[:, 0:1050], scratch[:, 1050:2098]
        ext_tail = ext[:, 1024:1050]
        gate = rot[:, 0:T]
        spread = rot[:, 0:512].rearrange("p (j b a) -> p j b a", j=N_PAGES, b=8)
        o_norm = rot[:, 512:768].rearrange("p (s d) -> p s d", s=2)
        junk = rot[:, 768:1024].rearrange("p (s d) -> p s d", s=2)
        s_score = rot[:, T + 8:T + 136].rearrange("p (c b j) -> p c b j", c=2, b=8)
        u_out, us_out, ks_out, conv_out = (rows_out[0:POOL_HIST, :], rows_out[32:40, :], rows_out[64:72, :],
                                           rows_out[96:122, :])
        lam_in = a_T[:, 0, :].rearrange("p (n d) -> p n d", n=4)
        soft = bq[0:16, 0:1025]
        probs = [scratch[:, 0:2048].rearrange("p (c k) -> p c k", c=2),
                 scratch[:, 2048:3072].rearrange("p (c k) -> p c k", c=2)]
        u_hist = ue[:, 1039:1167].rearrange("p (b j) -> p b j", b=8)
        qk8, comp8 = small[:, 0:8], small[:, 8:24].rearrange("p (c b) -> p c b", c=2)
        sel8, diag8 = small[0:16, 24:32], small[0:16, 32:40]
        soft_m, soft_nb, soft_l, soft_cf = (small[0:16, 40:41], small[0:16, 41:42], small[0:16, 42:43],
                                            small[0:16, 43:44])
        sub_gain, neg_lam = small[:, 44:45], small[:, 45:46]

        def inv_sum(n):
            if n == SAMPLES:
                return c_("ones", slice(0, DEC_BATCH))[:, 0:1]
            return stat[:, min(n, QT_N - 1) % 2, 7:8]

        soft_sign = lam[0:16, 8:10]

        def use(half, j):
            return j % 2, half + j // 2

        def use_head(l, h, name):
            return use(G_SETUP // 2 + l * (G_LAYER // 2) + h * (G_HEAD // 2), G0_HEADS + HG[name])

        def use_ffn(l, i, j):
            return use(G_SETUP // 2 + l * (G_LAYER // 2) + i * (G_FFN // 2), G0_FFN + j)

        def use_layer(l, j):
            return use(G_SETUP // 2 + l * (G_LAYER // 2), j)

        def full(eng, u):
            eng.wait_ge(g_full[u[0]], u[1] + 1)

        def released(eng, u):
            eng.wait_ge(g_free[u[0]], u[1] + 2)

        def t_head(l, h, name):
            return l * T_LAYER + h * T_HEAD + (T0_HEADS + HT[name])

        def t_ffn(l, i, j):
            return l * T_LAYER + i * 2 + (T0_FFN + j)

        def w_landed(eng, l, h_or_i, off, per):
            eng.wait_ge(w_in_s[off % SLOTS], (l * (U_LAYER // SLOTS) + h_or_i * per + off // SLOTS) * 16 + 16)

        N_POOL = cache_k.shape[0] // (DEPTH * N_HEADS * GROUPS)

        block = ctx.enter_context(nc.Block())

        @block.sync
        def _(sp):
            sp.dma_start(con[:, 0:CON_SMALL], table[:, 0:CON_SMALL]).then_inc(table_in, 16)
            for t in range(QT_N + 1):
                if t < QT_N:
                    sp.dma_start(x_buf(t), x_prompt[0, t * P:(t + 1) * P, :]).then_inc(x_in[t], 16)
                else:
                    sp.dma_start(x_buf(t)[0:8], x_sample.rearrange("b a d -> (b a) d")).then_inc(x_in[t], 16)
            for j in range(N_PAGES):
                sp.dma_start(pages[j * GROUPS:(j + 1) * GROUPS, :],
                             page_table[j:j + 1, :].broadcast_to([GROUPS, DEC_BATCH])).then_inc(pages_in, 16)
            for l in range(DEPTH):
                rows = [("conv_w", conv_w[l].rearrange("j (c p) -> (j c) p", p=P)),
                        ("conv_b", conv_b[l].rearrange("(c p) -> c p", p=P)),
                        ("norm1_g", norm1_g[l].rearrange("(c p) -> c p", p=P)),
                        ("norm2_g", norm2_g[l].rearrange("(c p) -> c p", p=P)),
                        ("pool_scale", pool_scale[l].rearrange("(c p) -> c p", p=P)),
                        ("subln_g", subln_g[l].rearrange("(c p) -> c p", p=P)),
                        ("final_g", final_g.rearrange("(c p) -> c p", p=P))]
                for name, src in rows:
                    a, n = PAR[name]
                    sp.dma_start(k_tok[a:a + n, l, :], src).then_inc(params_in, 16)
            for n, v in enumerate((lam_q1, lam_k1, lam_q2, lam_k2)):
                src = v.rearrange("l d -> (l d)").rearrange("(a n) -> a n", a=1).broadcast_to([P, DEPTH * HEAD_DIM])
                sp.dma_start(lam_in[:, n, :], src).then_inc(lam_in_s, 16)
            sp.dma_start(con[:, CON_SMALL:CON_W], table[:, CON_SMALL:CON_W]).then_inc(rope_in, 16)

            def load_unit(n, slot, src):
                sp.wait_ge(w_lo_done, n + 1)
                sp.dma_start(w_raw[:, slot, :], src).then_inc(w_in_s[slot], 16)

            def head_loads(l, h, next_units):
                it = l * N_HEADS + h
                sp.wait_ge(y_hi_done, it + 1)
                sp.dma_start(pw[:, :], pool_w[l, h]).then_inc(pw_in, 16)
                sp.wait_ge(t_full, l * T_LAYER)
                sp.dma_start(state_in[:, :], state_pool[l].rearrange("b j c -> (b j) c")[:, sl(h * P, P)]
                             ).then_inc(sp_in, 16)
                n0 = l * U_LAYER + h * U_HEAD
                load_unit(n0 + 2, 2, w_in[l, h + 8])
                load_unit(n0 + 3, 0, w_in[l, h + 12])
                load_unit(n0 + 4, 1, w_out[l, sl(h * P, P), :])
                load_unit(n0 + 5, 2, w_out[l, sl(h * P + POOL_W, P), :])

                next_units(n0 + U_HEAD)

            with sp.Fori(0, DEPTH) as l:
                def load_u_q(h, n0):
                    load_unit(n0, 0, w_in[l, h])
                    load_unit(n0 + 1, 1, w_in[l, h + 4])

                def load_a_b(n0):
                    load_unit(n0, 0, w_up[l, 0])
                    load_unit(n0 + 1, 1, w_up[l, FC])

                load_u_q(0, l * U_LAYER)
                with sp.Fori(0, N_HEADS - 1) as h:
                    head_loads(l, h, lambda n0: load_u_q(h + 1, n0))
                head_loads(l, N_HEADS - 1, load_a_b)

                def load_state(c):
                    sp.wait_ge(t_full, l * T_LAYER + c * 2 + (T0_FFN - 1))
                    sp.dma_start(state_in[0:16, :],
                                 state_conv[l].rearrange("b j c -> (b j) c")[:, sl(c * P, P)]
                                 ).then_inc(sc_in, 16)

                def load_a(i, n, slot):
                    load_unit(n, slot, w_up[l, i])

                def load_b(i, n, slot):
                    load_unit(n, slot, w_up[l, i + FC])

                def load_d(i, n, slot):
                    load_unit(n, slot, w_down[l, sl(i * P, P), :])

                f0 = l * U_LAYER + U_FFN0
                load_state(0)
                with sp.Fori(0, FC - 1) as i:
                    load_a(i + 1, f0 + i * 3 + 2, 2)
                    load_state(i + 1)
                    load_d(i, f0 + i * 3 + 3, 0)
                    load_b(i + 1, f0 + i * 3 + 4, 1)
                load_d(FC - 1, f0 + 3 * FC - 1, 2)

            for t in range(QT_N + 1):
                released(sp, use(G_SETUP // 2 + DEPTH * (G_LAYER // 2), t))
                rows = P if t < QT_N else 8
                dst = y_prompt[0, t * P:(t + 1) * P, :] if t < QT_N else y_sample.rearrange("b a d -> (b a) d")
                sp.dma_start(dst, x_buf(t)[0:rows]).then_inc(y_out, 16)
            sp.wait_ge(y_out, 16 * (QT_N + 1))

        @block.gpsimd
        def _(pool):
            for l in range(DEPTH):
                pool.dma_start(pool_new_sample[l, :, 0:POOL_HIST - 1, :], state_pool[l, :, 1:POOL_HIST, :]
                               ).then_inc(pool_copy, 16)

            def split_lo(n, slot):
                pool.wait_ge(w_hi_done, n + 1)
                pool.tensor_tensor(w_lo[:, slot, :], w_raw[:, slot, :], w_hi[:, slot, :].bitcast(F32), ALU.subtract
                                   ).then_inc(w_lo_done, 1)

            pool.memset(junk[:, 0, :], 0.0).then_inc(w_lo_done, W_CREDIT)
            pool.wait_ge(w_lo_done, W_CREDIT)

            neghalf = c_("neghalf")
            IDX_STEPS = 2 * DEC_BATCH + 2
            pool.wait_ge(idx_ready, 1)

            def norm_lo(ni, t_use):
                norm_rms(ni, t_use)
                for k in range(0, KC, 2):
                    pool.wait_ge(hi_done, ni * KC + k + 1)
                    pool.tensor_tensor(act_lo[:, k, :], sq_ring[k % 3], act_hi[:, k, :].bitcast(F32), ALU.subtract
                                       ).then_inc(lo_pool, 1)

            def norm_rms(ni, t_use):
                pool.wait_ge(t_free, t_use + 2)
                pool.tensor_tensor(rs[:, :], rs[:, :], neghalf.broadcast_to([P, QT_N + 1]), ALU.pow
                                   ).then_inc(norm_rs, 1)

            def head_rms(l, it, s):
                rows = out_rows(s)[1]
                ss = stat[0:rows, s % 2, 6:7]
                pool.wait_ge(att_sq, it * O_HEAD + s + 1)
                pool.tensor_tensor(ss, ss, c_("eps")[0:rows], ALU.add).then_inc(pool_step, 1)
                pool.wait_ge(pool_step, it * O_HEAD + s + 1)
                pool.tensor_tensor(ss, ss, neghalf[0:rows], ALU.pow).then_inc(att_rms, 1)

            with pool.Fori(0, DEPTH) as l:
                n0 = l * U_LAYER
                split_lo(n0, 0)
                split_lo(n0 + 1, 1)
                norm_lo(l * 2, l * T_LAYER)
                with pool.Fori(0, N_HEADS) as h:
                    it = l * N_HEADS + h
                    n = l * U_LAYER + h * U_HEAD

                    def k_product(b):
                        page_landed(pool, it, b)
                        kp = page[:, b % 4, :, :]
                        q_row = bq[:, None, b * P:(b + 1) * P].broadcast_to([P, N_PAGES, P])
                        pool.tensor_tensor(kp, kp, q_row, ALU.mult).then_inc(k_mul, 1)

                    steps = 0

                    def index_step(out, in0, in1):
                        nonlocal steps
                        pool.wait_ge(idx_step, it * IDX_STEPS + steps)
                        pool.tensor_tensor(out, in0, in1, ALU.add).then_inc(idx_step, 1)
                        steps += 1

                    def load(n):
                        if n < 4:
                            pool.wait_ge(v_used, it * DEC_BATCH + n + 5)
                        elif n < DEC_BATCH + 4:
                            pool.wait_ge(k_red, it * DEC_BATCH + n - 3)
                        else:
                            pool.wait_ge(v_used, it * DEC_BATCH + V_CREDIT + n - 11)
                        cache, rows = ((cache_k, idx_k), (cache_v, idx_v))[n // DEC_BATCH]
                        rows = rows[:, n % DEC_BATCH:n % DEC_BATCH + 1]
                        index_step(idx_now[:, :], rows, idx_inc[:, 0:1])
                        pool.indirect_dma_start(page[:, n % 4, :, :].rearrange("p t d -> p (t d)"), None, cache,
                                                bass.IndirectOffsetOnAxis(rows, 0)).then_inc(page_in[n % 4], 16)

                    for n_ in range(4):
                        load(n_)
                    split_lo(n + 2, 2)
                    split_lo(n + 3, 0)
                    split_lo(n + 4, 1)
                    released(pool, use_head(l, h, ("qb", 1)))
                    k_product(0)
                    for b in range(1, DEC_BATCH):
                        k_product(b)
                        if b < 5:
                            load(b + 3)
                        if b == 2:
                            split_lo(n + 5, 2)
                    index_step(idx_k[:, :], idx_k[:, :], idx_inc[:, :])
                    split_lo(n + 6, 0)
                    split_lo(n + 7, 1)
                    for s in range(QT_N + 1):
                        for b in {0: (0, 1), 1: (2, 3), 4: (4, 5), 5: (6, 7)}.get(s, ()):
                            load(DEC_BATCH + b)
                        head_rms(l, it, s)
                    for n_ in range(2 * DEC_BATCH - 4, 2 * DEC_BATCH):
                        page_landed(pool, it, n_)
                    index_step(idx_v[:, :], idx_v[:, :], idx_inc[:, :])
                    assert steps == IDX_STEPS
                norm_lo(l * 2 + 1, l * T_LAYER + T0_NORM2)
                f0 = l * U_LAYER + U_FFN0
                split_lo(f0 + 2, 2)
                with pool.Fori(0, FC - 1) as i:
                    split_lo(f0 + i * 3 + 3, 0)
                    split_lo(f0 + i * 3 + 4, 1)
                    split_lo(f0 + i * 3 + 5, 2)
            norm_rms(2 * DEPTH, DEPTH * T_LAYER)
            pool.wait_ge(pool_copy, 16 * DEPTH)

        @block.scalar
        def _(act):
            def split_hi(l, idx, off, per, last_use):
                w_landed(act, l, idx, off, per)
                full(act, last_use)
                act.activation(w_hi[:, off % SLOTS, :], w_raw[:, off % SLOTS, :], ACT.Copy).then_inc(w_hi_done, 1)

            def norm_sums(ni, t_use):
                act.wait_ge(t_full, t_use + 1)
                act.wait_ge(norm_diag, ni * 2)
                act.activation(rs[:, 0:QT_N], t_bank[:, 0:QT_N], ACT.Copy).then_inc(act_step, 1)
                act.activation(rs[0:8, QT_N:QT_N + 1], t_bank[0:8, QT_N:QT_N + 1], ACT.Copy).then_inc(t_free, 1)

            def norm(ni, last_add, t_use):
                released(act, last_add)
                act.activation(rot[:, 0:T], resid[:, 0, :], ACT.Square).then_inc(sq_done, 1)
                for k in range(1, KC):
                    if k >= 3:
                        act.wait_ge(acc_done, ni * (KC - 1) + k - 2)
                    act.activation(sq_ring[k % 2], resid[:, k, :], ACT.Square).then_inc(sq_done, 1)
                norm_sums(ni, t_use)
                for k in range(KC):
                    act.wait_ge(y_done, ni * KC + k + 1)
                    act.activation(act_hi[:, k, :], sq_ring[k % 3], ACT.Copy).then_inc(hi_done, 1)

            act.wait_ge(lam_sum, 1)
            act.activation(lam[:, 4:8], lam[:, 0:4], ACT.Exp).then_inc(lam_exp, 1)

            with act.Fori(0, DEPTH) as l:
                split_hi(l, 0, 0, 0, (0, l * (G_LAYER // 2)))
                split_hi(l, 0, 1, 0, (1, l * (G_LAYER // 2)))
                norm(l * 2, (1, G_SETUP // 2 - 1 + l * (G_LAYER // 2)), l * T_LAYER)

                with act.Fori(0, N_HEADS) as h:
                    it = l * N_HEADS + h
                    ug = lambda name: use_head(l, h, name)
                    ta = lambda name: t_head(l, h, name)

                    def hi(off, last_use):
                        split_hi(l, h, off, 2, last_use)

                    hi(2, use(G_SETUP // 2 + l * (G_LAYER // 2) + h * (G_HEAD // 2), 0))
                    full(act, ug(("u",)))
                    act.wait_ge(t_full, ta("state") + 1)
                    act.activation(u_hist[:, :, 0:POOL_HIST],
                                   t_bank[:, 0:120].rearrange("p (b j) -> p b j", b=8), ACT.Copy).then_inc(t_free, 1)
                    g = grp(ug(("u",))[0])
                    act.activation(ue[:, 15:15 + 2 * TW].rearrange("p (a b) -> p a b", a=2), g[:, 0:2, 0:TW], ACT.Copy
                                   ).then_inc(act_step, 1)
                    act.activation(ue[:, 15 + 2 * TW:15 + SEQ], g[:, 2, 0:TW - 8], ACT.Copy).then_inc(act_step, 1)
                    act.activation(u_hist[:, :, POOL_HIST], g[:, 2, TW - 8:TW], ACT.Copy
                                   ).then_inc(g_free[ug(("u",))[0]], 1)
                    hi(3, ug(("u",)))

                    def raw(name, dst):
                        u = ug(name)
                        full(act, u)
                        act.activation(tiles(dst[:, :]), grp3(u[0]), ACT.Copy).then_inc(g_free[u[0]], 1)

                    raw(("q",), qT)
                    act.wait_ge(t_full, ta("uout") + 1)
                    act.wait_ge(u_out_s, it * 32)
                    act.activation(u_out[:, :], t_bank[0:POOL_HIST, 0:P], ACT.Copy).then_inc(act_step, 1)
                    act.activation(us_out[:, :], t_bank[0:8, P:2 * P], ACT.Copy).then_inc(t_free, 1)
                    act.wait_ge(t_free, ta("uout") + 2)
                    act.dma_start(pool_new_prompt[l, 0, :, bass.ds(h * P, P)], u_out[:, :]).then_inc(u_out_s, 16)
                    act.dma_start(pool_new_sample[l, :, POOL_HIST - 1, bass.ds(h * P, P)], us_out[:, :]
                                  ).then_inc(u_out_s, 16)
                    hi(4, ug(("q",)))
                    raw(("k",), kT)
                    for n in range(2):
                        full(act, ug(("qb", n)))
                        act.activation(bq[:, n * 512:(n + 1) * 512], grp(ug(("qb", n))[0])[:, 0, :], ACT.Copy
                                       ).then_inc(g_free[ug(("qb", n))[0]], 1)
                    hi(5, ug(("k",)))
                    full(act, ug(("y",)))
                    act.activation(tiles(mix_hi[:, :]), grp3(ug(("y",))[0]), ACT.Copy,
                                   scale=p_at("pool_scale", l, h)).then_inc(y_hi_done, 1)
                    full(act, ug(("v",)))
                    act.wait_ge(roped, it * 2 + 2)
                    act.activation(rot[:, T:T + 8], grp(ug(("v",))[0])[:, NT - 1, TW - 8:TW], ACT.Copy
                                   ).then_inc(act_step, 1)
                    act.activation(tiles(v_T), grp3(ug(("v",))[0]), ACT.Copy).then_inc(g_free[ug(("v",))[0]], 1)
                    act.wait_ge(v_out_s, it * 16)
                    for r in range(2):
                        act.wait_ge(t_full, ta(("k", r)) + 1)
                        act.activation(k_tok[:, 4 * r:4 * r + 4, :], t_bank.rearrange("p (a b) -> p a b", a=4), ACT.Copy
                                       ).then_inc(t_free, 1)
                    act.wait_ge(t_free, ta(("k", 1)) + 2)
                    act.dma_start(k_new_prompt[l, 0, :, :, h, :].rearrange("t p d -> p t d"), k_tok[:, :, :]
                                  ).then_inc(k_out_s, 16)
                    act.wait_ge(t_full, ta("small") + 1)
                    act.wait_ge(small_out, it * 32)
                    act.activation(ks_out[:, :], t_bank[0:8, 0:P], ACT.Copy).then_inc(act_step, 1)
                    act.activation(v_dup[:, :], t_bank[0:16, P:2 * P], ACT.Copy).then_inc(t_free, 1)
                    act.wait_ge(t_free, ta("small") + 2)
                    act.dma_start(k_new_sample[l, :, 0, h, :], ks_out[:, :]).then_inc(small_out, 16)
                    act.dma_start(v_new_sample[l, :, 0, h, :], v_dup[0:8, :]).then_inc(small_out, 16)
                    hi(6, ug(("v",)))
                    act.wait_ge(k_out_s, it * 16 + 16)
                    for r in range(2):
                        act.wait_ge(t_full, ta(("v", r)) + 1)
                        act.activation(v_tok[:, 4 * r:4 * r + 4, :], t_bank.rearrange("p (a b) -> p a b", a=4), ACT.Copy
                                       ).then_inc(t_free, 1)
                    act.wait_ge(t_free, ta(("v", 1)) + 2)
                    act.dma_start(v_new_prompt[l, 0, :, :, h, :].rearrange("t p d -> p t d"), v_tok[:, :, :]
                                  ).then_inc(v_out_s, 16)
                    hi(7, ug(("wg", KC - 1)))

                    def exps(s):
                        width = (ORDER[s] + 1) * P
                        for c in range(2):
                            act.wait_ge(att_bias, it * 2 * QT_N + 2 * s + c + 1)
                            p = ug(("s", s, c))[0]
                            src = bank[:, 3 * p:3 * p + 2, :].rearrange("p a b -> p (a b)")[:, 0:width]
                            act.activation(probs[s % 2][:, c, 0:width], src, ACT.Exp,
                                           bias=stat[:, s % 2, 2 + c:3 + c], scale=HEAD_DIM ** -0.5,
                                           accum_out=stat[:, s % 2, 4 + c:5 + c]).then_inc(g_free[p], 1)

                    def squares(s):
                        rows = out_rows(s)[1]
                        act.wait_ge(o_full, it * O_HEAD + s + 1)
                        src = s_bank if s == SAMPLES else o_bank
                        if s != SAMPLES:
                            act.wait_ge(inv_done, it * QT_N + min(s, QT_N - 1) + 1)
                        act.activation(junk[0:rows, s % 2, :], src[0:rows, 0:P], ACT.Square, scale=inv_sum(s),
                                       accum_out=stat[0:rows, s % 2, 6:7]).then_inc(att_sq, 1)

                    def mix(s):
                        at, n = out_rows(s)
                        act.wait_ge(t_full, ta(("o", s)) + 1)
                        act.activation(mix_hi[:, at:at + n], t_bank[:, 0:n], ACT.Copy, scale=sub_gain
                                       ).then_inc(mix_hi_done, 1)

                    exps(0)
                    for s in range(QT_N):
                        if s >= 2:
                            mix(s - 2)
                        if s >= 1:
                            squares(s - 1)
                        for r, blocks in enumerate(rounds(ORDER[s])):
                            if r == 0:
                                act.wait_ge(p_full, it * QT_N + s + 1)
                                act.activation(a_T[:, 0, 0:P * len(blocks)], p_bank[:, 0:P * len(blocks)], ACT.Copy
                                               ).then_inc(p_free, 1)
                            else:
                                act.wait_ge(t_full, ta(("p", s)) + 1)
                                act.activation(a_T[:, 1, 0:P * len(blocks)], t_bank[:, 0:P * len(blocks)], ACT.Copy
                                               ).then_inc(t_free, 1)
                        if s + 1 < QT_N:
                            exps(s + 1)
                        if s == SOFTMAX_STEP:
                            u = ug(("soft",))
                            full(act, u)
                            p = u[0]
                            act.activation(soft[:, 0:PAST_LEN],
                                           bank[0:16, 3 * p:3 * p + 2, :].rearrange("p a b -> p (a b)"), ACT.Copy
                                           ).then_inc(act_step, 1)
                            act.activation(soft[:, PAST_LEN:PAST_LEN + 1], bank[0:16, 3 * p + 2, 0:1], ACT.Copy
                                           ).then_inc(g_free[p], 1)
                        if s == SOFTMAX_STEP + 1:
                            act.wait_ge(soft_bias, it + 1)
                            act.activation(soft[:, 0:PAST_LEN + 1], soft[:, 0:PAST_LEN + 1], ACT.Exp, bias=soft_nb,
                                           scale=HEAD_DIM ** -0.5, accum_out=soft_l).then_inc(soft_exp, 1)
                    squares(QT_N - 1)
                    mix(QT_N - 2)
                    squares(QT_N)
                    mix(QT_N - 1)
                    mix(QT_N)

                norm(l * 2 + 1, use_layer(l, G0_NORM2 - 1), l * T_LAYER + T0_NORM2)

                def evacuate_a(c, u):
                    full(act, u)
                    act.wait_ge(t_full, t_ffn(l, c, 0) + 1)
                    act.wait_ge(conv_done, l * FC + c)
                    rows = ext[:, 1026:1050].rearrange("p (b j) -> p b j", b=8)
                    act.activation(rows[:, :, 0:2], t_bank[:, 0:16].rearrange("p (b j) -> p b j", b=8), ACT.Copy
                                   ).then_inc(t_free, 1)
                    g = grp(u[0])
                    act.activation(ext[:, 2:2 + 2 * TW].rearrange("p (a b) -> p a b", a=2), g[:, 0:2, 0:TW], ACT.Copy
                                   ).then_inc(act_step, 1)
                    act.activation(ext[:, 2 + 2 * TW:2 + SEQ], g[:, 2, 0:TW - 8], ACT.Copy).then_inc(act_step, 1)
                    act.activation(rows[:, :, 2], g[:, 2, TW - 8:TW], ACT.Copy).then_inc(g_free[u[0]], 1)
                    released(act, u)
                    act.activation(conv_c[:, :], ext[:, 2:1050], ACT.Identity, bias=p_at("conv_b", l, c),
                                   scale=p_at("conv_w", l, c + 2 * FC)).then_inc(taps0, 1)

                def silu(c):
                    act.wait_ge(conv_done, l * FC + c + 1)
                    act.wait_ge(g_lo_done, l * FC + c)
                    act.activation(gate[:, 0:SEQ], conv_c[:, 0:SEQ], ACT.Silu).then_inc(act_step, 1)
                    act.activation(gate[:, SEQ:T], conv_c[:, 1026:1048:3], ACT.Silu).then_inc(silu_done, 1)

                def store_conv(c):
                    act.wait_ge(t_full, t_ffn(l, c, 1) + 1)
                    act.wait_ge(conv_out_s, (l * FC + c) * 48)
                    act.activation(conv_out[:, :], t_bank[0:26, 0:P], ACT.Copy).then_inc(t_free, 1)
                    act.wait_ge(t_free, t_ffn(l, c, 1) + 2)
                    act.dma_start(conv_new_prompt[l, 0, :, sl(c * P, P)], conv_out[0:2, :]
                                  ).then_inc(conv_out_s, 16)
                    for j in range(2):
                        act.dma_start(conv_new_sample[l, :, j, sl(c * P, P)], rows_out[99 + j:122:3, :]
                                      ).then_inc(conv_out_s, 16)

                def gate_hi(c, u):
                    released(act, u)
                    act.activation(mix_hi[:, :], gate[:, :], ACT.Copy).then_inc(g_hi_done, 1)

                split_hi(l, 0, U_FFN0 + 2, 0, use_layer(l, G0_NORM2 - 1))
                evacuate_a(0, use_layer(l, G0_A0))
                silu(0)
                with act.Fori(0, FC - 1) as i:
                    split_hi(l, i, U_FFN0 + 3, 1, use_ffn(l, i, -1))
                    store_conv(i)
                    gate_hi(i, use_ffn(l, i, 0))
                    split_hi(l, i, U_FFN0 + 4, 1, use_ffn(l, i, 0))
                    evacuate_a(i + 1, use_ffn(l, i, 1))
                    split_hi(l, i, U_FFN0 + 5, 1, use_ffn(l, i, 1))
                    silu(i + 1)
                store_conv(FC - 1)
                gate_hi(FC - 1, use_ffn(l, FC - 1, 0))

            last = DEPTH * (G_LAYER // 2)
            released(act, (1, G_SETUP // 2 - 1 + last))
            act.activation(rot[:, 0:T], resid[:, 0, :], ACT.Square).then_inc(sq_done, 1)
            for k in range(1, KC):
                if k >= 3:
                    act.wait_ge(acc_done, 2 * DEPTH * (KC - 1) + k - 2)
                act.activation(sq_ring[k % 2], resid[:, k, :], ACT.Square).then_inc(sq_done, 1)
            norm_sums(2 * DEPTH, DEPTH * T_LAYER)
            act.wait_ge(norm_rs, 2 * DEPTH + 1)
            for t in range(1, QT_N + 1, 2):
                u = use(G_SETUP // 2 + last, t)
                full(act, u)
                src = bank[:, 3 * u[0]:3 * u[0] + 2, :].rearrange("p a b -> p (a b)")
                act.activation(x_buf(t), src, ACT.Copy, scale=rs[:, t:t + 1]).then_inc(g_free[u[0]], 1)
            act.wait_ge(k_out_s, 16 * DEPTH * N_HEADS)
            act.wait_ge(v_out_s, 16 * DEPTH * N_HEADS)
            act.wait_ge(small_out, 32 * DEPTH * N_HEADS)
            act.wait_ge(u_out_s, 32 * DEPTH * N_HEADS)
            act.wait_ge(conv_out_s, 48 * DEPTH * FC)

        @block.tensor
        def _(pe):
            def wait_free(u):
                pe.wait_ge(g_free[u[0]], u[1] + 1)

            def wait_t(seq):
                pe.wait_ge(t_free, seq + 1)

            def unit_ready(n):
                pe.wait_ge(w_lo_done, n + (1 + W_CREDIT))

            def up_unit(n, slot, u, norm_index=None):
                unit_ready(n)
                wait_free(u)
                g = grp(u[0])
                for k in range(KC):
                    for n_, (w, x) in enumerate(((w_hi, act_hi), (w_lo, act_hi), (w_hi, act_lo))):
                        if norm_index is not None and n_ == 0:
                            pe.wait_ge(hi_done, norm_index * KC + k + 1)
                        if norm_index is not None and n_ == 2:
                            pe.wait_ge((lo_pool, lo_dve)[k % 2], norm_index * (KC // 2) + k // 2 + 1)
                        for t in range(NT):
                            ins = pe.matmul(g[:, t, 0:TW], w[:, slot, k * P:(k + 1) * P],
                                            x[:, k, t * TW:(t + 1) * TW], start=(k == 0 and n_ == 0),
                                            stop=(k == KC - 1 and n_ == 2))
                ins.then_inc(g_full[u[0]], 1)

            def down_part(slot, m, u, tiles_=range(NT), first=True, last=True):
                if first:
                    wait_free(u)
                g = grp(u[0])
                for n_, (w, x) in enumerate(((w_hi, mix_hi), (w_hi, mix_lo), (w_lo, mix_hi))):
                    for t in tiles_:
                        ins = pe.matmul(g[:, t, 0:TW], w[:, slot, m * P:(m + 1) * P], x[:, t * TW:(t + 1) * TW],
                                        start=(n_ == 0), stop=(n_ == 2))
                if last:
                    ins.then_inc(g_full[u[0]], 1)

            def down_unit(n, slot, uses):
                unit_ready(n)
                for m in range(KC):
                    down_part(slot, m, uses(m))

            pe.wait_ge(table_in, 16)
            for t in range(QT_N + 1):
                u = use(0, t)
                wait_free(u)
                pe.wait_ge(x_in[t], 16)
                rows = P if t < QT_N else 8
                g = bank[:, 3 * u[0]:3 * u[0] + 2, :].rearrange("p a b -> p (a b)")
                for k in range(KC):
                    ins = pe.transpose(g[:, k * P:k * P + rows], x_buf(t)[0:rows, k * P:(k + 1) * P],
                                       ident[0:rows, 0:rows])
                ins.then_inc(g_full[u[0]], 1)
            u = use(0, QT_N + 1)
            wait_free(u)
            pe.wait_ge(params_in, 16 * len(PAR) * DEPTH)
            for l in range(DEPTH):
                ins = pe.transpose(bank[:, 3 * u[0], l * P:l * P + PAR_W], k_tok[0:PAR_W, l, :],
                                   ident[0:PAR_W, 0:PAR_W])
            ins.then_inc(g_full[u[0]], 1)

            def token_sums(ni, t_use):
                wait_t(t_use)
                pe.wait_ge(acc_done, (ni + 1) * (KC - 1))
                for t in range(QT_N + 1):
                    rows = P if t < QT_N else 8
                    ins = pe.matmul(t_bank[0:rows, t:t + 1], rot[:, t * P:t * P + rows], ones[:, 0:1], start=True,
                                    stop=True)
                ins.then_inc(t_full, 1)

            def norm_sum(ni, u, t_use):
                token_sums(ni, t_use)
                wait_free(u)
                pe.wait_ge(norm_diag, (ni + 1) * 2)
                g = grp(u[0])
                for t in range(NT):
                    ins = pe.matmul(g[:, t, 0:TW], ones, bq[:, t * TW:(t + 1) * TW], start=True, stop=True)
                ins.then_inc(g_full[u[0]], 1)

            with pe.Fori(0, DEPTH) as l:
                norm_sum(l * 2, use_layer(l, 0), l * T_LAYER)
                with pe.Fori(0, N_HEADS) as h:
                    it = l * N_HEADS + h
                    n0 = l * U_LAYER + h * U_HEAD
                    ug = lambda name: use_head(l, h, name)
                    ta = lambda name: t_head(l, h, name)
                    pe.wait_ge(sp_in, (it + 1) * 16)
                    wait_t(ta("state"))
                    pe.transpose(t_bank[:, 0:120], state_in[:, :], ident[0:120, 0:120]).then_inc(t_full, 1)
                    up_unit(n0, 0, ug(("u",)), norm_index=l * 2)
                    up_unit(n0 + 1, 1, ug(("q",)))
                    released(pe, ug(("u",)))
                    wait_t(ta("uout"))
                    pe.transpose(t_bank[0:POOL_HIST, 0:P], ue[:, SEQ:SEQ + POOL_HIST], ident)
                    pe.transpose(t_bank[0:8, P:2 * P], u_hist[:, :, POOL_HIST], ident).then_inc(t_full, 1)
                    up_unit(n0 + 2, 2, ug(("k",)))
                    pe.wait_ge(diag_done, it + 1)
                    for n in range(2):
                        u = ug(("qb", n))
                        wait_free(u)
                        pe.matmul(grp(u[0])[:, 0, :], ones, bq[:, n * 512:(n + 1) * 512], start=True, stop=True
                                  ).then_inc(g_full[u[0]], 1)
                    u = ug(("y",))
                    wait_free(u)
                    pe.wait_ge(pool_d, it + 1)
                    pe.wait_ge(pw_in, (it + 1) * 16)
                    for t in range(NT):
                        ins = pe.matmul(grp(u[0])[:, t, 0:TW], pw[:, :], pool_dd[:, t * TW:(t + 1) * TW],
                                        start=True, stop=True)
                    ins.then_inc(g_full[u[0]], 1)
                    up_unit(n0 + 3, 0, ug(("v",)))

                    def turn(name, r, src):
                        wait_t(ta((name, r)))
                        for a in range(4):
                            i = 4 * r + a
                            ins = pe.transpose(t_bank[:, a * P:(a + 1) * P], src[:, i * P:(i + 1) * P], ident)
                        ins.then_inc(t_full, 1)

                    pe.wait_ge(roped, it * 2 + 2)
                    turn("k", 0, kT)
                    released(pe, ug(("y",)))
                    unit_ready(n0 + 4)
                    for m in range(KC):
                        down_part(1, m, ug(("wg", m)))
                        if m == 0:
                            turn("k", 1, kT)
                        if m == 1:
                            wait_t(ta("small"))
                            released(pe, ug(("v",)))
                            pe.transpose(t_bank[0:8, 0:P], kT[:, SEQ:T], ident)
                            pe.transpose(t_bank[0:16, P:2 * P], rot[:, SEQ:T + 8], ident).then_inc(t_full, 1)

                    def scores(s):
                        i = ORDER[s]
                        width = (i + 1) * P
                        for c in range(2):
                            u = ug(("s", s, c))
                            wait_free(u)
                            rows = slice(c * HEAD_DIM, (c + 1) * HEAD_DIM)
                            for n, at in enumerate(range(0, i * P, 512)):
                                w = min(512, i * P - at)
                                pe.matmul(bank[:, 3 * u[0] + n, 0:w], qT[rows, i * P:(i + 1) * P],
                                          kT[rows, at:at + w], start=True, stop=True)
                            last = bank[:, 3 * u[0] + i // 4, (i % 4) * P:(i % 4 + 1) * P]
                            pe.matmul(last, qT[rows, i * P:(i + 1) * P], kT[rows, i * P:(i + 1) * P],
                                      start=True, stop=False)
                            ins = pe.matmul(last, mask[:, 0, :], mask[:, 1, :], start=False, stop=True)
                            ins.then_inc(g_full[u[0]], 1)

                    def values(b):
                        page_landed(pe, it, DEC_BATCH + b)
                        for t in range(RUN):
                            ins = pe.matmul(s_bank[0:8, 0:P], spread[:, t, b, :], page[:, b % 4, t, :],
                                            start=(b == 0 and t == 0), stop=False)
                        ins.then_inc(v_used, 1)

                    def weigh(s):
                        i = ORDER[s]
                        rr = rounds(i)
                        pe.wait_ge(att_a, it * QT_N + s + 1)
                        for r, blocks in enumerate(rr):
                            to = (p_bank, t_bank)[r]
                            if r == 0:
                                pe.wait_ge(p_free, it * QT_N + s)
                            else:
                                wait_t(ta(("p", s)))
                            for n, b in enumerate(blocks):
                                ins = pe.transpose(to[:, n * P:(n + 1) * P], probs[s % 2][:, 0, b * P:(b + 1) * P],
                                                   ident)
                            ins.then_inc((p_full, t_full)[r], 1)
                        if s == min(VALUES_AT):
                            pe.wait_ge(spread_done, it + 1)
                        for b in VALUES_AT.get(s, ()):
                            values(b)
                        if s == max(VALUES_AT):
                            pe.matmul(s_bank[0:8, 0:P], diag8, v_dup[:, :], start=False, stop=True
                                      ).then_inc(o_full, 1)
                        pe.wait_ge(o_free, it * O_HEAD + s + 1)
                        if s == 0:
                            pe.wait_ge(t_free, ta(("v", 1)) + 2)
                        for r, blocks in enumerate(rr):
                            if r == 0:
                                pe.wait_ge(p_free, it * QT_N + s + 1)
                            else:
                                pe.wait_ge(t_free, ta(("p", s)) + 2)
                            for n, b in enumerate(blocks):
                                ins = pe.matmul(o_bank[:, 0:P], a_T[:, r, n * P:(n + 1) * P],
                                                v_tok[:, b, :], start=(b == 0), stop=(b == i))
                        ins.then_inc(o_full, 1)

                    def turn_out(s):
                        rows = out_rows(s)[1]
                        pe.wait_ge(o_free, it * O_HEAD + s + 2)
                        wait_t(ta(("o", s)))
                        pe.matmul(t_bank[:, 0:rows], o_norm[0:rows, s % 2, :], ident[0:rows, 0:rows], start=True,
                                  stop=True).then_inc(t_full, 1)

                    scores(0)
                    turn("v", 0, v_T)
                    turn("v", 1, v_T)
                    for s in range(QT_N):
                        if s + 1 < QT_N:
                            scores(s + 1)
                        weigh(s)
                        if s >= 1:
                            turn_out(s - 1)
                        if s == WEIGHTS_STEP:
                            pe.wait_ge(soft_sel, it + 1)
                            for j in range(N_PAGES):
                                ins = pe.matmul(s_bank[:, j * 8:j * 8 + 8], soft[:, j * P:(j + 1) * P], sel8,
                                                start=True, stop=True)
                            ins.then_inc(weights_full, 1)
                        if s == SOFTMAX_STEP:
                            u = ug(("soft",))
                            wait_free(u)
                            pe.wait_ge(k_red, (it + 1) * DEC_BATCH)
                            for j in range(N_PAGES):
                                pe.transpose(bank[0:16, 3 * u[0] + j // 4, (j % 4) * P:(j % 4 + 1) * P],
                                             s_score[:, :, :, j], ident)
                            pe.matmul(bank[0:16, 3 * u[0] + 2, 0:1], comp8, ones[:, 0:1], start=True, stop=True
                                      ).then_inc(g_full[u[0]], 1)
                    turn_out(QT_N - 1)
                    turn_out(QT_N)
                    unit_ready(n0 + 5)
                    pe.wait_ge(t_free, ta(("o", QT_N - 1)) + 2)
                    late = ORDER[-1] * P // TW
                    assert late == ((ORDER[-1] + 1) * P - 1) // TW
                    early = [t for t in range(NT) if t != late]
                    for m in range(2):
                        down_part(2, m, ug(("wh", m)), early, last=False)
                    pe.wait_ge(t_free, ta(("o", QT_N)) + 2)
                    for m in range(2):
                        down_part(2, m, ug(("wh", m)), (late,), first=False)
                    for m in range(2, KC):
                        down_part(2, m, ug(("wh", m)))

                norm_sum(l * 2 + 1, use_layer(l, G0_NORM2), l * T_LAYER + T0_NORM2)
                f0 = l * U_LAYER + U_FFN0

                def state_rows(c):
                    pe.wait_ge(sc_in, (l * FC + c + 1) * 16)
                    wait_t(t_ffn(l, c, 0))
                    pe.matmul(t_bank[:, 0:16], state_in[0:16, :], ident[0:16, 0:16], start=True, stop=True
                              ).then_inc(t_full, 1)

                def new_rows(c):
                    pe.wait_ge(taps0, l * FC + c + 1)
                    wait_t(t_ffn(l, c, 1))
                    pe.transpose(t_bank[0:26, 0:P], ext_tail, ident).then_inc(t_full, 1)

                def down(c, n, slot, first_use):
                    pe.wait_ge(g_lo_done, l * FC + c + 1)
                    down_unit(n, slot, lambda m: use_ffn(l, c, first_use + m))

                state_rows(0)
                up_unit(f0, 0, use_layer(l, G0_A0), norm_index=l * 2 + 1)
                with pe.Fori(0, FC - 1) as i:
                    up_unit(f0 + i * 3 + 1, 1, use_ffn(l, i, 0))
                    new_rows(i)
                    up_unit(f0 + i * 3 + 2, 2, use_ffn(l, i, 1))
                    state_rows(i + 1)
                    down(i, f0 + i * 3 + 3, 0, 2)
                up_unit(f0 + 3 * FC - 2, 1, use_ffn(l, FC - 1, 0))
                new_rows(FC - 1)
                down(FC - 1, f0 + 3 * FC - 1, 2, 1)

            token_sums(2 * DEPTH, DEPTH * T_LAYER)
            pe.wait_ge(y_done, 2 * DEPTH * KC + KC)
            for t in range(QT_N + 1):
                u = use(G_SETUP // 2 + DEPTH * (G_LAYER // 2), t)
                wait_free(u)
                rows = P if t < QT_N else 8
                g = bank[:, 3 * u[0]:3 * u[0] + 2, :].rearrange("p a b -> p (a b)")
                for k in range(KC):
                    ins = pe.transpose(g[0:rows, k * P:(k + 1) * P], resid[:, k, t * P:t * P + rows], ident)
                ins.then_inc(g_full[u[0]], 1)

        @block.vector
        def _(dve):
            class Chain:

                def __init__(self, base):
                    self.base, self.n = base, 0

                def __call__(self, ins):
                    self.n += 1
                    ins.then_inc(dve_step, 1)
                    dve.wait_ge(dve_step, self.base + self.n)

            STEP_SETUP, STEP_HEAD, STEP_FFN = 26, 60, 1
            STEP_LAYER = STEP_HEAD * N_HEADS + 1 + STEP_FFN * FC

            for p in range(2):
                dve.memset(small[:, p:p + 1], 0.0).then_inc(g_free[p], 1)
            dve.memset(small[:, 2:3], 0.0).then_inc(t_free, 1)
            dve.memset(small[:, 3:4], 0.0).then_inc(o_free, 1)
            dve.memset(small[:, 5:6], 0.0).then_inc(v_used, V_CREDIT)
            dve.memset(small[:, 6:7], 0.0).then_inc(y_hi_done, 1)
            for t in range(QT_N + 1):
                u = use(0, t)
                full(dve, u)
                rows = P if t < QT_N else 8
                g = bank[:, 3 * u[0]:3 * u[0] + 2, :].rearrange("p a b -> p (a b)").rearrange("p (k r) -> p k r", k=KC)
                dve.tensor_copy(resid[:, :, t * P:t * P + rows], g[:, :, 0:rows]).then_inc(g_free[u[0]], 1)
            step = Chain(0)
            dve.wait_ge(table_in, 16)
            step(dve.memset(rs[:, :], 1.0))
            step(dve.tensor_copy(mask[:, 0, :], ident))
            step(dve.tensor_copy(mask[:, 1, :], c_("causal")))
            dve.wait_ge(pages_in, 16 * N_PAGES)
            page_f, idx_f = small[:, 8:16], small[:, 16:24]
            step(dve.tensor_copy(page_f, pages[:, :]))
            step(dve.tensor_scalar(idx_f, page_f, float(GROUPS), None, ALU.mult))
            step(dve.tensor_scalar(idx_f, idx_f, c_("group"), None, ALU.add))
            step(dve.tensor_copy(idx_k[:, :], idx_f))
            step(dve.tensor_copy(idx_v[:, :], idx_f))
            step(dve.memset(page_f, float(GROUPS * N_POOL)))
            dve.tensor_copy(idx_inc[:, :], page_f).then_inc(idx_ready, 1)
            dve.wait_ge(lam_in_s, 64)
            for n in range(2):
                step(dve.tensor_tensor(lam_in[:, 2 * n, :], lam_in[:, 2 * n, :], lam_in[:, 2 * n + 1, :], ALU.mult))
            step(dve.tensor_reduce(lam[:, 0:2], lam_in[:, 0, :].rearrange("p (l d) -> p l d", l=DEPTH), AX_X, ALU.add))
            dve.tensor_reduce(lam[:, 2:4], lam_in[:, 2, :].rearrange("p (l d) -> p l d", l=DEPTH), AX_X, ALU.add
                              ).then_inc(lam_sum, 1)
            dve.wait_ge(lam_exp, 1)
            step(dve.tensor_tensor(lam[:, 0:2], lam[:, 4:6], lam[:, 6:8], ALU.subtract))
            step(dve.tensor_tensor(lam[:, 0:2], lam[:, 0:2], c_("lam_init"), ALU.add))
            for l in range(DEPTH):
                step(dve.scalar_tensor_tensor(out=lam[0:16, 8 + l:9 + l], in0=c_("sign", slice(0, 16))[:, 1:2],
                                              scalar=lam[0:16, l:l + 1], in1=c_("sign", slice(0, 16))[:, 0:1],
                                              op0=ALU.mult, op1=ALU.add))
            u = use(0, QT_N + 1)
            full(dve, u)
            for l in range(DEPTH):
                step(dve.tensor_copy(par[:, l, 0:PAR_W], bank[:, 3 * u[0], l * P:l * P + PAR_W]))
            for l in range(DEPTH):
                a, _ = PAR["norm1_g"]
                step(dve.tensor_scalar(par[:, l, a:a + 2 * KC], par[:, l, a:a + 2 * KC], math.sqrt(D_MODEL), None,
                                       ALU.mult))
                a, _ = PAR["final_g"]
                step(dve.tensor_scalar(par[:, l, a:a + KC], par[:, l, a:a + KC], math.sqrt(D_MODEL), None, ALU.mult))
                a, _ = PAR["subln_g"]
                one = CON["one_minus"][0]
                ins = dve.tensor_scalar(par[:, l, a:a + 1], par[:, l, a:a + 1], con[:, one + l:one + l + 1],
                                        math.sqrt(VDIM), ALU.mult, ALU.mult)
                if l == 0:
                    step(ins)
            ins.then_inc(g_free[u[0]], 1)
            released(dve, u)
            assert step.n <= STEP_SETUP, step.n
            base0 = step.n

            def norm_squares(ni):
                for k in range(1, KC):
                    dve.wait_ge(sq_done, ni * KC + k + 1)
                    if k == 1:
                        dve.scalar_tensor_tensor(out=rot[:, 0:T], in0=rot[:, 0:T], scalar=D_MODEL * EPS / P,
                                                 in1=sq_ring[1], op0=ALU.add, op1=ALU.add).then_inc(acc_done, 1)
                    else:
                        dve.wait_ge(acc_done, ni * (KC - 1) + k - 1)
                        dve.tensor_tensor(rot[:, 0:T], rot[:, 0:T], sq_ring[k % 2], ALU.add).then_inc(acc_done, 1)

            def norm_scale(ni, u):
                norm_squares(ni)
                dve.wait_ge(norm_rs, ni + 1)
                dve.tensor_tensor(bq[:, 0:SEQ].rearrange("p (b f) -> p b f", b=QT_N),
                                  ident[:, None, :].broadcast_to([P, QT_N, P]),
                                  rs[:, 0:QT_N].rearrange("p (b a) -> p b a", a=1).broadcast_to([P, QT_N, P]), ALU.mult
                                  ).then_inc(norm_diag, 1)
                dve.tensor_scalar(bq[:, SEQ:T], ident[:, 0:8], rs[:, QT_N:QT_N + 1], None, ALU.mult
                                  ).then_inc(norm_diag, 1)
                full(dve, u)

            def norm(ni, u, gains):
                norm_scale(ni, u)
                for k in range(KC + 1):
                    if k < KC:
                        if k >= 3:
                            j = k - 3
                            dve.wait_ge((lo_pool, lo_dve)[j % 2], ni * (KC // 2) + j // 2 + 1)
                        dve.scalar_tensor_tensor(out=tiles(sq_ring[k % 3]), in0=tiles(resid[:, k, :]), scalar=gains(k),
                                                 in1=grp3(u[0]), op0=ALU.mult, op1=ALU.mult).then_inc(y_done, 1)
                        if k == KC - 1:
                            dve.memset(small[:, 46:47], 0.0).then_inc(g_free[u[0]], 1)
                    j = k - 1
                    if j >= 1 and j % 2 == 1:
                        dve.wait_ge(hi_done, ni * KC + j + 1)
                        dve.tensor_tensor(act_lo[:, j, :], sq_ring[j % 3], act_hi[:, j, :].bitcast(F32), ALU.subtract
                                          ).then_inc(lo_dve, 1)

            def add_rows(uses, ms=range(KC)):
                for m in ms:
                    u = uses(m)
                    full(dve, u)
                    dve.tensor_tensor(tiles(resid[:, m, :]), grp3(u[0]), tiles(resid[:, m, :]), ALU.add
                                      ).then_inc(g_free[u[0]], 1)

            with dve.Fori(0, DEPTH) as l:
                norm(l * 2, use_layer(l, 0), lambda k: p_at("norm1_g", l, k))
                with dve.Fori(0, N_HEADS) as h:
                    it = l * N_HEADS + h
                    ug = lambda name: use_head(l, h, name)
                    ta = lambda name: t_head(l, h, name)
                    step = Chain(l * STEP_LAYER + h * STEP_HEAD + base0)
                    step(dve.tensor_copy(sub_gain, p_at("subln_g", l, 0)))
                    step(dve.tensor_scalar(neg_lam, lam[:, bass.ds(l, 1)], -1.0, None, ALU.mult))
                    released(dve, ug(("u",)))
                    step(dve.memset(ue[:, 0:POOL_HIST], 0.0))
                    src, dst = ue, pool_a
                    for k in range(4):
                        back, lo = 1 << k, (2 << k) - 1
                        step(dve.scalar_tensor_tensor(out=dst[:, lo:1167], in0=src[:, lo - back:1167 - back],
                                                      scalar=c_at("poolstep", h * 4 + k), in1=src[:, lo:1167],
                                                      op0=ALU.mult, op1=ALU.add))
                        src, dst = dst, (pool_b if k % 2 == 0 else pool_a)
                    step(dve.scalar_tensor_tensor(out=pool_dd[:, 0:SEQ], in0=pool_b[:, 15:15 + SEQ],
                                                  scalar=c_at("poolinv", h), in1=ue[:, 15:15 + SEQ],
                                                  op0=ALU.mult, op1=ALU.subtract))
                    step(dve.tensor_tensor(pool_dd[:, 0:16], pool_b[:, 15:31], c_at("poolhead", h * 16, 16), ALU.mult))
                    step(dve.tensor_tensor(pool_dd[:, 0:16], pool_dd[:, 0:16], ue[:, 15:31], ALU.subtract))
                    dve.scalar_tensor_tensor(out=pool_dd[:, SEQ:T], in0=pool_b[:, 1039 + 15:1167:16],
                                             scalar=c_at("poolinv", h), in1=ue[:, 1039 + 15:1167:16],
                                             op0=ALU.mult, op1=ALU.subtract).then_inc(pool_d, 1)

                    def rope(n, name, dst):
                        released(dve, ug(name))
                        for a in range(4):
                            to = 32 * (a ^ 1)
                            dve.tensor_copy(rot[to:to + 32, 0:T], dst[32 * a:32 * a + 32, :]).then_inc(dve_step, 1)
                        step.n += 4
                        dve.wait_ge(dve_step, step.base + step.n)
                        dve.tensor_tensor(dst[:, :], dst[:, :], c_("cos"), ALU.mult).then_inc(dve_step, 1)
                        dve.tensor_tensor(rot[:, 0:T], rot[:, 0:T], c_("sin"), ALU.mult).then_inc(dve_step, 1)
                        step.n += 2
                        dve.wait_ge(dve_step, step.base + step.n)
                        dve.tensor_tensor(dst[:, :], dst[:, :], rot[:, 0:T], ALU.add).then_inc(roped, 1)
                        dve.wait_ge(roped, it * 2 + n + 1)

                    dve.wait_ge(rope_in, 16)
                    rope(0, ("q",), qT)
                    dve.tensor_tensor(bq[:, 0:1024].rearrange("p (b f) -> p b f", b=8),
                                      ident[:, None, :].broadcast_to([P, 8, P]),
                                      qT[:, SEQ:T].rearrange("p (b a) -> p b a", a=1).broadcast_to([P, 8, P]), ALU.mult
                                      ).then_inc(diag_done, 1)
                    rope(1, ("k",), kT)
                    step(dve.tensor_tensor(qk8, qT[:, SEQ:T], kT[:, SEQ:T], ALU.mult))
                    step(dve.tensor_tensor(comp8, qk8[:, None, :].broadcast_to([P, 2, 8]),
                                           c_("compsel").rearrange("p (c a) -> p c a", a=1).broadcast_to([P, 2, 8]),
                                           ALU.mult))

                    def k_sum(b):
                        dve.wait_ge(k_mul, it * DEC_BATCH + b + 1)
                        src = page[:, b % 4, :, :].rearrange("p j (c d) -> p j c d", c=2)
                        dve.tensor_reduce(s_score[:, :, b, :].rearrange("p c j -> p j c"), src, AX_X, ALU.add
                                          ).then_inc(k_red, 1)

                    u = ug(("y",))
                    dve.wait_ge(y_hi_done, it + 2)
                    dve.scalar_tensor_tensor(out=tiles(mix_lo[:, :]), in0=grp3(u[0]), scalar=p_at("pool_scale", l, h),
                                             in1=tiles(mix_hi[:, :].bitcast(F32)), op0=ALU.mult, op1=ALU.subtract
                                             ).then_inc(g_free[u[0]], 1)
                    for b in range(3):
                        k_sum(b)
                    for m in range(KC):
                        add_rows(lambda m_: ug(("wg", m_)), (m,))
                        if m in (1, 3, 5):
                            k_sum(3 + m // 2)

                    def maxima(s):
                        width = (ORDER[s] + 1) * P
                        for c in range(2):
                            u = ug(("s", s, c))
                            full(dve, u)
                            src = bank[:, 3 * u[0]:3 * u[0] + 2, :].rearrange("p a b -> p (a b)")[:, 0:width]
                            step(dve.tensor_reduce(stat[:, s % 2, c:c + 1], src, AX_X, ALU.max))
                            dve.tensor_scalar(stat[:, s % 2, 2 + c:3 + c], stat[:, s % 2, c:c + 1],
                                              -(HEAD_DIM ** -0.5), None, ALU.mult).then_inc(att_bias, 1)

                    def combine(s):
                        width = (ORDER[s] + 1) * P
                        released(dve, ug(("s", s, 0)))
                        released(dve, ug(("s", s, 1)))
                        st = stat[:, s % 2, :]
                        step(dve.reciprocal(st[:, 5:6], st[:, 5:6]))
                        step(dve.scalar_tensor_tensor(out=st[:, 5:6], in0=st[:, 5:6], scalar=neg_lam, in1=st[:, 4:5],
                                                      op0=ALU.mult, op1=ALU.mult))
                        pr = probs[s % 2]
                        dve.scalar_tensor_tensor(out=pr[:, 0, 0:width], in0=pr[:, 1, 0:width], scalar=st[:, 5:6],
                                                 in1=pr[:, 0, 0:width], op0=ALU.mult, op1=ALU.add).then_inc(att_a, 1)
                        dve.reciprocal(st[:, 7:8], st[:, 4:5]).then_inc(inv_done, 1)

                    def normalise(s):
                        rows = out_rows(s)[1]
                        dve.wait_ge(att_rms, it * O_HEAD + s + 1)
                        ss = stat[0:rows, s % 2, 6:7]
                        src = s_bank if s == SAMPLES else o_bank
                        dve.tensor_scalar(o_norm[0:rows, s % 2, :], src[0:rows, 0:P], ss, inv_sum(s), ALU.mult, ALU.mult
                                          ).then_inc(o_free, 1)

                    def mix(s):
                        at, n = out_rows(s)
                        dve.wait_ge(mix_hi_done, it * O_HEAD + s + 1)
                        dve.scalar_tensor_tensor(out=mix_lo[:, at:at + n], in0=t_bank[:, 0:n],
                                                 scalar=sub_gain, in1=mix_hi[:, at:at + n].bitcast(F32),
                                                 op0=ALU.mult, op1=ALU.subtract).then_inc(t_free, 1)

                    maxima(0)
                    k_sum(6)
                    k_sum(7)
                    for s in range(QT_N):
                        if s >= 2:
                            mix(s - 2)
                        combine(s)
                        if s >= 1:
                            normalise(s - 1)
                        if s + 1 < QT_N:
                            maxima(s + 1)
                        if s == SOFTMAX_STEP + 1:
                            released(dve, ug(("soft",)))
                            step(dve.tensor_reduce(soft_m, soft[:, 0:PAST_LEN + 1], AX_X, ALU.max))
                            dve.tensor_scalar(soft_nb, soft_m, -(HEAD_DIM ** -0.5), None, ALU.mult
                                              ).then_inc(soft_bias, 1)
                        if s == WEIGHTS_STEP:
                            dve.wait_ge(soft_exp, it + 1)
                            step(dve.reciprocal(soft_l, soft_l))
                            step(dve.tensor_tensor(soft_cf, soft_l, lam[0:16, bass.ds(l + 8, 1)], ALU.mult))
                            step(dve.tensor_scalar(sel8, c_("rowsel", slice(0, 16)), soft_cf, None, ALU.mult))
                            dve.tensor_scalar(diag8, sel8, soft[:, PAST_LEN:PAST_LEN + 1], None, ALU.mult
                                              ).then_inc(soft_sel, 1)
                            dve.wait_ge(weights_full, it + 1)
                            w = s_bank[:, 0:64].rearrange("p (j b a) -> p j b a", j=8, a=1).broadcast_to([P, 8, 8, 8])
                            d = c_("delta").rearrange("p (o b a) -> p o b a", o=1, b=8).broadcast_to([P, 8, 8, 8])
                            dve.tensor_tensor(spread[:, :, :, :], w, d, ALU.mult).then_inc(spread_done, 1)
                    normalise(QT_N - 1)
                    mix(QT_N - 2)
                    normalise(QT_N)
                    mix(QT_N - 1)
                    mix(QT_N)
                    add_rows(lambda m: ug(("wh", m)))
                    assert step.n == STEP_HEAD, step.n

                norm(l * 2 + 1, use_layer(l, G0_NORM2), lambda k: p_at("norm2_g", l, k))
                fstep = l * STEP_LAYER + (N_HEADS * STEP_HEAD + 1 + base0)

                def taps(c):
                    dve.wait_ge(taps0, l * FC + c + 1)
                    dve.scalar_tensor_tensor(out=conv_c[:, :], in0=ext[:, 1:1049], scalar=p_at("conv_w", l, c + FC),
                                             in1=conv_c[:, :], op0=ALU.mult, op1=ALU.add).then_inc(dve_step, 1)
                    dve.wait_ge(dve_step, fstep + c + 1)
                    dve.scalar_tensor_tensor(out=conv_c[:, :], in0=ext[:, 0:1048], scalar=p_at("conv_w", l, c),
                                             in1=conv_c[:, :], op0=ALU.mult, op1=ALU.add).then_inc(conv_done, 1)

                def gate_b(c, u):
                    full(dve, u)
                    dve.wait_ge(silu_done, l * FC + c + 1)
                    dve.tensor_tensor(tiles(gate[:, :]), grp3(u[0]), tiles(gate[:, :]), ALU.mult
                                      ).then_inc(g_free[u[0]], 1)
                    dve.wait_ge(g_hi_done, l * FC + c + 1)
                    dve.tensor_tensor(mix_lo[:, :], gate[:, :], mix_hi[:, :].bitcast(F32), ALU.subtract
                                      ).then_inc(g_lo_done, 1)

                dve.wait_ge(taps0, l * FC + 1)
                dve.memset(ext[:, 0:2], 0.0).then_inc(dve_step, 1)
                dve.wait_ge(dve_step, fstep)
                taps(0)
                with dve.Fori(0, FC - 1) as i:
                    gate_b(i, use_ffn(l, i, 0))
                    add_rows(lambda m: use_ffn(l, i, 2 + m))
                    taps(i + 1)
                gate_b(FC - 1, use_ffn(l, FC - 1, 0))
                add_rows(lambda m: use_ffn(l, FC - 1, 1 + m))

            half = G_SETUP // 2 + DEPTH * (G_LAYER // 2)
            norm_squares(2 * DEPTH)
            for k in range(KC):
                dve.tensor_scalar(resid[:, k, :], resid[:, k, :], p_at("final_g", 0, k), None, ALU.mult
                                  ).then_inc(y_done, 1)
            dve.wait_ge(norm_rs, 2 * DEPTH + 1)
            for t in range(0, QT_N + 1, 2):
                u = use(half, t)
                full(dve, u)
                rows = P if t < QT_N else 8
                src = bank[0:rows, 3 * u[0]:3 * u[0] + 2, :].rearrange("p a b -> p (a b)")
                dve.tensor_scalar(x_buf(t)[0:rows, :], src, rs[0:rows, t:t + 1], None, ALU.mult
                                  ).then_inc(g_free[u[0]], 1)


_INS = ["x_prompt", "x_sample", "cache_k", "cache_v", "state_pool", "state_conv", "page_table", "norm1_g", "w_in",
        "pool_w", "pool_scale", "lam_q1", "lam_k1", "lam_q2", "lam_k2", "subln_g", "w_out", "norm2_g", "w_up",
        "conv_w", "conv_b", "w_down", "final_g"]
_OUTS = [(1, SEQ, D_MODEL), (DEC_BATCH, 1, D_MODEL), (DEPTH, 1, SEQ // PAGE_SIZE, PAGE_SIZE, N_HEADS, VDIM),
         (DEPTH, 1, SEQ // PAGE_SIZE, PAGE_SIZE, N_HEADS, VDIM), (DEPTH, 1, POOL_HIST, POOL_W), (DEPTH, 1, 2, D_FF),
         (DEPTH, DEC_BATCH, 1, N_HEADS, VDIM), (DEPTH, DEC_BATCH, 1, N_HEADS, VDIM),
         (DEPTH, DEC_BATCH, POOL_HIST, POOL_W), (DEPTH, DEC_BATCH, 2, D_FF)]


def layouts(inputs):
    arrays = {f"in_{name}": np.asarray(inputs[name]) for name in _INS}
    for name in ("in_cache_k", "in_cache_v"):
        arrays[name] = arrays[name].transpose(0, 3, 1, 2, 4).reshape(-1, RUN * VDIM)
    for name in ("in_w_in", "in_w_up"):
        w = arrays[name].reshape(DEPTH, KC, P, -1, P)
        arrays[name] = w.transpose(0, 3, 2, 1, 4).reshape(DEPTH, -1, P, KC * P)
    arrays["in_page_table"] = arrays["in_page_table"].transpose(1, 0)
    arrays = {name: np.ascontiguousarray(a) for name, a in arrays.items()}
    arrays["in_table"] = constants()
    return arrays


def kernel(**inputs):
    import concourse.bacc as bacc
    from concourse.bass_utils import run_bass_kernel_spmd

    nc = bacc.Bacc("TRN2", target_bir_lowering=False, num_devices=1)
    arrays = layouts(inputs)
    args = [nc.dram_tensor(name, a.shape, mybir.dt.from_np(a.dtype), kind="ExternalInput").ap()
            for name, a in arrays.items()]
    args += [nc.dram_tensor(f"out_{i}", shape, F32, kind="ExternalOutput").ap() for i, shape in enumerate(_OUTS)]
    hybrid_decoder_kernel(nc, *args)
    r = run_bass_kernel_spmd(nc, [arrays], core_ids=[0])
    return tuple(r.results[0][f"out_{i}"] for i in range(len(_OUTS)))
```

```python
import math
from contextlib import ExitStack

import numpy as np

import concourse.bass as bass
from concourse import mybir

F32 = mybir.dt.float32
F32R = mybir.dt.float32r
I32 = mybir.dt.int32
BF16 = mybir.dt.bfloat16
ALU = mybir.AluOpType
ACT = mybir.ActivationFunctionType
AX_X = mybir.AxisListType.X

P = 128
D_MODEL, SEQ, DEPTH, DEC_BATCH = 1024, 1024, 2, 8
PAST_LEN, PAGE_SIZE = 1024, 128
N_PAGES = PAST_LEN // PAGE_SIZE
RUN = 8
GROUPS = PAGE_SIZE // RUN
assert GROUPS * N_PAGES == P and RUN == N_PAGES
POOL_W, POOL_WINDOWS, POOL_HIST = 512, (2, 4, 8, 16), 15
N_HEADS, HEAD_DIM = 4, 64
VDIM = 2 * HEAD_DIM
D_FF = 2816
EPS = 1e-6
ROPE_THETA = 10000.0
NEG = -2.0 ** 100

T = SEQ + DEC_BATCH
NT = 3
TW = T // NT
KC = D_MODEL // P
FC = D_FF // P
QT_N = SEQ // P
T_ORDER = (0, 2, 1)
PAIRS = KC // 2
TILE_USES = NT * PAIRS
PARTS = [(a, min(P, TW - a)) for a in range(0, TW, P)]
CONV_TAPS = 3

SLOTS = 3
U_HEAD = 6
U_FFN0 = U_HEAD * N_HEADS
U_LAYER = U_FFN0 + 3 * FC

ORDER = [7, 0, 6, 1, 5, 2, 4, 3]
SOFTMAX_STEP = 1
WEIGHTS_STEP = 3
VALUES_AT = {4: (0, 1), 5: (2, 3), 6: (4, 5), 7: (6, 7)}


def rounds(i):
    return [list(range(a, min(a + 4, i + 1))) for a in range(0, i + 1, 4)]


def head_uses():
    g, t = [("u",), ("q",), ("k",), ("qb", 0), ("qb", 1), ("y",), ("v",)], ["state", "uout"]
    t += [("k", 0), ("k", 1), "small"]
    g += [("wg", m) for m in range(KC)]
    t += [("v", 0), ("v", 1)]
    g += [("s", 0, 0), ("s", 0, 1)]
    for s in range(QT_N):
        if s + 1 < QT_N:
            g += [("s", s + 1, 0), ("s", s + 1, 1)]
        t += [("p", s)] * (len(rounds(ORDER[s])) - 1)
        if s >= 1:
            t.append(("o", s - 1))
        if s == SOFTMAX_STEP:
            g.append(("soft",))
    t += [("o", QT_N - 1), ("o", QT_N)]
    g += [("wh", j) for j in range(TILE_USES)]
    return {k: n for n, k in enumerate(g)}, {k: n for n, k in enumerate(t)}


HG, HT = head_uses()
G_HEAD, T_HEAD, O_HEAD = len(HG), len(HT), QT_N + 1
assert G_HEAD % 2 == 0
G_SETUP = 10
G_FFN = 2 + KC
G0_A0 = G_HEAD * N_HEADS
G0_FFN = G0_A0 + 1
G_LAYER = G0_FFN + G_FFN * (FC - 1) + 1 + TILE_USES
assert G_LAYER % 2 == 0
T0_HEADS = NT
T0_NORM2 = T0_HEADS + T_HEAD * N_HEADS
T0_FFN = T0_NORM2 + NT
T_LAYER = T0_FFN + 2 * FC
W_CREDIT, V_CREDIT = SLOTS, DEC_BATCH
SAMPLES = QT_N - 1


def out_rows(n):
    return (SEQ, DEC_BATCH) if n == SAMPLES else (ORDER[min(n, QT_N - 1)] * P, P)


CON = {}
for _name, _width in (("ident", P), ("ones", P), ("causal", P), ("delta", 64), ("rowsel", 8), ("sign", 2),
                      ("compsel", 2), ("group", 1), ("neghalf", 1), ("eps", 1), ("eps_d", 1), ("poolstep", 16),
                      ("poolinv", 4), ("poolhead", 64), ("lam_init", DEPTH),
                      ("one_minus", DEPTH), ("cos", T), ("sin", T)):
    _at = sum(w for _, w in CON.values())
    CON[_name] = (_at, _width)
CON_W = sum(w for _, w in CON.values())
CON_SMALL = CON["cos"][0]

PAR = {}
for _name, _n in (("conv_w", CONV_TAPS * FC), ("conv_b", FC), ("norm1_g", KC), ("norm2_g", KC), ("pool_scale", 4),
                  ("subln_g", 1), ("final_g", KC)):
    PAR[_name] = (sum(n for _, n in PAR.values()), _n)
PAR_W = sum(n for _, n in PAR.values())


def constants():
    c = np.zeros((P, CON_W), np.float32)

    def put(name, value, rows=slice(None)):
        a, w = CON[name]
        c[rows, a:a + w] = np.asarray(value, np.float32).reshape(-1, w) if np.ndim(value) else value

    put("ident", np.eye(P))
    put("ones", 1.0)
    put("causal", np.where(np.arange(P)[None, :] > np.arange(P)[:, None], NEG, 0.0))
    put("delta", np.broadcast_to(np.eye(8).reshape(1, 64), (P, 64)))
    put("rowsel", np.tile(np.eye(8), (2, 1)), slice(0, 16))
    put("sign", np.repeat([[1.0, 0.0], [0.0, -1.0]], 8, axis=0), slice(0, 16))
    put("compsel", np.repeat(np.eye(2), 64, axis=0))
    put("group", (np.arange(P) % GROUPS).reshape(P, 1))
    put("neghalf", -0.5)
    put("eps", VDIM * EPS)
    put("eps_d", D_MODEL * EPS)
    put("poolstep", np.broadcast_to([[1.0 if k <= g else 0.0 for g in range(4) for k in range(4)]], (P, 16)))
    put("poolinv", np.broadcast_to([[1.0 / w for w in POOL_WINDOWS]], (P, 4)))
    put("poolhead", np.broadcast_to([[1.0 / min(t + 1, w) for w in POOL_WINDOWS for t in range(16)]], (P, 64)))
    li = [0.8 - 0.6 * math.exp(-0.3 * n) for n in range(DEPTH)]
    put("lam_init", np.broadcast_to([li], (P, DEPTH)))
    put("one_minus", np.broadcast_to([[1.0 - x for x in li]], (P, DEPTH)))
    half = HEAD_DIM // 2
    inv = (1.0 / (np.float32(ROPE_THETA) ** (np.arange(half, dtype=np.float32) * np.float32(2.0 / HEAD_DIM)))
           ).astype(np.float32)
    pos = np.concatenate([np.arange(SEQ), np.full(DEC_BATCH, PAST_LEN)]).astype(np.float32)
    ang = (pos[None, :] * inv[:, None]).astype(np.float32).astype(np.float64)
    cos, sin = np.cos(ang), np.sin(ang)
    put("cos", np.tile(cos, (4, 1)))
    put("sin", np.concatenate([-sin, sin, -sin, sin]))
    return c


def hybrid_decoder_kernel(nc, x_prompt, x_sample, cache_k, cache_v, state_pool, state_conv, page_table, norm1_g, w_in,
                          pool_w, pool_scale, lam_q1, lam_k1, lam_q2, lam_k2, subln_g, w_out, norm2_g, w_up, conv_w,
                          conv_b, w_down, final_g, table, y_prompt, y_sample, k_new_prompt, v_new_prompt,
                          pool_new_prompt, conv_new_prompt, k_new_sample, v_new_sample, pool_new_sample,
                          conv_new_sample):
    with ExitStack() as ctx:
        def sb(name, shape, dt=F32):
            return ctx.enter_context(nc.sbuf_tensor(name, shape, dt))

        def sem(name):
            return ctx.enter_context(nc.semaphore(name))

        resid = sb("resid", [P, KC, T])
        act_hi = sb("act_hi", [P, KC, T], F32R)
        act_lo = sb("act_lo", [P, KC, T], F32R)
        w_raw = sb("w_raw", [P, SLOTS, 1024])
        w_hi = sb("w_hi", [P, SLOTS, 1024], F32R)
        w_lo = sb("w_lo", [P, SLOTS, 1024], F32R)
        con = sb("con", [P, CON_W])
        par = sb("par", [P, DEPTH, P])
        mask = sb("mask", [P, 2, P], BF16)
        scratch = sb("scratch", [P, 3104])
        rot = sb("rot", [P, 1168])
        bq = sb("bq", [P, T])
        qT = sb("qT", [P, T])
        kT = sb("kT", [P, T])
        v_tok = sb("v_tok", [P, QT_N, P])
        k_tok = v_tok
        mix_hi = sb("mix_hi", [P, T], F32R)
        mix_lo = sb("mix_lo", [P, T], F32R)
        a_T = sb("a_T", [P, 2, 512])
        page = sb("page", [P, 4, RUN, P])
        stat = sb("stat", [P, 2, 8])
        small = sb("small", [P, 48])
        rs = sb("rs", [P, QT_N + 1])
        pw = sb("pw", [P, P])
        state_in = sb("state_in", [120, P])
        rows_out = sb("rows_out", [P, P])
        v_dup = sb("v_dup", [16, P])
        lam = sb("lam", [P, 16])
        pages = sb("pages", [P, DEC_BATCH], I32)
        idx_k = sb("idx_k", [P, DEC_BATCH], I32)
        idx_v = sb("idx_v", [P, DEC_BATCH], I32)
        idx_now = sb("idx_now", [P, 1], I32)
        idx_inc = sb("idx_inc", [P, DEC_BATCH], I32)

        bank = ctx.enter_context(nc.psum_tensor("bank", [P, 8, 512], F32))
        t_bank = bank[:, 6, :]
        o_bank = bank[:, 7, :]
        p_bank = bank[:, 2, :]
        s_bank = bank[:, 5, :]

        table_in, rope_in, params_in, lam_in_s, pages_in = (sem("table_in"), sem("rope_in"), sem("params_in"),
                                                            sem("lam_landed"), sem("pages_in"))
        x_in = [sem(f"x_in{i}") for i in range(QT_N + 1)]
        w_in_s = [sem(f"w_landed{i}") for i in range(SLOTS)]
        page_in = [sem(f"page_landed{i}") for i in range(4)]
        pw_in, sp_in, sc_in = sem("pool_w_landed"), sem("state_pool_landed"), sem("state_conv_landed")
        k_out_s, v_out_s, small_out, u_out_s = sem("k_stored"), sem("v_stored"), sem("small_stored"), sem("u_stored")
        conv_out_s, pool_copy, y_out = sem("conv_stored"), sem("pool_copied"), sem("y_stored")
        g_full, g_free = [sem("group0_full"), sem("group1_full")], [sem("group0_free"), sem("group1_free")]
        t_full, t_free = sem("tbank_full"), sem("tbank_free")
        p_full, p_free = sem("pbank_full"), sem("pbank_free")
        o_full, o_free = sem("obank_full"), sem("obank_free")
        w_hi_done, w_lo_done = sem("w_hi_done"), sem("w_lo_done")
        sum_done, bc_full, bc_free = sem("square_sums"), sem("rms_spread"), sem("rms_taken")
        sq_done, acc_done, y_done, hi_done = sem("sq_done"), sem("acc_done"), sem("y_done"), sem("act_hi_done")
        lo_pool, lo_dve = sem("act_lo_pool"), sem("act_lo_dve")
        pool_d, roped, diag_done = sem("pool_d_done"), sem("roped"), sem("diag_done")
        y_hi_done, k_mul, k_red = sem("pool_y_hi_done"), sem("k_multiplied"), sem("k_reduced")
        att_bias, att_a, att_sq, mix_hi_done = (sem("att_bias"), sem("att_weights"), sem("att_squares"),
                                                sem("mix_hi_done"))
        inv_done = sem("inv_sum_done")
        idx_ready, idx_step = sem("idx_ready"), sem("idx_step")
        att_rms, pool_step, norm_diag, norm_rs = sem("att_rms"), sem("pool_step"), sem("norm_diag"), sem("norm_rs")
        weights_full, spread_done = sem("sample_weights_full"), sem("sample_weights_spread")
        soft_exp = sem("soft_exp_done")
        soft_bias, soft_sel, v_used = sem("soft_bias"), sem("soft_sel"), sem("v_used")
        taps0, conv_done, silu_done, g_hi_done, g_lo_done = (sem("tap2_done"), sem("conv_done"), sem("silu_done"),
                                                             sem("gate_hi_done"), sem("gate_lo_done"))
        dve_step, act_step, lam_sum, lam_exp = sem("dve_step"), sem("act_step"), sem("lam_sum"), sem("lam_exp")

        def c_(name, rows=slice(None)):
            a, w = CON[name]
            return con[rows, a:a + w]

        def sl(n, width):
            return slice(n, n + width) if isinstance(n, int) else bass.ds(n, width)

        def c_at(name, n, width=1, rows=slice(None)):
            a, _ = CON[name]
            return con[rows, sl(n + a, width)]

        def p_at(name, layer, n, width=1):
            a, _ = PAR[name]
            return par[:, layer, sl(n + a, width)]

        ident, ones = c_("ident"), c_("ones")

        def tile_of(i):
            return slice(T_ORDER[i] * TW, (T_ORDER[i] + 1) * TW)

        page_all = page[:, :, :, :].rearrange("p s t d -> p (s t d)")

        def squares_of(i, j):
            if i < 2:
                src = (scratch, page_all)[i][:, 2 * TW * j:2 * TW * (j + 1)]
            else:
                src = (page_all[:, TW * KC:TW * (KC + 2)], a_T[:, :, :].rearrange("p a b -> p (a b)")[:, 0:2 * TW],
                       v_tok[:, :, :].rearrange("p a b -> p (a b)")[:, 0:2 * TW], rot[:, 0:2 * TW])[j]
            return src.rearrange("p (a b) -> p a b", a=2)

        def low_by_dve(n):
            return n % 3 == 2

        def low_done(eng, ni, n):
            if low_by_dve(n):
                eng.wait_ge(lo_dve, ni * (NT * KC // 3) + n // 3 + 1)
            else:
                eng.wait_ge(lo_pool, ni * (2 * NT * KC // 3) + n - n // 3 + 1)

        def scaled(n):
            at = n % 6
            return (qT, kT)[at // 3][:, at % 3 * TW:(at % 3 + 1) * TW]

        def x_buf(t):
            if t < 3:
                return scratch[:, 1024 * t:1024 * t + 1024]
            if t < 7:
                return page[:, t - 3, :, :].rearrange("p t d -> p (t d)")
            return (qT, kT)[t - 7][:, 0:1024]

        def page_landed(eng, it, n):
            eng.wait_ge(page_in[n % 4], (it * (2 * DEC_BATCH // 4) + n // 4 + 1) * 16)

        def grp(p):
            return bank[:, 3 * p:3 * p + 3, :]

        def grp3(p):
            return bank[:, 3 * p:3 * p + 3, 0:TW]

        def tiles(ap):
            return ap.rearrange("p (a b) -> p a b", a=NT)

        sq_ring = [scratch[:, i * T:(i + 1) * T] for i in range(3)]
        ue, pool_a, pool_b = scratch[:, 0:1167], scratch[:, 1167:2334], rot[:, 0:1167]
        pool_dd = scratch[:, 1167:1167 + T]
        v_T = rot[:, 0:T]
        ext, conv_c = scratch[:, 0:1050], scratch[:, 1050:2098]
        ext_tail = ext[:, 1024:1050]
        gate = rot[:, 0:T]
        spread = rot[:, 0:512].rearrange("p (j b a) -> p j b a", j=N_PAGES, b=8)
        o_norm = rot[:, 512:768].rearrange("p (s d) -> p s d", s=2)
        junk = rot[:, 768:1024].rearrange("p (s d) -> p s d", s=2)
        s_score = rot[:, T + 8:T + 136].rearrange("p (c b j) -> p c b j", c=2, b=8)
        u_out, us_out, ks_out, conv_out = (rows_out[0:POOL_HIST, :], rows_out[32:40, :], rows_out[64:72, :],
                                           rows_out[96:122, :])
        lam_in = a_T[:, 0, :].rearrange("p (n d) -> p n d", n=4)
        soft = bq[0:16, 0:1025]
        probs = [scratch[:, 0:2048].rearrange("p (c k) -> p c k", c=2),
                 scratch[:, 2048:3072].rearrange("p (c k) -> p c k", c=2)]
        u_hist = ue[:, 1039:1167].rearrange("p (b j) -> p b j", b=8)
        qk8, comp8 = small[:, 0:8], small[:, 8:24].rearrange("p (c b) -> p c b", c=2)
        sel8, diag8 = small[0:16, 24:32], small[0:16, 32:40]
        soft_m, soft_nb, soft_l, soft_cf = (small[0:16, 40:41], small[0:16, 41:42], small[0:16, 42:43],
                                            small[0:16, 43:44])
        sub_gain, neg_lam = small[:, 44:45], small[:, 45:46]

        def inv_sum(n):
            if n == SAMPLES:
                return c_("ones", slice(0, DEC_BATCH))[:, 0:1]
            return stat[:, min(n, QT_N - 1) % 2, 7:8]

        def use(half, j):
            return j % 2, half + j // 2

        def use_head(l, h, name):
            return use(G_SETUP // 2 + l * (G_LAYER // 2) + h * (G_HEAD // 2), HG[name])

        def use_ffn(l, i, j):
            return use(G_SETUP // 2 + l * (G_LAYER // 2) + i * (G_FFN // 2), G0_FFN + j)

        def use_layer(l, j):
            return use(G_SETUP // 2 + l * (G_LAYER // 2), j)

        def full(eng, u):
            eng.wait_ge(g_full[u[0]], u[1] + 1)

        def released(eng, u):
            eng.wait_ge(g_free[u[0]], u[1] + 2)

        def t_head(l, h, name):
            return l * T_LAYER + h * T_HEAD + (T0_HEADS + HT[name])

        def t_ffn(l, i, j):
            return l * T_LAYER + i * 2 + (T0_FFN + j)

        def w_landed(eng, l, h_or_i, off, per):
            eng.wait_ge(w_in_s[off % SLOTS], (l * (U_LAYER // SLOTS) + h_or_i * per + off // SLOTS) * 16 + 16)

        N_POOL = cache_k.shape[0] // (DEPTH * N_HEADS * GROUPS)

        block = ctx.enter_context(nc.Block())

        @block.sync
        def _(sp):
            sp.dma_start(con[:, 0:CON_SMALL], table[:, 0:CON_SMALL]).then_inc(table_in, 16)
            for t in range(QT_N + 1):
                if t < QT_N:
                    sp.dma_start(x_buf(t), x_prompt[0, t * P:(t + 1) * P, :]).then_inc(x_in[t], 16)
                else:
                    sp.dma_start(x_buf(t)[0:8], x_sample.rearrange("b a d -> (b a) d")).then_inc(x_in[t], 16)
            for j in range(N_PAGES):
                sp.dma_start(pages[j * GROUPS:(j + 1) * GROUPS, :],
                             page_table[j:j + 1, :].broadcast_to([GROUPS, DEC_BATCH])).then_inc(pages_in, 16)
            for l in range(DEPTH):
                rows = [("conv_w", conv_w[l].rearrange("j (c p) -> (j c) p", p=P)),
                        ("conv_b", conv_b[l].rearrange("(c p) -> c p", p=P)),
                        ("norm1_g", norm1_g[l].rearrange("(c p) -> c p", p=P)),
                        ("norm2_g", norm2_g[l].rearrange("(c p) -> c p", p=P)),
                        ("pool_scale", pool_scale[l].rearrange("(c p) -> c p", p=P)),
                        ("subln_g", subln_g[l].rearrange("(c p) -> c p", p=P)),
                        ("final_g", final_g.rearrange("(c p) -> c p", p=P))]
                for name, src in rows:
                    a, n = PAR[name]
                    sp.dma_start(k_tok[a:a + n, l, :], src).then_inc(params_in, 16)
            for n, v in enumerate((lam_q1, lam_k1, lam_q2, lam_k2)):
                src = v.rearrange("l d -> (l d)").rearrange("(a n) -> a n", a=1).broadcast_to([P, DEPTH * HEAD_DIM])
                sp.dma_start(lam_in[:, n, :], src).then_inc(lam_in_s, 16)
            sp.dma_start(con[:, CON_SMALL:CON_W], table[:, CON_SMALL:CON_W]).then_inc(rope_in, 16)

            def load_unit(n, slot, src):
                sp.wait_ge(w_lo_done, n + 1)
                sp.dma_start(w_raw[:, slot, :], src).then_inc(w_in_s[slot], 16)

            def head_loads(l, h, next_units):
                it = l * N_HEADS + h
                sp.wait_ge(y_hi_done, it + 1)
                sp.dma_start(pw[:, :], pool_w[l, h]).then_inc(pw_in, 16)
                sp.wait_ge(t_full, l * T_LAYER)
                sp.dma_start(state_in[:, :], state_pool[l].rearrange("b j c -> (b j) c")[:, sl(h * P, P)]
                             ).then_inc(sp_in, 16)
                n0 = l * U_LAYER + h * U_HEAD
                load_unit(n0 + 2, 2, w_in[l, h + 8])
                load_unit(n0 + 3, 0, w_in[l, h + 12])
                load_unit(n0 + 4, 1, w_out[l, sl(h * P, P), :])
                load_unit(n0 + 5, 2, w_out[l, sl(h * P + POOL_W, P), :])

                next_units(n0 + U_HEAD)

            with sp.Fori(0, DEPTH) as l:
                def load_u_q(h, n0):
                    load_unit(n0, 0, w_in[l, h])
                    load_unit(n0 + 1, 1, w_in[l, h + 4])

                def load_a_b(n0):
                    load_unit(n0, 0, w_up[l, 0])
                    load_unit(n0 + 1, 1, w_up[l, FC])

                load_u_q(0, l * U_LAYER)
                with sp.Fori(0, N_HEADS - 1) as h:
                    head_loads(l, h, lambda n0: load_u_q(h + 1, n0))
                head_loads(l, N_HEADS - 1, load_a_b)

                def load_state(c):
                    sp.wait_ge(t_full, l * T_LAYER + c * 2 + (T0_FFN - 1))
                    sp.dma_start(state_in[0:16, :],
                                 state_conv[l].rearrange("b j c -> (b j) c")[:, sl(c * P, P)]
                                 ).then_inc(sc_in, 16)

                def load_a(i, n, slot):
                    load_unit(n, slot, w_up[l, i])

                def load_b(i, n, slot):
                    load_unit(n, slot, w_up[l, i + FC])

                def load_d(i, n, slot):
                    load_unit(n, slot, w_down[l, sl(i * P, P), :])

                f0 = l * U_LAYER + U_FFN0
                load_state(0)
                with sp.Fori(0, FC - 1) as i:
                    load_a(i + 1, f0 + i * 3 + 2, 2)
                    load_state(i + 1)
                    load_d(i, f0 + i * 3 + 3, 0)
                    load_b(i + 1, f0 + i * 3 + 4, 1)
                load_d(FC - 1, f0 + 3 * FC - 1, 2)

            for t in range(QT_N + 1):
                released(sp, use(G_SETUP // 2 + DEPTH * (G_LAYER // 2), t))
                rows = P if t < QT_N else 8
                dst = y_prompt[0, t * P:(t + 1) * P, :] if t < QT_N else y_sample.rearrange("b a d -> (b a) d")
                sp.dma_start(dst, x_buf(t)[0:rows]).then_inc(y_out, 16)
            sp.wait_ge(y_out, 16 * (QT_N + 1))

        @block.gpsimd
        def _(pool):
            for l in range(DEPTH):
                pool.dma_start(pool_new_sample[l, :, 0:POOL_HIST - 1, :], state_pool[l, :, 1:POOL_HIST, :]
                               ).then_inc(pool_copy, 16)

            def split_lo(n, slot):
                pool.wait_ge(w_hi_done, n + 1)
                pool.tensor_tensor(w_lo[:, slot, :], w_raw[:, slot, :], w_hi[:, slot, :].bitcast(F32), ALU.subtract
                                   ).then_inc(w_lo_done, 1)

            pool.memset(junk[:, 0, :], 0.0).then_inc(w_lo_done, W_CREDIT)
            pool.wait_ge(w_lo_done, W_CREDIT)

            neghalf = c_("neghalf")
            IDX_STEPS = 2 * DEC_BATCH + 2
            pool.wait_ge(idx_ready, 1)

            def norm(ni, t_use):
                def pair_sums(i):
                    for half in range(2):
                        pool.wait_ge(sq_done, ni * TILE_USES + i * PAIRS + half * 2 + 2)
                        a, b = squares_of(i, 2 * half), squares_of(i, 2 * half + 1)
                        pool.tensor_tensor(a, a, b, ALU.add).then_inc(sum_done, 1)

                def rms(i):
                    pool.wait_ge(t_free, t_use + i + 2)
                    cols = rs[:, i * len(PARTS):(i + 1) * len(PARTS)]
                    pool.tensor_tensor(cols, cols, neghalf.broadcast_to([P, len(PARTS)]), ALU.pow).then_inc(norm_rs, 1)

                def low(i, k):
                    n = i * KC + k
                    pool.wait_ge(hi_done, ni * NT * KC + n + 1)
                    pool.tensor_tensor(act_lo[:, k, tile_of(i)], scaled(n), act_hi[:, k, tile_of(i)].bitcast(F32),
                                       ALU.subtract).then_inc(lo_pool, 1)

                pair_sums(0)
                pair_sums(1)
                rms(0)
                pair_sums(2)
                rms(1)
                for n in range(NT * KC):
                    if n == 4:
                        rms(2)
                    if not low_by_dve(n):
                        low(n // KC, n % KC)

            def output_rms(l, it, s):
                rows = out_rows(s)[1]
                ss = stat[0:rows, s % 2, 6:7]
                pool.wait_ge(att_sq, it * O_HEAD + s + 1)
                pool.tensor_tensor(ss, ss, c_("eps")[0:rows], ALU.add).then_inc(pool_step, 1)
                pool.wait_ge(pool_step, it * O_HEAD + s + 1)
                pool.tensor_tensor(ss, ss, neghalf[0:rows], ALU.pow).then_inc(att_rms, 1)

            with pool.Fori(0, DEPTH) as l:
                n0 = l * U_LAYER
                split_lo(n0, 0)
                split_lo(n0 + 1, 1)
                norm(l * 2, l * T_LAYER)
                with pool.Fori(0, N_HEADS) as h:
                    it = l * N_HEADS + h
                    n = l * U_LAYER + h * U_HEAD

                    def k_product(b):
                        page_landed(pool, it, b)
                        kp = page[:, b % 4, :, :]
                        q_row = bq[:, None, b * P:(b + 1) * P].broadcast_to([P, N_PAGES, P])
                        pool.tensor_tensor(kp, kp, q_row, ALU.mult).then_inc(k_mul, 1)

                    steps = 0

                    def index_step(out, in0, in1):
                        nonlocal steps
                        pool.wait_ge(idx_step, it * IDX_STEPS + steps)
                        pool.tensor_tensor(out, in0, in1, ALU.add).then_inc(idx_step, 1)
                        steps += 1

                    def load(n):
                        if n < 4:
                            pool.wait_ge(v_used, it * DEC_BATCH + n + 5)
                        elif n < DEC_BATCH + 4:
                            pool.wait_ge(k_red, it * DEC_BATCH + n - 3)
                        else:
                            pool.wait_ge(v_used, it * DEC_BATCH + V_CREDIT + n - 11)
                        cache, rows = ((cache_k, idx_k), (cache_v, idx_v))[n // DEC_BATCH]
                        rows = rows[:, n % DEC_BATCH:n % DEC_BATCH + 1]
                        index_step(idx_now[:, :], rows, idx_inc[:, 0:1])
                        pool.indirect_dma_start(page[:, n % 4, :, :].rearrange("p t d -> p (t d)"), None, cache,
                                                bass.IndirectOffsetOnAxis(rows, 0)).then_inc(page_in[n % 4], 16)

                    for n_ in range(4):
                        load(n_)
                    split_lo(n + 2, 2)
                    split_lo(n + 3, 0)
                    split_lo(n + 4, 1)
                    released(pool, use_head(l, h, ("qb", 1)))
                    k_product(0)
                    for b in range(1, DEC_BATCH):
                        k_product(b)
                        if b < 5:
                            load(b + 3)
                        if b == 2:
                            split_lo(n + 5, 2)
                    index_step(idx_k[:, :], idx_k[:, :], idx_inc[:, :])
                    split_lo(n + 6, 0)
                    split_lo(n + 7, 1)
                    for s in range(QT_N + 1):
                        for b in {0: (0, 1), 1: (2, 3), 4: (4, 5), 5: (6, 7)}.get(s, ()):
                            load(DEC_BATCH + b)
                        output_rms(l, it, s)
                    for n_ in range(2 * DEC_BATCH - 4, 2 * DEC_BATCH):
                        page_landed(pool, it, n_)
                    index_step(idx_v[:, :], idx_v[:, :], idx_inc[:, :])
                    assert steps == IDX_STEPS
                norm(l * 2 + 1, l * T_LAYER + T0_NORM2)
                f0 = l * U_LAYER + U_FFN0
                split_lo(f0 + 2, 2)
                with pool.Fori(0, FC - 1) as i:
                    split_lo(f0 + i * 3 + 3, 0)
                    split_lo(f0 + i * 3 + 4, 1)
                    split_lo(f0 + i * 3 + 5, 2)
            pool.wait_ge(t_free, DEPTH * T_LAYER + 2)
            pool.tensor_tensor(rs[:, :], rs[:, :], neghalf.broadcast_to([P, QT_N + 1]), ALU.pow).then_inc(norm_rs, 1)
            pool.wait_ge(pool_copy, 16 * DEPTH)

        @block.scalar
        def _(act):
            def split_hi(l, idx, off, per, last_use):
                w_landed(act, l, idx, off, per)
                full(act, last_use)
                act.activation(w_hi[:, off % SLOTS, :], w_raw[:, off % SLOTS, :], ACT.Copy).then_inc(w_hi_done, 1)

            def norm(ni, half, first_use, t_use, v_stored):
                def squares(i):
                    for j in range(PAIRS):
                        released(act, use(half, first_use + i * PAIRS + j))
                        if i == 2 and j == 2:
                            act.wait_ge(v_out_s, v_stored)
                        act.activation(squares_of(i, j), resid[:, 2 * j:2 * j + 2, tile_of(i)], ACT.Square
                                       ).then_inc(sq_done, 1)

                def sums(i):
                    act.wait_ge(t_full, t_use + i + 1)
                    act.wait_ge(norm_diag, ni * 2 * NT)
                    at, rows = i * len(PARTS), PARTS[-1][1]
                    act.activation(rs[:, at:at + 2], t_bank[:, 0:2], ACT.Identity, bias=c_("eps_d")
                                   ).then_inc(act_step, 1)
                    act.activation(rs[0:rows, at + 2:at + 3], t_bank[0:rows, 2:3], ACT.Identity,
                                   bias=c_("eps_d", slice(0, rows))).then_inc(t_free, 1)

                def high(i, k):
                    act.wait_ge(y_done, (ni * NT + i) * KC + k + 1)
                    act.activation(act_hi[:, k, tile_of(i)], scaled(i * KC + k), ACT.Copy).then_inc(hi_done, 1)

                squares(0)
                squares(1)
                sums(0)
                squares(2)
                sums(1)
                for k in range(KC // 2):
                    high(0, k)
                sums(2)
                for n in range(KC // 2, NT * KC):
                    high(n // KC, n % KC)

            act.wait_ge(lam_sum, 1)
            act.activation(lam[:, 4:8], lam[:, 0:4], ACT.Exp).then_inc(lam_exp, 1)

            released(act, use(0, QT_N))
            released(act, use(0, QT_N + 1))
            with act.Fori(0, DEPTH) as l:
                split_hi(l, 0, 0, 0, (0, l * (G_LAYER // 2)))
                split_hi(l, 0, 1, 0, (1, l * (G_LAYER // 2)))
                norm(l * 2, G_SETUP // 2 + l * (G_LAYER // 2), -TILE_USES, l * T_LAYER, l * (16 * N_HEADS))

                with act.Fori(0, N_HEADS) as h:
                    it = l * N_HEADS + h
                    ug = lambda name: use_head(l, h, name)
                    ta = lambda name: t_head(l, h, name)

                    def hi(off, last_use):
                        split_hi(l, h, off, 2, last_use)

                    hi(2, use(G_SETUP // 2 + l * (G_LAYER // 2) + h * (G_HEAD // 2), -1))
                    full(act, ug(("u",)))
                    act.wait_ge(t_full, ta("state") + 1)
                    act.activation(u_hist[:, :, 0:POOL_HIST],
                                   t_bank[:, 0:120].rearrange("p (b j) -> p b j", b=8), ACT.Copy).then_inc(t_free, 1)
                    g = grp(ug(("u",))[0])
                    act.activation(ue[:, 15:15 + 2 * TW].rearrange("p (a b) -> p a b", a=2), g[:, 0:2, 0:TW], ACT.Copy
                                   ).then_inc(act_step, 1)
                    act.activation(ue[:, 15 + 2 * TW:15 + SEQ], g[:, 2, 0:TW - 8], ACT.Copy).then_inc(act_step, 1)
                    act.activation(u_hist[:, :, POOL_HIST], g[:, 2, TW - 8:TW], ACT.Copy
                                   ).then_inc(g_free[ug(("u",))[0]], 1)
                    hi(3, ug(("u",)))

                    def raw(name, dst):
                        u = ug(name)
                        full(act, u)
                        act.activation(tiles(dst[:, :]), grp3(u[0]), ACT.Copy).then_inc(g_free[u[0]], 1)

                    raw(("q",), qT)
                    act.wait_ge(t_full, ta("uout") + 1)
                    act.wait_ge(u_out_s, it * 32)
                    act.activation(u_out[:, :], t_bank[0:POOL_HIST, 0:P], ACT.Copy).then_inc(act_step, 1)
                    act.activation(us_out[:, :], t_bank[0:8, P:2 * P], ACT.Copy).then_inc(t_free, 1)
                    act.wait_ge(t_free, ta("uout") + 2)
                    act.dma_start(pool_new_prompt[l, 0, :, bass.ds(h * P, P)], u_out[:, :]).then_inc(u_out_s, 16)
                    act.dma_start(pool_new_sample[l, :, POOL_HIST - 1, bass.ds(h * P, P)], us_out[:, :]
                                  ).then_inc(u_out_s, 16)
                    hi(4, ug(("q",)))
                    raw(("k",), kT)
                    for n in range(2):
                        full(act, ug(("qb", n)))
                        act.activation(bq[:, n * 512:(n + 1) * 512], grp(ug(("qb", n))[0])[:, 0, :], ACT.Copy
                                       ).then_inc(g_free[ug(("qb", n))[0]], 1)
                    hi(5, ug(("k",)))
                    full(act, ug(("y",)))
                    act.activation(tiles(mix_hi[:, :]), grp3(ug(("y",))[0]), ACT.Copy,
                                   scale=p_at("pool_scale", l, h)).then_inc(y_hi_done, 1)
                    full(act, ug(("v",)))
                    act.wait_ge(roped, it * 2 + 2)
                    act.activation(rot[:, T:T + 8], grp(ug(("v",))[0])[:, NT - 1, TW - 8:TW], ACT.Copy
                                   ).then_inc(act_step, 1)
                    act.activation(tiles(v_T), grp3(ug(("v",))[0]), ACT.Copy).then_inc(g_free[ug(("v",))[0]], 1)
                    act.wait_ge(v_out_s, it * 16)
                    for r in range(2):
                        act.wait_ge(t_full, ta(("k", r)) + 1)
                        act.activation(k_tok[:, 4 * r:4 * r + 4, :], t_bank.rearrange("p (a b) -> p a b", a=4), ACT.Copy
                                       ).then_inc(t_free, 1)
                    act.wait_ge(t_free, ta(("k", 1)) + 2)
                    act.dma_start(k_new_prompt[l, 0, :, :, h, :].rearrange("t p d -> p t d"), k_tok[:, :, :]
                                  ).then_inc(k_out_s, 16)
                    act.wait_ge(t_full, ta("small") + 1)
                    act.wait_ge(small_out, it * 32)
                    act.activation(ks_out[:, :], t_bank[0:8, 0:P], ACT.Copy).then_inc(act_step, 1)
                    act.activation(v_dup[:, :], t_bank[0:16, P:2 * P], ACT.Copy).then_inc(t_free, 1)
                    act.wait_ge(t_free, ta("small") + 2)
                    act.dma_start(k_new_sample[l, :, 0, h, :], ks_out[:, :]).then_inc(small_out, 16)
                    act.dma_start(v_new_sample[l, :, 0, h, :], v_dup[0:8, :]).then_inc(small_out, 16)
                    hi(6, ug(("v",)))
                    act.wait_ge(k_out_s, it * 16 + 16)
                    for r in range(2):
                        act.wait_ge(t_full, ta(("v", r)) + 1)
                        act.activation(v_tok[:, 4 * r:4 * r + 4, :], t_bank.rearrange("p (a b) -> p a b", a=4), ACT.Copy
                                       ).then_inc(t_free, 1)
                    act.wait_ge(t_free, ta(("v", 1)) + 2)
                    act.dma_start(v_new_prompt[l, 0, :, :, h, :].rearrange("t p d -> p t d"), v_tok[:, :, :]
                                  ).then_inc(v_out_s, 16)
                    hi(7, ug(("wg", KC - 1)))

                    def exps(s):
                        width = (ORDER[s] + 1) * P
                        for c in range(2):
                            act.wait_ge(att_bias, it * 2 * QT_N + 2 * s + c + 1)
                            p = ug(("s", s, c))[0]
                            src = bank[:, 3 * p:3 * p + 2, :].rearrange("p a b -> p (a b)")[:, 0:width]
                            act.activation(probs[s % 2][:, c, 0:width], src, ACT.Exp,
                                           bias=stat[:, s % 2, 2 + c:3 + c], scale=HEAD_DIM ** -0.5,
                                           accum_out=stat[:, s % 2, 4 + c:5 + c]).then_inc(g_free[p], 1)

                    def squares(s):
                        rows = out_rows(s)[1]
                        act.wait_ge(o_full, it * O_HEAD + s + 1)
                        src = s_bank if s == SAMPLES else o_bank
                        if s != SAMPLES:
                            act.wait_ge(inv_done, it * QT_N + min(s, QT_N - 1) + 1)
                        act.activation(junk[0:rows, s % 2, :], src[0:rows, 0:P], ACT.Square, scale=inv_sum(s),
                                       accum_out=stat[0:rows, s % 2, 6:7]).then_inc(att_sq, 1)

                    def mix(s):
                        at, n = out_rows(s)
                        act.wait_ge(t_full, ta(("o", s)) + 1)
                        act.activation(mix_hi[:, at:at + n], t_bank[:, 0:n], ACT.Copy, scale=sub_gain
                                       ).then_inc(mix_hi_done, 1)

                    exps(0)
                    for s in range(QT_N):
                        if s >= 2:
                            mix(s - 2)
                        if s >= 1:
                            squares(s - 1)
                        for r, blocks in enumerate(rounds(ORDER[s])):
                            if r == 0:
                                act.wait_ge(p_full, it * QT_N + s + 1)
                                act.activation(a_T[:, 0, 0:P * len(blocks)], p_bank[:, 0:P * len(blocks)], ACT.Copy
                                               ).then_inc(p_free, 1)
                            else:
                                act.wait_ge(t_full, ta(("p", s)) + 1)
                                act.activation(a_T[:, 1, 0:P * len(blocks)], t_bank[:, 0:P * len(blocks)], ACT.Copy
                                               ).then_inc(t_free, 1)
                        if s + 1 < QT_N:
                            exps(s + 1)
                        if s == SOFTMAX_STEP:
                            u = ug(("soft",))
                            full(act, u)
                            p = u[0]
                            act.activation(soft[:, 0:PAST_LEN],
                                           bank[0:16, 3 * p:3 * p + 2, :].rearrange("p a b -> p (a b)"), ACT.Copy
                                           ).then_inc(act_step, 1)
                            act.activation(soft[:, PAST_LEN:PAST_LEN + 1], bank[0:16, 3 * p + 2, 0:1], ACT.Copy
                                           ).then_inc(g_free[p], 1)
                        if s == SOFTMAX_STEP + 1:
                            act.wait_ge(soft_bias, it + 1)
                            act.activation(soft[:, 0:PAST_LEN + 1], soft[:, 0:PAST_LEN + 1], ACT.Exp, bias=soft_nb,
                                           scale=HEAD_DIM ** -0.5, accum_out=soft_l).then_inc(soft_exp, 1)
                    squares(QT_N - 1)
                    mix(QT_N - 2)
                    squares(QT_N)
                    mix(QT_N - 1)
                    mix(QT_N)

                norm(l * 2 + 1, G_SETUP // 2 + l * (G_LAYER // 2), G0_A0 - TILE_USES, l * T_LAYER + T0_NORM2,
                     l * (16 * N_HEADS) + 16 * N_HEADS)

                def evacuate_a(c, u):
                    full(act, u)
                    act.wait_ge(t_full, t_ffn(l, c, 0) + 1)
                    act.wait_ge(conv_done, l * FC + c)
                    rows = ext[:, 1026:1050].rearrange("p (b j) -> p b j", b=8)
                    act.activation(rows[:, :, 0:2], t_bank[:, 0:16].rearrange("p (b j) -> p b j", b=8), ACT.Copy
                                   ).then_inc(t_free, 1)
                    g = grp(u[0])
                    act.activation(ext[:, 2:2 + 2 * TW].rearrange("p (a b) -> p a b", a=2), g[:, 0:2, 0:TW], ACT.Copy
                                   ).then_inc(act_step, 1)
                    act.activation(ext[:, 2 + 2 * TW:2 + SEQ], g[:, 2, 0:TW - 8], ACT.Copy).then_inc(act_step, 1)
                    act.activation(rows[:, :, 2], g[:, 2, TW - 8:TW], ACT.Copy).then_inc(g_free[u[0]], 1)
                    released(act, u)
                    act.activation(conv_c[:, :], ext[:, 2:1050], ACT.Identity, bias=p_at("conv_b", l, c),
                                   scale=p_at("conv_w", l, c + 2 * FC)).then_inc(taps0, 1)

                def silu(c):
                    act.wait_ge(conv_done, l * FC + c + 1)
                    act.wait_ge(g_lo_done, l * FC + c)
                    act.activation(gate[:, 0:SEQ], conv_c[:, 0:SEQ], ACT.Silu).then_inc(act_step, 1)
                    act.activation(gate[:, SEQ:T], conv_c[:, 1026:1048:3], ACT.Silu).then_inc(silu_done, 1)

                def store_conv(c):
                    act.wait_ge(t_full, t_ffn(l, c, 1) + 1)
                    act.wait_ge(conv_out_s, (l * FC + c) * 48)
                    act.activation(conv_out[:, :], t_bank[0:26, 0:P], ACT.Copy).then_inc(t_free, 1)
                    act.wait_ge(t_free, t_ffn(l, c, 1) + 2)
                    act.dma_start(conv_new_prompt[l, 0, :, sl(c * P, P)], conv_out[0:2, :]
                                  ).then_inc(conv_out_s, 16)
                    for j in range(2):
                        act.dma_start(conv_new_sample[l, :, j, sl(c * P, P)], rows_out[99 + j:122:3, :]
                                      ).then_inc(conv_out_s, 16)

                def gate_hi(c, u):
                    released(act, u)
                    act.activation(mix_hi[:, :], gate[:, :], ACT.Copy).then_inc(g_hi_done, 1)

                split_hi(l, 0, U_FFN0 + 2, 0, use_layer(l, G0_A0 - 1))
                evacuate_a(0, use_layer(l, G0_A0))
                silu(0)
                with act.Fori(0, FC - 1) as i:
                    split_hi(l, i, U_FFN0 + 3, 1, use_ffn(l, i, -1))
                    store_conv(i)
                    gate_hi(i, use_ffn(l, i, 0))
                    split_hi(l, i, U_FFN0 + 4, 1, use_ffn(l, i, 0))
                    evacuate_a(i + 1, use_ffn(l, i, 1))
                    split_hi(l, i, U_FFN0 + 5, 1, use_ffn(l, i, 1))
                    silu(i + 1)
                store_conv(FC - 1)
                gate_hi(FC - 1, use_ffn(l, FC - 1, 0))

            last = DEPTH * (G_LAYER // 2)
            released(act, (1, G_SETUP // 2 - 1 + last))
            act.activation(rot[:, 0:T], resid[:, 0, :], ACT.Square).then_inc(sq_done, 1)
            for k in range(1, KC):
                if k >= 3:
                    act.wait_ge(acc_done, k - 2)
                act.activation(sq_ring[k % 2], resid[:, k, :], ACT.Square).then_inc(sq_done, 1)
            act.wait_ge(t_full, DEPTH * T_LAYER + 1)
            act.wait_ge(norm_diag, 2 * DEPTH * 2 * NT)
            act.activation(rs[:, 0:QT_N], t_bank[:, 0:QT_N], ACT.Copy).then_inc(act_step, 1)
            act.activation(rs[0:8, QT_N:QT_N + 1], t_bank[0:8, QT_N:QT_N + 1], ACT.Copy).then_inc(t_free, 1)
            act.wait_ge(norm_rs, 2 * DEPTH * NT + 1)
            for t in range(1, QT_N + 1, 2):
                u = use(G_SETUP // 2 + last, t)
                full(act, u)
                src = bank[:, 3 * u[0]:3 * u[0] + 2, :].rearrange("p a b -> p (a b)")
                act.activation(x_buf(t), src, ACT.Copy, scale=rs[:, t:t + 1]).then_inc(g_free[u[0]], 1)
            act.wait_ge(k_out_s, 16 * DEPTH * N_HEADS)
            act.wait_ge(v_out_s, 16 * DEPTH * N_HEADS)
            act.wait_ge(small_out, 32 * DEPTH * N_HEADS)
            act.wait_ge(u_out_s, 32 * DEPTH * N_HEADS)
            act.wait_ge(conv_out_s, 48 * DEPTH * FC)

        @block.tensor
        def _(pe):
            def wait_free(u):
                pe.wait_ge(g_free[u[0]], u[1] + 1)

            def wait_t(seq):
                pe.wait_ge(t_free, seq + 1)

            def unit_ready(n):
                pe.wait_ge(w_lo_done, n + (1 + W_CREDIT))

            PRODUCTS = ((w_hi, act_hi), (w_lo, act_hi), (w_hi, act_lo))

            def up_unit(n, slot, u):
                unit_ready(n)
                wait_free(u)
                g = grp(u[0])
                for k in range(KC):
                    for n_, (w, x) in enumerate(PRODUCTS):
                        for t in range(NT):
                            ins = pe.matmul(g[:, t, 0:TW], w[:, slot, k * P:(k + 1) * P],
                                            x[:, k, t * TW:(t + 1) * TW], start=(k == 0 and n_ == 0),
                                            stop=(k == KC - 1 and n_ == 2))
                ins.then_inc(g_full[u[0]], 1)

            def up_unit_by_tile(n, slot, u, ni):
                unit_ready(n)
                wait_free(u)
                g = grp(u[0])
                for i in range(NT):
                    for k in range(KC):
                        at = i * KC + k
                        for n_, (w, x) in enumerate(PRODUCTS):
                            if n_ == 0:
                                pe.wait_ge(hi_done, ni * (NT * KC) + at + 1)
                            if n_ == 2:
                                low_done(pe, ni, at)
                            ins = pe.matmul(g[:, T_ORDER[i], 0:TW], w[:, slot, k * P:(k + 1) * P],
                                            x[:, k, tile_of(i)], start=(k == 0 and n_ == 0),
                                            stop=(k == KC - 1 and n_ == 2))
                ins.then_inc(g_full[u[0]], 1)

            def down_part(slot, m, u):
                wait_free(u)
                g = grp(u[0])
                for n_, (w, x) in enumerate(((w_hi, mix_hi), (w_hi, mix_lo), (w_lo, mix_hi))):
                    for t in range(NT):
                        ins = pe.matmul(g[:, t, 0:TW], w[:, slot, m * P:(m + 1) * P], x[:, t * TW:(t + 1) * TW],
                                        start=(n_ == 0), stop=(n_ == 2))
                ins.then_inc(g_full[u[0]], 1)

            def down_unit(n, slot, uses):
                unit_ready(n)
                for m in range(KC):
                    down_part(slot, m, uses(m))

            def down_tile(slot, i, uses):
                for j in range(PAIRS):
                    u = uses(i * PAIRS + j)
                    wait_free(u)
                    for a in range(2):
                        m = 2 * j + a
                        for n_, (w, x) in enumerate(((w_hi, mix_hi), (w_hi, mix_lo), (w_lo, mix_hi))):
                            ins = pe.matmul(grp(u[0])[:, a, 0:TW], w[:, slot, m * P:(m + 1) * P], x[:, tile_of(i)],
                                            start=(n_ == 0), stop=(n_ == 2))
                    ins.then_inc(g_full[u[0]], 1)

            pe.wait_ge(table_in, 16)
            for t in range(QT_N + 1):
                u = use(0, t)
                wait_free(u)
                pe.wait_ge(x_in[t], 16)
                rows = P if t < QT_N else 8
                g = bank[:, 3 * u[0]:3 * u[0] + 2, :].rearrange("p a b -> p (a b)")
                for k in range(KC):
                    ins = pe.transpose(g[:, k * P:k * P + rows], x_buf(t)[0:rows, k * P:(k + 1) * P],
                                       ident[0:rows, 0:rows])
                ins.then_inc(g_full[u[0]], 1)
            u = use(0, QT_N + 1)
            wait_free(u)
            pe.wait_ge(params_in, 16 * len(PAR) * DEPTH)
            for l in range(DEPTH):
                ins = pe.transpose(bank[:, 3 * u[0], l * P:l * P + PAR_W], k_tok[0:PAR_W, l, :],
                                   ident[0:PAR_W, 0:PAR_W])
            ins.then_inc(g_full[u[0]], 1)

            def norm(ni, t_use):
                def sums(i):
                    wait_t(t_use + i)
                    pe.wait_ge(sum_done, ni * (2 * NT) + 2 * i + 2)
                    parts = [squares_of(i, j)[:, a, :] for j in (0, 2) for a in range(2)]
                    for n, (at, rows) in enumerate(PARTS):
                        for m, sq in enumerate(parts):
                            ins = pe.matmul(t_bank[0:rows, n:n + 1], sq[:, at:at + rows], ones[:, 0:1],
                                            start=(m == 0), stop=(m == len(parts) - 1))
                    ins.then_inc(t_full, 1)

                def spread_rms(i):
                    pe.wait_ge(norm_diag, ni * (2 * NT) + 2 * i + 2)
                    pe.wait_ge(bc_free, ni * NT + i)
                    pe.matmul(o_bank[:, 0:TW], ones, bq[:, tile_of(i)], start=True, stop=True).then_inc(bc_full, 1)

                sums(0)
                sums(1)
                spread_rms(0)
                sums(2)
                spread_rms(1)
                spread_rms(2)

            with pe.Fori(0, DEPTH) as l:
                norm(l * 2, l * T_LAYER)
                with pe.Fori(0, N_HEADS) as h:
                    it = l * N_HEADS + h
                    n0 = l * U_LAYER + h * U_HEAD
                    ug = lambda name: use_head(l, h, name)
                    ta = lambda name: t_head(l, h, name)
                    pe.wait_ge(sp_in, (it + 1) * 16)
                    wait_t(ta("state"))
                    pe.transpose(t_bank[:, 0:120], state_in[:, :], ident[0:120, 0:120]).then_inc(t_full, 1)
                    up_unit_by_tile(n0, 0, ug(("u",)), l * 2)
                    up_unit(n0 + 1, 1, ug(("q",)))
                    released(pe, ug(("u",)))
                    wait_t(ta("uout"))
                    pe.transpose(t_bank[0:POOL_HIST, 0:P], ue[:, SEQ:SEQ + POOL_HIST], ident)
                    pe.transpose(t_bank[0:8, P:2 * P], u_hist[:, :, POOL_HIST], ident).then_inc(t_full, 1)
                    up_unit(n0 + 2, 2, ug(("k",)))
                    pe.wait_ge(diag_done, it + 1)
                    for n in range(2):
                        u = ug(("qb", n))
                        wait_free(u)
                        pe.matmul(grp(u[0])[:, 0, :], ones, bq[:, n * 512:(n + 1) * 512], start=True, stop=True
                                  ).then_inc(g_full[u[0]], 1)
                    u = ug(("y",))
                    wait_free(u)
                    pe.wait_ge(pool_d, it + 1)
                    pe.wait_ge(pw_in, (it + 1) * 16)
                    for t in range(NT):
                        ins = pe.matmul(grp(u[0])[:, t, 0:TW], pw[:, :], pool_dd[:, t * TW:(t + 1) * TW],
                                        start=True, stop=True)
                    ins.then_inc(g_full[u[0]], 1)
                    up_unit(n0 + 3, 0, ug(("v",)))

                    def turn(name, r, src):
                        wait_t(ta((name, r)))
                        for a in range(4):
                            i = 4 * r + a
                            ins = pe.transpose(t_bank[:, a * P:(a + 1) * P], src[:, i * P:(i + 1) * P], ident)
                        ins.then_inc(t_full, 1)

                    pe.wait_ge(roped, it * 2 + 2)
                    turn("k", 0, kT)
                    released(pe, ug(("y",)))
                    unit_ready(n0 + 4)
                    for m in range(KC):
                        down_part(1, m, ug(("wg", m)))
                        if m == 0:
                            turn("k", 1, kT)
                        if m == 1:
                            wait_t(ta("small"))
                            released(pe, ug(("v",)))
                            pe.transpose(t_bank[0:8, 0:P], kT[:, SEQ:T], ident)
                            pe.transpose(t_bank[0:16, P:2 * P], rot[:, SEQ:T + 8], ident).then_inc(t_full, 1)

                    def scores(s):
                        i = ORDER[s]
                        width = (i + 1) * P
                        for c in range(2):
                            u = ug(("s", s, c))
                            wait_free(u)
                            rows = slice(c * HEAD_DIM, (c + 1) * HEAD_DIM)
                            for n, at in enumerate(range(0, i * P, 512)):
                                w = min(512, i * P - at)
                                pe.matmul(bank[:, 3 * u[0] + n, 0:w], qT[rows, i * P:(i + 1) * P],
                                          kT[rows, at:at + w], start=True, stop=True)
                            last = bank[:, 3 * u[0] + i // 4, (i % 4) * P:(i % 4 + 1) * P]
                            pe.matmul(last, qT[rows, i * P:(i + 1) * P], kT[rows, i * P:(i + 1) * P],
                                      start=True, stop=False)
                            ins = pe.matmul(last, mask[:, 0, :], mask[:, 1, :], start=False, stop=True)
                            ins.then_inc(g_full[u[0]], 1)

                    def values(b):
                        page_landed(pe, it, DEC_BATCH + b)
                        for t in range(RUN):
                            ins = pe.matmul(s_bank[0:8, 0:P], spread[:, t, b, :], page[:, b % 4, t, :],
                                            start=(b == 0 and t == 0), stop=False)
                        ins.then_inc(v_used, 1)

                    def weigh(s):
                        i = ORDER[s]
                        rr = rounds(i)
                        pe.wait_ge(att_a, it * QT_N + s + 1)
                        for r, blocks in enumerate(rr):
                            to = (p_bank, t_bank)[r]
                            if r == 0:
                                pe.wait_ge(p_free, it * QT_N + s)
                            else:
                                wait_t(ta(("p", s)))
                            for n, b in enumerate(blocks):
                                ins = pe.transpose(to[:, n * P:(n + 1) * P], probs[s % 2][:, 0, b * P:(b + 1) * P],
                                                   ident)
                            ins.then_inc((p_full, t_full)[r], 1)
                        if s == min(VALUES_AT):
                            pe.wait_ge(spread_done, it + 1)
                        for b in VALUES_AT.get(s, ()):
                            values(b)
                        if s == max(VALUES_AT):
                            pe.matmul(s_bank[0:8, 0:P], diag8, v_dup[:, :], start=False, stop=True
                                      ).then_inc(o_full, 1)
                        pe.wait_ge(o_free, it * O_HEAD + s + 1)
                        if s == 0:
                            pe.wait_ge(t_free, ta(("v", 1)) + 2)
                        for r, blocks in enumerate(rr):
                            if r == 0:
                                pe.wait_ge(p_free, it * QT_N + s + 1)
                            else:
                                pe.wait_ge(t_free, ta(("p", s)) + 2)
                            for n, b in enumerate(blocks):
                                ins = pe.matmul(o_bank[:, 0:P], a_T[:, r, n * P:(n + 1) * P],
                                                v_tok[:, b, :], start=(b == 0), stop=(b == i))
                        ins.then_inc(o_full, 1)

                    def turn_out(s):
                        rows = out_rows(s)[1]
                        pe.wait_ge(o_free, it * O_HEAD + s + 2)
                        wait_t(ta(("o", s)))
                        pe.matmul(t_bank[:, 0:rows], o_norm[0:rows, s % 2, :], ident[0:rows, 0:rows], start=True,
                                  stop=True).then_inc(t_full, 1)

                    scores(0)
                    turn("v", 0, v_T)
                    turn("v", 1, v_T)
                    for s in range(QT_N):
                        if s + 1 < QT_N:
                            scores(s + 1)
                        weigh(s)
                        if s >= 1:
                            turn_out(s - 1)
                        if s == WEIGHTS_STEP:
                            pe.wait_ge(soft_sel, it + 1)
                            for j in range(N_PAGES):
                                ins = pe.matmul(s_bank[:, j * 8:j * 8 + 8], soft[:, j * P:(j + 1) * P], sel8,
                                                start=True, stop=True)
                            ins.then_inc(weights_full, 1)
                        if s == SOFTMAX_STEP:
                            u = ug(("soft",))
                            wait_free(u)
                            pe.wait_ge(k_red, (it + 1) * DEC_BATCH)
                            for j in range(N_PAGES):
                                pe.transpose(bank[0:16, 3 * u[0] + j // 4, (j % 4) * P:(j % 4 + 1) * P],
                                             s_score[:, :, :, j], ident)
                            pe.matmul(bank[0:16, 3 * u[0] + 2, 0:1], comp8, ones[:, 0:1], start=True, stop=True
                                      ).then_inc(g_full[u[0]], 1)
                    turn_out(QT_N - 1)
                    turn_out(QT_N)
                    assert ORDER[-1] * P // TW == ((ORDER[-1] + 1) * P - 1) // TW == T_ORDER[-1]
                    unit_ready(n0 + 5)
                    pe.wait_ge(t_free, ta(("o", QT_N - 1)) + 2)
                    for i in range(NT):
                        if i == NT - 1:
                            pe.wait_ge(t_free, ta(("o", QT_N)) + 2)
                        down_tile(2, i, lambda j: ug(("wh", j)))

                norm(l * 2 + 1, l * T_LAYER + T0_NORM2)
                f0 = l * U_LAYER + U_FFN0

                def state_rows(c):
                    pe.wait_ge(sc_in, (l * FC + c + 1) * 16)
                    wait_t(t_ffn(l, c, 0))
                    pe.matmul(t_bank[:, 0:16], state_in[0:16, :], ident[0:16, 0:16], start=True, stop=True
                              ).then_inc(t_full, 1)

                def new_rows(c):
                    pe.wait_ge(taps0, l * FC + c + 1)
                    wait_t(t_ffn(l, c, 1))
                    pe.transpose(t_bank[0:26, 0:P], ext_tail, ident).then_inc(t_full, 1)

                def down(c, n, slot, first_use):
                    pe.wait_ge(g_lo_done, l * FC + c + 1)
                    down_unit(n, slot, lambda m: use_ffn(l, c, first_use + m))

                state_rows(0)
                up_unit_by_tile(f0, 0, use_layer(l, G0_A0), l * 2 + 1)
                with pe.Fori(0, FC - 1) as i:
                    up_unit(f0 + i * 3 + 1, 1, use_ffn(l, i, 0))
                    new_rows(i)
                    up_unit(f0 + i * 3 + 2, 2, use_ffn(l, i, 1))
                    state_rows(i + 1)
                    down(i, f0 + i * 3 + 3, 0, 2)
                up_unit(f0 + 3 * FC - 2, 1, use_ffn(l, FC - 1, 0))
                new_rows(FC - 1)
                pe.wait_ge(g_lo_done, (l + 1) * FC)
                unit_ready(f0 + 3 * FC - 1)
                for i in range(NT):
                    down_tile(2, i, lambda j: use_ffn(l, FC - 1, 1 + j))

            wait_t(DEPTH * T_LAYER)
            pe.wait_ge(acc_done, KC - 1)
            for t in range(QT_N + 1):
                rows = P if t < QT_N else 8
                ins = pe.matmul(t_bank[0:rows, t:t + 1], rot[:, t * P:t * P + rows], ones[:, 0:1], start=True,
                                stop=True)
            ins.then_inc(t_full, 1)
            pe.wait_ge(y_done, 2 * DEPTH * NT * KC + KC)
            for t in range(QT_N + 1):
                u = use(G_SETUP // 2 + DEPTH * (G_LAYER // 2), t)
                wait_free(u)
                rows = P if t < QT_N else 8
                g = bank[:, 3 * u[0]:3 * u[0] + 2, :].rearrange("p a b -> p (a b)")
                for k in range(KC):
                    ins = pe.transpose(g[0:rows, k * P:(k + 1) * P], resid[:, k, t * P:t * P + rows], ident)
                ins.then_inc(g_full[u[0]], 1)

        @block.vector
        def _(dve):
            class Chain:

                def __init__(self, base):
                    self.base, self.n = base, 0

                def __call__(self, ins):
                    self.n += 1
                    ins.then_inc(dve_step, 1)
                    dve.wait_ge(dve_step, self.base + self.n)

            STEP_SETUP, STEP_HEAD, STEP_FFN = 26, 60, 1
            STEP_LAYER = STEP_HEAD * N_HEADS + 1 + STEP_FFN * FC

            for p in range(2):
                dve.memset(small[:, p:p + 1], 0.0).then_inc(g_free[p], 1)
            dve.memset(small[:, 2:3], 0.0).then_inc(t_free, 1)
            dve.memset(small[:, 3:4], 0.0).then_inc(o_free, 1)
            dve.memset(small[:, 5:6], 0.0).then_inc(v_used, V_CREDIT)
            dve.memset(small[:, 6:7], 0.0).then_inc(y_hi_done, 1)
            for t in range(QT_N + 1):
                u = use(0, t)
                full(dve, u)
                rows = P if t < QT_N else 8
                g = bank[:, 3 * u[0]:3 * u[0] + 2, :].rearrange("p a b -> p (a b)").rearrange("p (k r) -> p k r", k=KC)
                dve.tensor_copy(resid[:, :, t * P:t * P + rows], g[:, :, 0:rows]).then_inc(g_free[u[0]], 1)
            step = Chain(0)
            dve.wait_ge(table_in, 16)
            step(dve.memset(rs[:, :], 1.0))
            step(dve.tensor_copy(mask[:, 0, :], ident))
            step(dve.tensor_copy(mask[:, 1, :], c_("causal")))
            dve.wait_ge(pages_in, 16 * N_PAGES)
            page_f, idx_f = small[:, 8:16], small[:, 16:24]
            step(dve.tensor_copy(page_f, pages[:, :]))
            step(dve.tensor_scalar(idx_f, page_f, float(GROUPS), None, ALU.mult))
            step(dve.tensor_scalar(idx_f, idx_f, c_("group"), None, ALU.add))
            step(dve.tensor_copy(idx_k[:, :], idx_f))
            step(dve.tensor_copy(idx_v[:, :], idx_f))
            step(dve.memset(page_f, float(GROUPS * N_POOL)))
            dve.tensor_copy(idx_inc[:, :], page_f).then_inc(idx_ready, 1)
            dve.wait_ge(lam_in_s, 64)
            for n in range(2):
                step(dve.tensor_tensor(lam_in[:, 2 * n, :], lam_in[:, 2 * n, :], lam_in[:, 2 * n + 1, :], ALU.mult))
            step(dve.tensor_reduce(lam[:, 0:2], lam_in[:, 0, :].rearrange("p (l d) -> p l d", l=DEPTH), AX_X, ALU.add))
            dve.tensor_reduce(lam[:, 2:4], lam_in[:, 2, :].rearrange("p (l d) -> p l d", l=DEPTH), AX_X, ALU.add
                              ).then_inc(lam_sum, 1)
            dve.wait_ge(lam_exp, 1)
            step(dve.tensor_tensor(lam[:, 0:2], lam[:, 4:6], lam[:, 6:8], ALU.subtract))
            step(dve.tensor_tensor(lam[:, 0:2], lam[:, 0:2], c_("lam_init"), ALU.add))
            for l in range(DEPTH):
                step(dve.scalar_tensor_tensor(out=lam[0:16, 8 + l:9 + l], in0=c_("sign", slice(0, 16))[:, 1:2],
                                              scalar=lam[0:16, l:l + 1], in1=c_("sign", slice(0, 16))[:, 0:1],
                                              op0=ALU.mult, op1=ALU.add))
            u = use(0, QT_N + 1)
            full(dve, u)
            for l in range(DEPTH):
                step(dve.tensor_copy(par[:, l, 0:PAR_W], bank[:, 3 * u[0], l * P:l * P + PAR_W]))
            for l in range(DEPTH):
                a, _ = PAR["norm1_g"]
                step(dve.tensor_scalar(par[:, l, a:a + 2 * KC], par[:, l, a:a + 2 * KC], math.sqrt(D_MODEL), None,
                                       ALU.mult))
                a, _ = PAR["final_g"]
                step(dve.tensor_scalar(par[:, l, a:a + KC], par[:, l, a:a + KC], math.sqrt(D_MODEL), None, ALU.mult))
                a, _ = PAR["subln_g"]
                one = CON["one_minus"][0]
                ins = dve.tensor_scalar(par[:, l, a:a + 1], par[:, l, a:a + 1], con[:, one + l:one + l + 1],
                                        math.sqrt(VDIM), ALU.mult, ALU.mult)
                if l == 0:
                    step(ins)
            ins.then_inc(g_free[u[0]], 1)
            released(dve, u)
            assert step.n <= STEP_SETUP, step.n
            base0 = step.n

            def norm(ni, gains):
                def diagonal(i):
                    dve.wait_ge(norm_rs, ni * NT + i + 1)
                    at, (last_at, rows) = i * len(PARTS), PARTS[-1]
                    to = bq[:, tile_of(i)]
                    dve.tensor_tensor(to[:, 0:last_at].rearrange("p (b f) -> p b f", b=2),
                                      ident[:, None, :].broadcast_to([P, 2, P]),
                                      rs[:, at:at + 2].rearrange("p (b a) -> p b a", a=1).broadcast_to([P, 2, P]),
                                      ALU.mult).then_inc(norm_diag, 1)
                    dve.tensor_scalar(to[:, last_at:TW], ident[:, 0:rows], rs[:, at + 2:at + 3], None, ALU.mult
                                      ).then_inc(norm_diag, 1)

                def take(i):
                    dve.wait_ge(bc_full, ni * NT + i + 1)
                    dve.tensor_copy(bq[:, tile_of(i)], o_bank[:, 0:TW]).then_inc(bc_free, 1)
                    dve.wait_ge(bc_free, ni * NT + i + 1)

                def low(n):
                    dve.wait_ge(hi_done, ni * (NT * KC) + n + 1)
                    at = tile_of(n // KC)
                    dve.tensor_tensor(act_lo[:, n % KC, at], scaled(n), act_hi[:, n % KC, at].bitcast(F32),
                                      ALU.subtract).then_inc(lo_dve, 1)

                def scale(ns):
                    for n in ns:
                        if n >= 6:
                            low_done(dve, ni, n - 6)
                        at = tile_of(n // KC)
                        dve.scalar_tensor_tensor(out=scaled(n), in0=resid[:, n % KC, at], scalar=gains(n % KC),
                                                 in1=bq[:, at], op0=ALU.mult, op1=ALU.mult).then_inc(y_done, 1)
                        if n > 0 and low_by_dve(n - 1):
                            low(n - 1)

                diagonal(0)
                take(0)
                scale(range(0, 4))
                diagonal(1)
                scale(range(4, KC))
                diagonal(2)
                take(1)
                scale(range(KC, KC + 4))
                take(2)
                scale(range(KC + 4, NT * KC))
                low(NT * KC - 1)

            def add_tiles(uses):
                for n in range(TILE_USES):
                    i, j = n // PAIRS, n % PAIRS
                    u = uses(n)
                    full(dve, u)
                    rows = resid[:, 2 * j:2 * j + 2, tile_of(i)]
                    dve.tensor_tensor(rows, grp3(u[0])[:, 0:2, :], rows, ALU.add).then_inc(g_free[u[0]], 1)

            def add_rows(uses, ms=range(KC)):
                for m in ms:
                    u = uses(m)
                    full(dve, u)
                    dve.tensor_tensor(tiles(resid[:, m, :]), grp3(u[0]), tiles(resid[:, m, :]), ALU.add
                                      ).then_inc(g_free[u[0]], 1)

            with dve.Fori(0, DEPTH) as l:
                norm(l * 2, lambda k: p_at("norm1_g", l, k))
                with dve.Fori(0, N_HEADS) as h:
                    it = l * N_HEADS + h
                    ug = lambda name: use_head(l, h, name)
                    ta = lambda name: t_head(l, h, name)
                    step = Chain(l * STEP_LAYER + h * STEP_HEAD + base0)
                    step(dve.tensor_copy(sub_gain, p_at("subln_g", l, 0)))
                    step(dve.tensor_scalar(neg_lam, lam[:, bass.ds(l, 1)], -1.0, None, ALU.mult))
                    released(dve, ug(("u",)))
                    step(dve.memset(ue[:, 0:POOL_HIST], 0.0))
                    src, dst = ue, pool_a
                    for k in range(4):
                        back, lo = 1 << k, (2 << k) - 1
                        step(dve.scalar_tensor_tensor(out=dst[:, lo:1167], in0=src[:, lo - back:1167 - back],
                                                      scalar=c_at("poolstep", h * 4 + k), in1=src[:, lo:1167],
                                                      op0=ALU.mult, op1=ALU.add))
                        src, dst = dst, (pool_b if k % 2 == 0 else pool_a)
                    step(dve.scalar_tensor_tensor(out=pool_dd[:, 0:SEQ], in0=pool_b[:, 15:15 + SEQ],
                                                  scalar=c_at("poolinv", h), in1=ue[:, 15:15 + SEQ],
                                                  op0=ALU.mult, op1=ALU.subtract))
                    step(dve.tensor_tensor(pool_dd[:, 0:16], pool_b[:, 15:31], c_at("poolhead", h * 16, 16), ALU.mult))
                    step(dve.tensor_tensor(pool_dd[:, 0:16], pool_dd[:, 0:16], ue[:, 15:31], ALU.subtract))
                    dve.scalar_tensor_tensor(out=pool_dd[:, SEQ:T], in0=pool_b[:, 1039 + 15:1167:16],
                                             scalar=c_at("poolinv", h), in1=ue[:, 1039 + 15:1167:16],
                                             op0=ALU.mult, op1=ALU.subtract).then_inc(pool_d, 1)

                    def rope(n, name, dst):
                        released(dve, ug(name))
                        for a in range(4):
                            to = 32 * (a ^ 1)
                            dve.tensor_copy(rot[to:to + 32, 0:T], dst[32 * a:32 * a + 32, :]).then_inc(dve_step, 1)
                        step.n += 4
                        dve.wait_ge(dve_step, step.base + step.n)
                        dve.tensor_tensor(dst[:, :], dst[:, :], c_("cos"), ALU.mult).then_inc(dve_step, 1)
                        dve.tensor_tensor(rot[:, 0:T], rot[:, 0:T], c_("sin"), ALU.mult).then_inc(dve_step, 1)
                        step.n += 2
                        dve.wait_ge(dve_step, step.base + step.n)
                        dve.tensor_tensor(dst[:, :], dst[:, :], rot[:, 0:T], ALU.add).then_inc(roped, 1)
                        dve.wait_ge(roped, it * 2 + n + 1)

                    dve.wait_ge(rope_in, 16)
                    rope(0, ("q",), qT)
                    dve.tensor_tensor(bq[:, 0:1024].rearrange("p (b f) -> p b f", b=8),
                                      ident[:, None, :].broadcast_to([P, 8, P]),
                                      qT[:, SEQ:T].rearrange("p (b a) -> p b a", a=1).broadcast_to([P, 8, P]), ALU.mult
                                      ).then_inc(diag_done, 1)
                    rope(1, ("k",), kT)
                    step(dve.tensor_tensor(qk8, qT[:, SEQ:T], kT[:, SEQ:T], ALU.mult))
                    step(dve.tensor_tensor(comp8, qk8[:, None, :].broadcast_to([P, 2, 8]),
                                           c_("compsel").rearrange("p (c a) -> p c a", a=1).broadcast_to([P, 2, 8]),
                                           ALU.mult))

                    def k_sum(b):
                        dve.wait_ge(k_mul, it * DEC_BATCH + b + 1)
                        src = page[:, b % 4, :, :].rearrange("p j (c d) -> p j c d", c=2)
                        dve.tensor_reduce(s_score[:, :, b, :].rearrange("p c j -> p j c"), src, AX_X, ALU.add
                                          ).then_inc(k_red, 1)

                    u = ug(("y",))
                    dve.wait_ge(y_hi_done, it + 2)
                    dve.scalar_tensor_tensor(out=tiles(mix_lo[:, :]), in0=grp3(u[0]), scalar=p_at("pool_scale", l, h),
                                             in1=tiles(mix_hi[:, :].bitcast(F32)), op0=ALU.mult, op1=ALU.subtract
                                             ).then_inc(g_free[u[0]], 1)
                    for b in range(3):
                        k_sum(b)
                    for m in range(KC):
                        add_rows(lambda m_: ug(("wg", m_)), (m,))
                        if m in (1, 3, 5):
                            k_sum(3 + m // 2)

                    def maxima(s):
                        width = (ORDER[s] + 1) * P
                        for c in range(2):
                            u = ug(("s", s, c))
                            full(dve, u)
                            src = bank[:, 3 * u[0]:3 * u[0] + 2, :].rearrange("p a b -> p (a b)")[:, 0:width]
                            step(dve.tensor_reduce(stat[:, s % 2, c:c + 1], src, AX_X, ALU.max))
                            dve.tensor_scalar(stat[:, s % 2, 2 + c:3 + c], stat[:, s % 2, c:c + 1],
                                              -(HEAD_DIM ** -0.5), None, ALU.mult).then_inc(att_bias, 1)

                    def combine(s):
                        width = (ORDER[s] + 1) * P
                        released(dve, ug(("s", s, 0)))
                        released(dve, ug(("s", s, 1)))
                        st = stat[:, s % 2, :]
                        step(dve.reciprocal(st[:, 5:6], st[:, 5:6]))
                        step(dve.scalar_tensor_tensor(out=st[:, 5:6], in0=st[:, 5:6], scalar=neg_lam, in1=st[:, 4:5],
                                                      op0=ALU.mult, op1=ALU.mult))
                        pr = probs[s % 2]
                        dve.scalar_tensor_tensor(out=pr[:, 0, 0:width], in0=pr[:, 1, 0:width], scalar=st[:, 5:6],
                                                 in1=pr[:, 0, 0:width], op0=ALU.mult, op1=ALU.add).then_inc(att_a, 1)
                        dve.reciprocal(st[:, 7:8], st[:, 4:5]).then_inc(inv_done, 1)

                    def normalise(s):
                        rows = out_rows(s)[1]
                        dve.wait_ge(att_rms, it * O_HEAD + s + 1)
                        ss = stat[0:rows, s % 2, 6:7]
                        src = s_bank if s == SAMPLES else o_bank
                        dve.tensor_scalar(o_norm[0:rows, s % 2, :], src[0:rows, 0:P], ss, inv_sum(s), ALU.mult, ALU.mult
                                          ).then_inc(o_free, 1)

                    def mix(s):
                        at, n = out_rows(s)
                        dve.wait_ge(mix_hi_done, it * O_HEAD + s + 1)
                        dve.scalar_tensor_tensor(out=mix_lo[:, at:at + n], in0=t_bank[:, 0:n],
                                                 scalar=sub_gain, in1=mix_hi[:, at:at + n].bitcast(F32),
                                                 op0=ALU.mult, op1=ALU.subtract).then_inc(t_free, 1)

                    maxima(0)
                    k_sum(6)
                    k_sum(7)
                    for s in range(QT_N):
                        if s >= 2:
                            mix(s - 2)
                        combine(s)
                        if s >= 1:
                            normalise(s - 1)
                        if s + 1 < QT_N:
                            maxima(s + 1)
                        if s == SOFTMAX_STEP + 1:
                            released(dve, ug(("soft",)))
                            step(dve.tensor_reduce(soft_m, soft[:, 0:PAST_LEN + 1], AX_X, ALU.max))
                            dve.tensor_scalar(soft_nb, soft_m, -(HEAD_DIM ** -0.5), None, ALU.mult
                                              ).then_inc(soft_bias, 1)
                        if s == WEIGHTS_STEP:
                            dve.wait_ge(soft_exp, it + 1)
                            step(dve.reciprocal(soft_l, soft_l))
                            step(dve.tensor_tensor(soft_cf, soft_l, lam[0:16, bass.ds(l + 8, 1)], ALU.mult))
                            step(dve.tensor_scalar(sel8, c_("rowsel", slice(0, 16)), soft_cf, None, ALU.mult))
                            dve.tensor_scalar(diag8, sel8, soft[:, PAST_LEN:PAST_LEN + 1], None, ALU.mult
                                              ).then_inc(soft_sel, 1)
                            dve.wait_ge(weights_full, it + 1)
                            w = s_bank[:, 0:64].rearrange("p (j b a) -> p j b a", j=8, a=1).broadcast_to([P, 8, 8, 8])
                            d = c_("delta").rearrange("p (o b a) -> p o b a", o=1, b=8).broadcast_to([P, 8, 8, 8])
                            dve.tensor_tensor(spread[:, :, :, :], w, d, ALU.mult).then_inc(spread_done, 1)
                    normalise(QT_N - 1)
                    mix(QT_N - 2)
                    normalise(QT_N)
                    mix(QT_N - 1)
                    mix(QT_N)
                    add_tiles(lambda j: ug(("wh", j)))
                    assert step.n == STEP_HEAD, step.n

                norm(l * 2 + 1, lambda k: p_at("norm2_g", l, k))
                fstep = l * STEP_LAYER + (N_HEADS * STEP_HEAD + 1 + base0)

                def taps(c):
                    dve.wait_ge(taps0, l * FC + c + 1)
                    dve.scalar_tensor_tensor(out=conv_c[:, :], in0=ext[:, 1:1049], scalar=p_at("conv_w", l, c + FC),
                                             in1=conv_c[:, :], op0=ALU.mult, op1=ALU.add).then_inc(dve_step, 1)
                    dve.wait_ge(dve_step, fstep + c + 1)
                    dve.scalar_tensor_tensor(out=conv_c[:, :], in0=ext[:, 0:1048], scalar=p_at("conv_w", l, c),
                                             in1=conv_c[:, :], op0=ALU.mult, op1=ALU.add).then_inc(conv_done, 1)

                def gate_b(c, u):
                    full(dve, u)
                    dve.wait_ge(silu_done, l * FC + c + 1)
                    dve.tensor_tensor(tiles(gate[:, :]), grp3(u[0]), tiles(gate[:, :]), ALU.mult
                                      ).then_inc(g_free[u[0]], 1)
                    dve.wait_ge(g_hi_done, l * FC + c + 1)
                    dve.tensor_tensor(mix_lo[:, :], gate[:, :], mix_hi[:, :].bitcast(F32), ALU.subtract
                                      ).then_inc(g_lo_done, 1)

                dve.wait_ge(taps0, l * FC + 1)
                dve.memset(ext[:, 0:2], 0.0).then_inc(dve_step, 1)
                dve.wait_ge(dve_step, fstep)
                taps(0)
                with dve.Fori(0, FC - 1) as i:
                    gate_b(i, use_ffn(l, i, 0))
                    add_rows(lambda m: use_ffn(l, i, 2 + m))
                    taps(i + 1)
                gate_b(FC - 1, use_ffn(l, FC - 1, 0))
                add_tiles(lambda j: use_ffn(l, FC - 1, 1 + j))

            half = G_SETUP // 2 + DEPTH * (G_LAYER // 2)
            for k in range(1, KC):
                dve.wait_ge(sq_done, 2 * DEPTH * TILE_USES + k + 1)
                if k == 1:
                    dve.scalar_tensor_tensor(out=rot[:, 0:T], in0=rot[:, 0:T], scalar=D_MODEL * EPS / P,
                                             in1=sq_ring[1], op0=ALU.add, op1=ALU.add).then_inc(acc_done, 1)
                else:
                    dve.wait_ge(acc_done, k - 1)
                    dve.tensor_tensor(rot[:, 0:T], rot[:, 0:T], sq_ring[k % 2], ALU.add).then_inc(acc_done, 1)
            for k in range(KC):
                dve.tensor_scalar(resid[:, k, :], resid[:, k, :], p_at("final_g", 0, k), None, ALU.mult
                                  ).then_inc(y_done, 1)
            dve.wait_ge(norm_rs, 2 * DEPTH * NT + 1)
            for t in range(0, QT_N + 1, 2):
                u = use(half, t)
                full(dve, u)
                rows = P if t < QT_N else 8
                src = bank[0:rows, 3 * u[0]:3 * u[0] + 2, :].rearrange("p a b -> p (a b)")
                dve.tensor_scalar(x_buf(t)[0:rows, :], src, rs[0:rows, t:t + 1], None, ALU.mult
                                  ).then_inc(g_free[u[0]], 1)


_INS = ["x_prompt", "x_sample", "cache_k", "cache_v", "state_pool", "state_conv", "page_table", "norm1_g", "w_in",
        "pool_w", "pool_scale", "lam_q1", "lam_k1", "lam_q2", "lam_k2", "subln_g", "w_out", "norm2_g", "w_up",
        "conv_w", "conv_b", "w_down", "final_g"]
_OUTS = [(1, SEQ, D_MODEL), (DEC_BATCH, 1, D_MODEL), (DEPTH, 1, SEQ // PAGE_SIZE, PAGE_SIZE, N_HEADS, VDIM),
         (DEPTH, 1, SEQ // PAGE_SIZE, PAGE_SIZE, N_HEADS, VDIM), (DEPTH, 1, POOL_HIST, POOL_W), (DEPTH, 1, 2, D_FF),
         (DEPTH, DEC_BATCH, 1, N_HEADS, VDIM), (DEPTH, DEC_BATCH, 1, N_HEADS, VDIM),
         (DEPTH, DEC_BATCH, POOL_HIST, POOL_W), (DEPTH, DEC_BATCH, 2, D_FF)]


def layouts(inputs):
    arrays = {f"in_{name}": np.asarray(inputs[name]) for name in _INS}
    for name in ("in_cache_k", "in_cache_v"):
        arrays[name] = arrays[name].transpose(0, 3, 1, 2, 4).reshape(-1, RUN * VDIM)
    for name in ("in_w_in", "in_w_up"):
        w = arrays[name].reshape(DEPTH, KC, P, -1, P)
        arrays[name] = w.transpose(0, 3, 2, 1, 4).reshape(DEPTH, -1, P, KC * P)
    arrays["in_page_table"] = arrays["in_page_table"].transpose(1, 0)
    arrays = {name: np.ascontiguousarray(a) for name, a in arrays.items()}
    arrays["in_table"] = constants()
    return arrays


def kernel(**inputs):
    import concourse.bacc as bacc
    from concourse.bass_utils import run_bass_kernel_spmd

    nc = bacc.Bacc("TRN2", target_bir_lowering=False, num_devices=1)
    arrays = layouts(inputs)
    args = [nc.dram_tensor(name, a.shape, mybir.dt.from_np(a.dtype), kind="ExternalInput").ap()
            for name, a in arrays.items()]
    args += [nc.dram_tensor(f"out_{i}", shape, F32, kind="ExternalOutput").ap() for i, shape in enumerate(_OUTS)]
    hybrid_decoder_kernel(nc, *args)
    r = run_bass_kernel_spmd(nc, [arrays], core_ids=[0])
    return tuple(r.results[0][f"out_{i}"] for i in range(len(_OUTS)))
```
